# Optimizing a Trainium2 kernel written in Bass

```python
import math
import jax, jax.numpy as jnp
from jax import lax
import numpy as np

D_MODEL = 2048
BATCH = 1
SEQ = 256
DEPTH = 1

N_MEM = 256
D_MIX = 2 * D_MODEL
D_SSD = D_MIX // 2
D_SC = D_MIX - D_SSD
SSD_HEADDIM = 64
SSD_HEADS = D_SSD // SSD_HEADDIM
SSD_GROUPS = 4
SSD_STATE = 128
SSD_CONV = 4
SSD_CHUNK = 256
D_XBC = D_SSD + 2 * SSD_GROUPS * SSD_STATE
DT_MIN = 1e-3
DT_MAX = 1e-1
SC_CONV = 3
SC_GROUPS = 16
XA_HEADS = 4
XA_HEADDIM = 128
D_XA = XA_HEADS * XA_HEADDIM
D_FF = ((8 * D_MODEL + 3 * 256 - 1) // (3 * 256)) * 256
NORM_EPS = 1e-5
D_IN_PROJ = D_SSD + D_XBC + SSD_HEADS + 3 * D_SC
IN_SPLITS = [D_SSD,
             D_SSD + D_XBC,
             D_SSD + D_XBC + SSD_HEADS,
             D_SSD + D_XBC + SSD_HEADS + D_SC,
             D_SSD + D_XBC + SSD_HEADS + 2 * D_SC]


def rmsnorm(x, g):
    xf = x.astype(jnp.float32)
    xf = xf * lax.rsqrt(jnp.mean(xf * xf, axis=-1, keepdims=True) + NORM_EPS)
    return (xf * g.astype(jnp.float32)).astype(x.dtype)

def grouped_rmsnorm(x, g, n_groups):
    shp = x.shape
    xf = x.astype(jnp.float32).reshape(shp[:-1] + (n_groups, shp[-1] // n_groups))
    xf = xf * lax.rsqrt(jnp.mean(xf * xf, axis=-1, keepdims=True) + NORM_EPS)
    return (xf.reshape(shp) * g.astype(jnp.float32)).astype(x.dtype)

def causal_dwconv(x, w):
    k, c = w.shape
    return lax.conv_general_dilated(
        x, w[:, None, :].astype(x.dtype), window_strides=(1,), padding=[(k - 1, 0)],
        dimension_numbers=("NWC", "WIO", "NWC"), feature_group_count=c)

def ssd_chunked(xh, dt, a, bm, cm):
    f32 = jnp.float32
    bsz, seqlen, nh, hd = xh.shape
    g, n = bm.shape[2], bm.shape[3]
    r = nh // g
    pad = (-seqlen) % SSD_CHUNK
    xh, dt, bm, cm = (t.astype(f32) for t in (xh, dt, bm, cm))
    if pad:
        xh = jnp.pad(xh, ((0, 0), (0, pad), (0, 0), (0, 0)))
        dt = jnp.pad(dt, ((0, 0), (0, pad), (0, 0)))
        bm = jnp.pad(bm, ((0, 0), (0, pad), (0, 0), (0, 0)))
        cm = jnp.pad(cm, ((0, 0), (0, pad), (0, 0), (0, 0)))
    nc = (seqlen + pad) // SSD_CHUNK
    L = SSD_CHUNK
    x = (xh * dt[..., None]).reshape(bsz, nc, L, g, r, hd)
    a_dt = jnp.moveaxis((dt * a.astype(f32)).reshape(bsz, nc, L, g, r), 2, -1)
    a_cs = jnp.cumsum(a_dt, axis=-1)
    bc = bm.reshape(bsz, nc, L, g, n)
    cc = cm.reshape(bsz, nc, L, g, n)
    causal = jnp.tril(jnp.ones((L, L), dtype=bool))
    decay = jnp.exp(jnp.where(causal, a_cs[..., :, None] - a_cs[..., None, :], -jnp.inf))
    cb = jnp.einsum("bclgn,bcsgn->bcgls", cc, bc)
    scores = cb[:, :, :, None] * decay
    y_diag = jnp.einsum("bcgrls,bcsgrp->bclgrp", scores, x)
    decay_states = jnp.exp(a_cs[..., -1:] - a_cs)
    states = jnp.einsum("bclgn,bcgrl,bclgrp->bcgrpn", bc, decay_states, x)
    chunk_decay = jnp.exp(a_cs[..., -1])

    def step(h, inp):
        s_c, d_c = inp
        return h * d_c[..., None, None] + s_c, h

    h0 = jnp.zeros_like(states[:, 0])
    _, prev = lax.scan(step, h0, (jnp.moveaxis(states, 1, 0), jnp.moveaxis(chunk_decay, 1, 0)))
    prev = jnp.moveaxis(prev, 0, 1)
    y_off = jnp.einsum("bclgn,bcgrpn,bcgrl->bclgrp", cc, prev, jnp.exp(a_cs))
    y = (y_diag + y_off).reshape(bsz, nc * L, nh, hd)
    return y[:, :seqlen]

def hybrid_mixer(h, w_in, ssd_conv_w, ssd_conv_b, dt_bias, a_log, d_skip, ssd_norm,
                 sc_conv_w, sc_norm, w_out):
    bsz, seqlen, _ = h.shape
    proj = h @ w_in
    z, xbc, dt_raw, sc_u, sc_b, sc_c = jnp.split(proj, IN_SPLITS, axis=-1)
    xbc = jax.nn.silu(causal_dwconv(xbc, ssd_conv_w) + ssd_conv_b)
    xs, bm, cm = jnp.split(xbc, [D_SSD, D_SSD + SSD_GROUPS * SSD_STATE], axis=-1)
    xh = xs.reshape(bsz, seqlen, SSD_HEADS, SSD_HEADDIM)
    dt = jax.nn.softplus(dt_raw.astype(jnp.float32) + dt_bias.astype(jnp.float32))
    a = -jnp.exp(a_log.astype(jnp.float32))
    y = ssd_chunked(xh, dt, a,
                    bm.reshape(bsz, seqlen, SSD_GROUPS, SSD_STATE),
                    cm.reshape(bsz, seqlen, SSD_GROUPS, SSD_STATE))
    y = y + xh.astype(jnp.float32) * d_skip.astype(jnp.float32)[:, None]
    y = y.reshape(bsz, seqlen, D_SSD).astype(h.dtype)
    y_ssd = grouped_rmsnorm(y * jax.nn.silu(z), ssd_norm, SSD_GROUPS)
    v = sc_b * causal_dwconv(sc_c * sc_u, sc_conv_w)
    y_sc = grouped_rmsnorm(v, sc_norm, SC_GROUPS)
    return jnp.concatenate([y_ssd, y_sc], axis=-1) @ w_out

def memory_cross_attention(h, mem_n, w_q, w_k, w_v, w_o):
    bsz, seqlen, _ = h.shape
    n_mem = mem_n.shape[1]
    q = (h @ w_q).reshape(bsz, seqlen, XA_HEADS, XA_HEADDIM)
    k = (mem_n @ w_k).reshape(bsz, n_mem, XA_HEADS, XA_HEADDIM)
    v = (mem_n @ w_v).reshape(bsz, n_mem, XA_HEADS, XA_HEADDIM)
    scores = jnp.einsum("bshd,bmhd->bhsm", q, k).astype(jnp.float32) * (XA_HEADDIM ** -0.5)
    p = jax.nn.softmax(scores, axis=-1).astype(v.dtype)
    o = jnp.einsum("bhsm,bmhd->bshd", p, v).reshape(bsz, seqlen, D_XA)
    return o @ w_o

def swiglu(h, w_gate, w_up, w_down):
    return (jax.nn.silu(h @ w_gate) * (h @ w_up)) @ w_down

def first_inputs(seed: int = 0) -> dict:
    key = jax.random.key(seed)
    ks = jax.random.split(key, 24)
    f32 = jnp.float32

    def nrm(k, shape, scale):
        return jax.random.normal(k, shape, f32) * scale

    def gain(k, shape):
        return 1.0 + 0.02 * jax.random.normal(k, shape, f32)

    x = nrm(ks[0], (BATCH, SEQ, D_MODEL), 1.0)
    mem = nrm(ks[1], (BATCH, N_MEM, D_MODEL), 1.0)
    norm_mix = gain(ks[2], (DEPTH, D_MODEL))
    w_in = nrm(ks[3], (DEPTH, D_MODEL, D_IN_PROJ), D_MODEL ** -0.5)
    ssd_conv_w = nrm(ks[4], (DEPTH, SSD_CONV, D_XBC), SSD_CONV ** -0.5)
    ssd_conv_b = nrm(ks[5], (DEPTH, D_XBC), 0.02)
    dt0 = jnp.exp(jax.random.uniform(ks[6], (DEPTH, SSD_HEADS), f32, math.log(DT_MIN), math.log(DT_MAX)))
    dt_bias = dt0 + jnp.log(-jnp.expm1(-dt0))
    a_log = jnp.log(jax.random.uniform(ks[7], (DEPTH, SSD_HEADS), f32, 1.0, 16.0))
    d_skip = gain(ks[8], (DEPTH, SSD_HEADS))
    ssd_norm = gain(ks[9], (DEPTH, D_SSD))
    sc_conv_w = nrm(ks[10], (DEPTH, SC_CONV, D_SC), SC_CONV ** -0.5)
    sc_norm = gain(ks[11], (DEPTH, D_SC))
    w_out = nrm(ks[12], (DEPTH, D_MIX, D_MODEL), D_MIX ** -0.5)
    mem_norm = gain(ks[13], (D_MODEL,))
    norm_xa = gain(ks[14], (DEPTH, D_MODEL))
    w_q = nrm(ks[15], (DEPTH, D_MODEL, D_XA), D_MODEL ** -0.5)
    w_k = nrm(ks[16], (DEPTH, D_MODEL, D_XA), D_MODEL ** -0.5)
    w_v = nrm(ks[17], (DEPTH, D_MODEL, D_XA), D_MODEL ** -0.5)
    w_o = nrm(ks[18], (DEPTH, D_XA, D_MODEL), D_XA ** -0.5)
    norm_ffn = gain(ks[19], (DEPTH, D_MODEL))
    w_gate = nrm(ks[20], (DEPTH, D_MODEL, D_FF), D_MODEL ** -0.5)
    w_up = nrm(ks[21], (DEPTH, D_MODEL, D_FF), D_MODEL ** -0.5)
    w_down = nrm(ks[22], (DEPTH, D_FF, D_MODEL), D_FF ** -0.5)
    norm_final = gain(ks[23], (D_MODEL,))
    return {"x": x, "mem": mem, "norm_mix": norm_mix, "w_in": w_in,
            "ssd_conv_w": ssd_conv_w, "ssd_conv_b": ssd_conv_b, "dt_bias": dt_bias,
            "a_log": a_log, "d_skip": d_skip, "ssd_norm": ssd_norm,
            "sc_conv_w": sc_conv_w, "sc_norm": sc_norm, "w_out": w_out,
            "mem_norm": mem_norm, "norm_xa": norm_xa, "w_q": w_q, "w_k": w_k,
            "w_v": w_v, "w_o": w_o, "norm_ffn": norm_ffn, "w_gate": w_gate,
            "w_up": w_up, "w_down": w_down, "norm_final": norm_final}

def first_block(x, mem, norm_mix, w_in, ssd_conv_w, ssd_conv_b, dt_bias, a_log, d_skip,
              ssd_norm, sc_conv_w, sc_norm, w_out, mem_norm, norm_xa, w_q, w_k, w_v, w_o,
              norm_ffn, w_gate, w_up, w_down, norm_final):
    mem_n = rmsnorm(mem, mem_norm)
    h = x
    for i in range(DEPTH):
        h = h + hybrid_mixer(rmsnorm(h, norm_mix[i]), w_in[i], ssd_conv_w[i], ssd_conv_b[i],
                             dt_bias[i], a_log[i], d_skip[i], ssd_norm[i],
                             sc_conv_w[i], sc_norm[i], w_out[i])
        h = h + memory_cross_attention(rmsnorm(h, norm_xa[i]), mem_n, w_q[i], w_k[i], w_v[i], w_o[i])
        h = h + swiglu(rmsnorm(h, norm_ffn[i]), w_gate[i], w_up[i], w_down[i])
    return rmsnorm(h, norm_final)


D_MIX_2 = D_MODEL
D_POOL = D_MIX_2 // 4
D_HYENA = 3 * D_MIX_2 // 8
D_GMLP = D_MIX_2 - D_POOL - D_HYENA
POOL_WINDOWS = (2, 4, 8, 16)
N_POOL_GROUPS = len(POOL_WINDOWS)
POOL_GROUP_DIM = D_POOL // N_POOL_GROUPS
HYENA_GROUP_DIM = 128
N_HYENA_GROUPS = D_HYENA // HYENA_GROUP_DIM
FILTER_BANDS = 16
FILTER_EMB = 1 + 2 * FILTER_BANDS
FILTER_HIDDEN = 64
DECAY_TARGET = 1e-2
FAST_DECAY_PCT = 0.3
SLOW_DECAY_PCT = 1.5
CHUNK = 128
GMLP_HEAD_DIM = 128
N_GMLP_HEADS = D_GMLP // GMLP_HEAD_DIM
D_IN_PROJ_2 = D_POOL + 3 * D_HYENA + 2 * D_GMLP
D_FF_2 = 5632
CONV_WIDTH = 3
RMS_EPS = 1e-6
LN_EPS = 1e-5


def rmsnorm_2(x, g):
    xf = x.astype(jnp.float32)
    y = xf * lax.rsqrt(jnp.mean(xf * xf, axis=-1, keepdims=True) + RMS_EPS)
    return (y * g.astype(jnp.float32)).astype(x.dtype)

def layernorm(x, g, b):
    xf = x.astype(jnp.float32)
    mu = jnp.mean(xf, axis=-1, keepdims=True)
    var = jnp.mean(jnp.square(xf - mu), axis=-1, keepdims=True)
    y = (xf - mu) * lax.rsqrt(var + LN_EPS)
    return (y * g.astype(jnp.float32) + b.astype(jnp.float32)).astype(x.dtype)

def dwconv3(x, w, b):
    L = x.shape[1]
    xp = jnp.pad(x, ((0, 0), (1, 1), (0, 0)))
    return xp[:, :L] * w[0] + xp[:, 1:L + 1] * w[1] + xp[:, 2:] * w[2] + b

def multiscale_pool_mixer(xa, w_pool, b_pool, scale):
    B, L, _ = xa.shape
    xf = xa.reshape(B, L, N_POOL_GROUPS, POOL_GROUP_DIM).astype(jnp.float32)
    csum = jnp.concatenate([jnp.zeros_like(xf[:, :1]), jnp.cumsum(xf, axis=1)], axis=1)
    t = np.arange(L)
    pooled = []
    for g, w in enumerate(POOL_WINDOWS):
        lo = np.maximum(t - w // 2, 0)
        hi = np.minimum(t + w // 2 - 1, L - 1)
        cnt = (hi - lo + 1).astype(np.float32)
        s = csum[:, hi + 1, g] - csum[:, lo, g]
        pooled.append(s / cnt[None, :, None])
    pooled = jnp.stack(pooled, axis=2)
    diff = (pooled - xf).astype(xa.dtype)
    y = jnp.einsum('blgc,gcd->blgd', diff, w_pool) + b_pool
    return y.reshape(B, L, D_POOL) * scale

def filter_features(L):
    t = jnp.linspace(0.0, 1.0, L, dtype=jnp.float32)[:, None]
    w = 2.0 * math.pi * jnp.arange(L, dtype=jnp.float32)[:, None] / L
    f = jnp.linspace(1e-4, FILTER_BANDS - 1, FILTER_BANDS, dtype=jnp.float32)[None, :]
    return jnp.concatenate([t, jnp.cos(f * w), -jnp.sin(f * w)], axis=-1), t

def implicit_filters(feat, t, w1, b1, fr1, w2, b2, fr2, w3):
    f32 = lambda a: a.astype(jnp.float32)
    h = jnp.sin(f32(fr1) * (feat @ f32(w1) + f32(b1)))
    h = jnp.sin(f32(fr2) * (h @ f32(w2) + f32(b2)))
    h = h @ f32(w3)
    deltas = jnp.linspace(math.log(DECAY_TARGET) / SLOW_DECAY_PCT,
                          math.log(DECAY_TARGET) / FAST_DECAY_PCT, D_HYENA, dtype=jnp.float32)
    decay = jnp.exp(-t * jnp.abs(deltas)[None, :])
    return h[:, :D_HYENA] * decay, h[:, D_HYENA:] * decay

def bidirectional_fftconv(z, h_fwd, h_bwd):
    B, L, C = z.shape
    k = jnp.concatenate([h_fwd, jnp.zeros((1, C), h_fwd.dtype), h_bwd[:0:-1]], axis=0)
    k_f = jnp.fft.rfft(k, n=2 * L, axis=0)
    z_f = jnp.fft.rfft(z.astype(jnp.float32), n=2 * L, axis=1)
    return jnp.fft.irfft(z_f * k_f[None], n=2 * L, axis=1)[:, :L]

def hyena_mixer(xb, short_w, short_b, h_fwd, h_bwd, d_skip):
    xs = dwconv3(xb, short_w, short_b)
    x0, x1, v = jnp.split(xs, 3, axis=-1)
    z = x1 * v
    y = bidirectional_fftconv(z, h_fwd, h_bwd).astype(z.dtype) + d_skip * z
    return x0 * y

def chunked_spatial_gating(xc, ln_g, ln_b, w_s, b_s):
    B, L, _ = xc.shape
    z = jax.nn.gelu(xc)
    u, v = jnp.split(z, 2, axis=-1)
    v = layernorm(v, ln_g, ln_b).reshape(B, L // CHUNK, CHUNK, N_GMLP_HEADS, GMLP_HEAD_DIM)
    g = jnp.einsum('bnpec,eqp->bnqec', v, w_s) + b_s.T[:, :, None]
    return u * g.reshape(B, L, D_GMLP)

def second_inputs(seed: int = 0) -> dict:
    key = jax.random.key(seed)
    ks = jax.random.split(key, 27)
    nrm = lambda k, shape, s: s * jax.random.normal(k, shape, jnp.float32)
    c = POOL_GROUP_DIM
    return {
        "x": nrm(ks[0], (BATCH, SEQ, D_MODEL), 1.0),
        "norm_mix": 1.0 + nrm(ks[1], (DEPTH, D_MODEL), 0.05),
        "w_in": nrm(ks[2], (DEPTH, D_MODEL, D_IN_PROJ_2), D_MODEL ** -0.5),
        "pool_w": nrm(ks[3], (DEPTH, N_POOL_GROUPS, c, c), c ** -0.5),
        "pool_b": nrm(ks[4], (DEPTH, N_POOL_GROUPS, c), 0.02),
        "pool_scale": 1.0 + nrm(ks[5], (DEPTH, D_POOL), 0.1),
        "hy_short_w": nrm(ks[6], (DEPTH, CONV_WIDTH, 3 * D_HYENA), 0.5),
        "hy_short_b": nrm(ks[7], (DEPTH, 3 * D_HYENA), 0.02),
        "hy_filt_w1": nrm(ks[8], (DEPTH, FILTER_EMB, FILTER_HIDDEN), FILTER_EMB ** -0.5),
        "hy_filt_b1": nrm(ks[9], (DEPTH, FILTER_HIDDEN), 0.5),
        "hy_filt_freq1": 1.0 + nrm(ks[10], (DEPTH, FILTER_HIDDEN), 0.1),
        "hy_filt_w2": nrm(ks[11], (DEPTH, FILTER_HIDDEN, FILTER_HIDDEN), FILTER_HIDDEN ** -0.5),
        "hy_filt_b2": nrm(ks[12], (DEPTH, FILTER_HIDDEN), 0.5),
        "hy_filt_freq2": 1.0 + nrm(ks[13], (DEPTH, FILTER_HIDDEN), 0.1),
        "hy_filt_w3": nrm(ks[14], (DEPTH, FILTER_HIDDEN, 2 * D_HYENA), 0.005),
        "hy_skip": nrm(ks[15], (DEPTH, D_HYENA), 0.5),
        "gm_ln_g": 1.0 + nrm(ks[16], (DEPTH, D_GMLP), 0.05),
        "gm_ln_b": nrm(ks[17], (DEPTH, D_GMLP), 0.02),
        "gm_w_s": nrm(ks[18], (DEPTH, N_GMLP_HEADS, CHUNK, CHUNK), CHUNK ** -0.5),
        "gm_b_s": 1.0 + nrm(ks[19], (DEPTH, N_GMLP_HEADS, CHUNK), 0.1),
        "w_out": nrm(ks[20], (DEPTH, D_MIX_2, D_MODEL), D_MIX_2 ** -0.5),
        "norm_ffn": 1.0 + nrm(ks[21], (DEPTH, D_MODEL), 0.05),
        "ffn_w_up": nrm(ks[22], (DEPTH, D_MODEL, 2 * D_FF_2), D_MODEL ** -0.5),
        "ffn_conv_w": nrm(ks[23], (DEPTH, CONV_WIDTH, 2 * D_FF_2), 0.5),
        "ffn_conv_b": nrm(ks[24], (DEPTH, 2 * D_FF_2), 0.02),
        "ffn_w_down": nrm(ks[25], (DEPTH, D_FF_2, D_MODEL), D_FF_2 ** -0.5),
        "norm_final": 1.0 + nrm(ks[26], (D_MODEL,), 0.05),
    }

def second_block(x, norm_mix, w_in, pool_w, pool_b, pool_scale, hy_short_w, hy_short_b,
              hy_filt_w1, hy_filt_b1, hy_filt_freq1, hy_filt_w2, hy_filt_b2, hy_filt_freq2,
              hy_filt_w3, hy_skip, gm_ln_g, gm_ln_b, gm_w_s, gm_b_s, w_out, norm_ffn,
              ffn_w_up, ffn_conv_w, ffn_conv_b, ffn_w_down, norm_final):
    L = x.shape[1]
    feat, t = filter_features(L)
    a_end = D_POOL
    b_end = D_POOL + 3 * D_HYENA
    for i in range(DEPTH):
        h = rmsnorm_2(x, norm_mix[i])
        p = h @ w_in[i]
        y_a = multiscale_pool_mixer(p[..., :a_end], pool_w[i], pool_b[i], pool_scale[i])
        h_fwd, h_bwd = implicit_filters(feat, t, hy_filt_w1[i], hy_filt_b1[i], hy_filt_freq1[i],
                                        hy_filt_w2[i], hy_filt_b2[i], hy_filt_freq2[i], hy_filt_w3[i])
        y_b = hyena_mixer(p[..., a_end:b_end], hy_short_w[i], hy_short_b[i], h_fwd, h_bwd, hy_skip[i])
        y_c = chunked_spatial_gating(p[..., b_end:], gm_ln_g[i], gm_ln_b[i], gm_w_s[i], gm_b_s[i])
        x = x + jnp.concatenate([y_a, y_b, y_c], axis=-1) @ w_out[i]
        h = rmsnorm_2(x, norm_ffn[i])
        up = dwconv3(h @ ffn_w_up[i], ffn_conv_w[i], ffn_conv_b[i])
        gate, val = jnp.split(up, 2, axis=-1)
        x = x + (jax.nn.silu(gate) * val) @ ffn_w_down[i]
    return rmsnorm_2(x, norm_final)


def setup_inputs(seed=0):
    out = dict(first_inputs(seed))
    for name, value in second_inputs(seed + 1).items():
        if name != "x":
            out[name + "_2"] = value
    return out


def reference(
    x, mem, norm_mix, w_in, ssd_conv_w, ssd_conv_b, dt_bias, a_log, d_skip, ssd_norm, sc_conv_w,
    sc_norm, w_out, mem_norm, norm_xa, w_q, w_k, w_v, w_o, norm_ffn, w_gate, w_up, w_down,
    norm_final, norm_mix_2, w_in_2, pool_w_2, pool_b_2, pool_scale_2, hy_short_w_2,
    hy_short_b_2, hy_filt_w1_2, hy_filt_b1_2, hy_filt_freq1_2, hy_filt_w2_2, hy_filt_b2_2,
    hy_filt_freq2_2, hy_filt_w3_2, hy_skip_2, gm_ln_g_2, gm_ln_b_2, gm_w_s_2, gm_b_s_2, w_out_2,
    norm_ffn_2, ffn_w_up_2, ffn_conv_w_2, ffn_conv_b_2, ffn_w_down_2, norm_final_2,
):
    x = first_block(
        x, mem, norm_mix, w_in, ssd_conv_w, ssd_conv_b, dt_bias, a_log, d_skip, ssd_norm,
        sc_conv_w, sc_norm, w_out, mem_norm, norm_xa, w_q, w_k, w_v, w_o, norm_ffn, w_gate,
        w_up, w_down, norm_final,
    )
    return second_block(
        x, norm_mix_2, w_in_2, pool_w_2, pool_b_2, pool_scale_2, hy_short_w_2, hy_short_b_2,
        hy_filt_w1_2, hy_filt_b1_2, hy_filt_freq1_2, hy_filt_w2_2, hy_filt_b2_2,
        hy_filt_freq2_2, hy_filt_w3_2, hy_skip_2, gm_ln_g_2, gm_ln_b_2, gm_w_s_2, gm_b_s_2,
        w_out_2, norm_ffn_2, ffn_w_up_2, ffn_conv_w_2, ffn_conv_b_2, ffn_w_down_2, norm_final_2,
    )


_drawn_inputs = setup_inputs


def setup_inputs(seed=0):
    import zlib

    import numpy as np

    out = dict(_drawn_inputs(seed))
    spreads = {}
    factors = {'ssd_conv_b': 3.171,
     'd_skip': 6.956,
     'ssd_norm': 4.543,
     'sc_norm': 4.616,
     'mem_norm': 8.0,
     'norm_xa': 8.0,
     'norm_ffn': 4.46,
     'pool_b_2': 6.734,
     'hy_short_b_2': 8.0,
     'hy_filt_freq1_2': 8.0,
     'hy_filt_freq2_2': 23.059,
     'gm_ln_g_2': 3.082,
     'gm_ln_b_2': 8.0,
     'ffn_conv_b_2': 5.179,
     'norm_ffn_2': 3.046}
    for name, (base, spread) in spreads.items():
        noise = np.random.default_rng([zlib.crc32(name.encode()), seed]).standard_normal(out[name].shape)
        drawn = base * np.exp(spread * noise) if base else spread * noise
        out[name] = __import__('jax').numpy.asarray(drawn.astype(out[name].dtype))
    for name, factor in factors.items():
        out[name] = (out[name] * factor).astype(out[name].dtype)
    return out
```

```python
from collections import deque

import concourse.bass as bass
from concourse import mybir

F32 = mybir.dt.float32
F32R = mybir.dt.float32r
ALU = mybir.AluOpType
ACT = mybir.ActivationFunctionType
AX = mybir.AxisListType

L = 256
D = 2048
KT = 16
FT = 44
NRAW = 4
NW = 3
UK = 4
UN = UK * 256
SPLIT_AHEAD = 2

PARAMS = [
    ("norm_mix", 16), ("conv_w", 96), ("conv_b", 24), ("ssd_norm", 16), ("d_skip", 16),
    ("sc_w", 48), ("sc_norm", 16), ("mem_norm", 16), ("norm_xa", 16), ("norm_ffn", 16),
    ("norm_final", 16), ("norm_mix_2", 16), ("pool_b", 4), ("pool_scale", 4), ("hy_w", 54),
    ("hy_b", 18), ("hy_skip", 6), ("norm_ffn_2", 16), ("fc_w", 264), ("fc_b", 88),
    ("norm_final_2", 16), ("dt_bias", 1), ("a_log", 1), ("f_b1", 1), ("f_fr1", 1), ("f_b2", 1),
    ("f_fr2", 1), ("rcnt", 64),
]
POFF = {}
_o = 0
for _n, _c in PARAMS:
    POFF[_n] = _o
    _o += _c
NPAR = _o

MAP = {}
_o = 0
for _n, _c in [("hT", 4096), ("X1", 8192), ("XG", 8192), ("raw", NRAW * UN), ("wh", NW * UN), ("wl", NW * UN),
               ("par", NPAR), ("ident", 128), ("ones", 128), ("T", 10 * 256), ("R", 4 * 264), ("A", 17000)]:
    MAP[_n] = _o
    _o += (_c + 7) // 8 * 8
NWORDS = _o

A_ATT = dict(kT=0, v=1024)
A_MIX = dict(XS=2048, ZS=4096, BT=6144, CT=7168, cbm=8192, mask=9728, dtb=10112, dcol=12160, D=12288, M=13056,
             xdt=13824, U=14080, C=14592, B=15104, V=15616)
A_XA = dict(qT=2048, P=3072, PT=5120, st=7168)
A_FIL = dict(K=0, F=3840, G=4864, dec=5888, w3=7424, hf=8960, feat=12032, w1=12288, w2=12352, s=12416)
A_B2 = dict(K=0, F=3840, IF=4864, z=5888, x0=7424, vg=8960, ws=10496, bs=11264, wp=12032, t=12544, rc=13700)
G_B2 = dict(zt=2048, zf=5120, vt=6656, gain=0)


class Queue:

    def __init__(self, name, sem):
        self.name, self.sem, self.n, self.items = name, sem, 0, []

    def add(self, fn, waits, inc):
        tok = None
        if inc:
            self.n += 1
            tok = (self.sem, self.n)
        self.items.append((flat(waits), fn, inc))
        return tok

    def play(self, eng):
        seen = {}
        for waits, fn, inc in self.items:
            for sem, val in waits:
                if seen.get(id(sem), 0) < val:
                    eng.wait_ge(sem, val)
                    seen[id(sem)] = val
            ins = fn(eng)
            if inc:
                ins.then_inc(self.sem, 1)


def flat(x):
    if x is None:
        return []
    if isinstance(x, tuple) and len(x) == 2 and isinstance(x[1], int):
        return [x]
    out = []
    for y in x:
        out += flat(y)
    return out


class Slot:
    def __init__(self, ap):
        self.ap, self.free = ap, []


class Ring:

    def __init__(self, aps):
        self.slots = deque(Slot(a) for a in aps)

    def take(self):
        assert self.slots, "no buffer left"
        return self.slots.popleft()

    def give(self, slot, *toks):
        slot.free = flat(toks)
        self.slots.append(slot)


def program(nc, T_):
    sems = []

    def sem(name):
        g = nc.semaphore(name)
        s = g.__enter__()
        sems.append(g)
        return s

    def at(name, words, dt=F32, base=None, off=0):
        b = MAP[base or name] + off
        return nc.alloc_sbuf_tensor_at(name, [128, words], dt, offset=4 * b + BASE)

    BASE = (nc.sbuf_base + 31) // 32 * 32
    slab = nc.sbuf_tensor("slab", [128, NWORDS + 8], F32)
    slab.__enter__()
    hT = at("hT", 4096)
    X1 = at("X1", 8192, F32R)
    XG = at("XG", 8192, F32R)
    Gf = at("Gf", 8192, F32, base="XG")
    raw = at("raw", NRAW * UN)
    wh = at("wh", NW * UN, F32R)
    wl = at("wl", NW * UN, F32R)
    par = at("par", NPAR)
    ident = at("ident", 128)
    ones = at("ones", 128)
    Tt = at("T", 10 * 256)
    Rt = at("R", 4 * 264)
    A = at("A", 17000)

    pguards = [nc.psum_tensor(f"ps{i}", [128, 512], F32) for i in range(8)]
    banks = [g.__enter__() for g in pguards]

    q = {n: Queue(n, sem("s_" + n)) for n in ("pe", "act", "dve", "pool", "sp")}

    def pe(fn, *w, inc=True):
        return q["pe"].add(fn, w, inc)

    def act(fn, *w):
        return q["act"].add(fn, w, True)

    def dve(fn, *w):
        return q["dve"].add(fn, w, True)

    def pool(fn, *w):
        return q["pool"].add(fn, w, True)

    dcount = {}

    def dma(queue, s, out, in_, *w):
        dcount[id(s)] = dcount.get(id(s), 0) + 16

        def fn(e):
            return e.dma_start(out, in_).then_inc(s, 16)
        q[queue].add(fn, w, False)
        return (s, dcount[id(s)])

    def done():
        return [(x.sem, x.n) for x in q.values() if x.n and x.name != "sp"]

    def P(name, i=0, n=1, p=128):
        return par[0:p, POFF[name] + i:POFF[name] + i + n]

    def a_(off, n, p=128):
        return A[0:p, off:off + n]

    TR = Ring([Tt[:, i * 256:(i + 1) * 256] for i in range(10)])
    RR = Ring([Rt[:, i * 264:(i + 1) * 264] for i in range(4)])
    AUX = Ring([banks[i][:, :] for i in range(4, 8)])

    s_par, s_x, s_mem = sem("d_par"), [sem(f"d_x{i}") for i in range(4)], sem("d_mem")
    memT = Gf[:, 4096:8192]
    t_mem = dma("sp", s_mem, memT, T_["memT"])
    dma("sp", s_par, par[:, :], T_["par"])
    t_par = dma("sp", s_par, ident[:, :], T_["ident"])
    t_ones = pool(lambda e: e.memset(ones[:, :], 1.0))
    t_pad = pool(lambda e: e.memset(Rt[:, :], 0.0))
    for s in RR.slots:
        s.free = [t_pad]
    t_x = []

    def load_x():
        for i in range(4):
            t = dma("sp", s_x[i], hT[:, i * 1024:(i + 1) * 1024], T_["xT"][:, i * 1024:(i + 1) * 1024])
            t_x.extend([t] * 4)

    h = [[None] for _ in range(KT)]

    def hk(k):
        return hT[:, k * 256:(k + 1) * 256]

    def rstd(ps, tok, n, eps, bank=None):
        v, y, u = TR.take(), TR.take(), TR.take()
        t = dve(lambda e: e.tensor_scalar(v.ap, ps, 1.0 / n, eps, ALU.mult, ALU.add), tok, v.free)
        if bank is not None:
            AUX.give(bank, t)
        t1 = act(lambda e: e.activation(u.ap, v.ap, ACT.Ln), t, u.free)
        t2 = act(lambda e: e.activation(y.ap, u.ap, ACT.Exp, scale=-0.5), t1, y.free)
        t3 = dve(lambda e: e.tensor_tensor(u.ap, y.ap, y.ap, ALU.mult), t2)
        t4 = dve(lambda e: e.scalar_tensor_tensor(u.ap, u.ap, -0.5, v.ap, ALU.mult, ALU.mult), t3)
        t5 = dve(lambda e: e.scalar_tensor_tensor(y.ap, u.ap, 1.5, y.ap, ALU.add, ALU.mult), t4)
        TR.give(v, t4)
        TR.give(u, t5)
        return y, t5

    def split_to(X, k, src, tok, free):
        hi = X[:, k * 512:k * 512 + 256]
        lo = X[:, k * 512 + 256:k * 512 + 512]
        t1 = act(lambda e: e.activation(hi, src, ACT.Copy), tok, free)
        t2 = dve(lambda e: e.tensor_tensor(lo, src, hi.bitcast(F32), ALU.subtract), tok, t1, free)
        return [t1, t2]

    class Norm:

        def __init__(self, n):
            self.n, self.i, self.bank = n, 0, AUX.take()

        def square(self, src, tok):
            s = TR.take()
            t = act(lambda e: e.activation(s.ap, src, ACT.Square), tok, s.free)
            return s, t

        def total(self, s, t):
            i = self.i
            self.i += 1
            ps = self.bank.ap[:, 0:256]
            self.tok = pe(lambda e: e.matmul(ps, ones[:, :], s.ap, start=(i == 0), stop=(i == self.n - 1)),
                          t, t_ones, self.bank.free if i == 0 else None)
            TR.give(s, self.tok)

        def add(self, src, tok):
            s, t = self.square(src, tok)
            self.total(s, t)

        def finish(self, n, eps):
            assert self.i == self.n
            return rstd(self.bank.ap[:, 0:256], self.tok, n, eps, self.bank)

    def normalise(rs, rtok, srcs, gain, dst):
        pend = None
        last = None
        for k, (src, tok) in enumerate(srcs):
            s = TR.take()
            t = dve(lambda e, s=s, src=src, k=k: e.scalar_tensor_tensor(s.ap, src, gain(k), rs.ap, ALU.mult, ALU.mult),
                    tok, rtok, s.free, t_par)
            last = t
            if pend:
                pend()

            def fin(k=k, s=s, t=t):
                TR.give(s, dst(k, s.ap, t))
            pend = fin
        pend()
        TR.give(rs, last)

    def evac(bank, tok, free, out, ofree, dt=None):
        tmp = TR.take()
        t1 = act(lambda e: e.activation(tmp.ap, bank[:, 256:512], ACT.Copy), tok, tmp.free)
        t2 = dve(lambda e: e.tensor_tensor(out, bank[:, 0:256], tmp.ap, ALU.add), t1, ofree)
        TR.give(tmp, t2)
        free.append(t2)
        return t2

    units = []

    def proj(W, col, groups, X, post, w=256, kn=UK, mode="A", pre=None):
        n = len(groups)
        for i, g in enumerate(groups):
            units.append(dict(src=W[col, g], g=g, kn=kn, w=w, X=X, post=post if i == n - 1 else None,
                              start=i == 0, stop=i == n - 1, mode=mode, col=col, pre=pre if i == 0 else None))

    s_raw = [sem(f"d_raw{i}") for i in range(NRAW)]
    raw_free = [[] for _ in range(NRAW)]
    w_free = [[] for _ in range(NW)]
    bank_free = [[[], []], [[], []]]
    raw_tok, split_tok = {}, {}

    def load_unit(i):
        s = i % NRAW
        raw_tok[i] = dma("sp", s_raw[s], raw[:, s * UN:(s + 1) * UN], units[i]["src"], raw_free[s])

    def split_unit(i):
        s, r = i % NW, i % NRAW
        src, hi, lo = raw[:, r * UN:(r + 1) * UN], wh[:, s * UN:(s + 1) * UN], wl[:, s * UN:(s + 1) * UN]
        t1 = act(lambda e: e.activation(hi, src, ACT.Copy), raw_tok[i], w_free[s])
        t2 = dve(lambda e: e.tensor_tensor(lo, src, hi.bitcast(F32), ALU.subtract), t1, w_free[s])
        raw_free[r] = [t1, t2]
        split_tok[i] = [t1, t2]

    tasks = deque()

    def step():
        while tasks:
            try:
                next(tasks[0][1])
                return
            except StopIteration:
                tasks.popleft()

    def drain(name=None):
        while any(name is None or n == name for n, _ in tasks):
            try:
                next(tasks[0][1])
            except StopIteration:
                tasks.popleft()

    def run():
        pair = [0]
        for j in range(min(NRAW, len(units))):
            load_unit(j)
        for j in range(SPLIT_AHEAD):
            split_unit(j)
            if j + NRAW < len(units):
                load_unit(j + NRAW)
        for i, u in enumerate(units):
            if i + SPLIT_AHEAD < len(units):
                split_unit(i + SPLIT_AHEAD)
                if i + SPLIT_AHEAD + NRAW < len(units):
                    load_unit(i + SPLIT_AHEAD + NRAW)
            if u["pre"]:
                u["pre"]()
            s, w, kn = i % NW, u["w"], u["kn"]
            p = pair[0] % 2
            nb = 2 if w == 256 else 1
            for kk in range(kn):
                k = u["g"] * kn + kk
                x, xt = u["X"](k)
                for c in range(nb):
                    bank = banks[2 * p + c]
                    st, sp = u["start"] and kk == 0, u["stop"] and kk == kn - 1
                    last = c == nb - 1 and kk == kn - 1
                    wt = [split_tok[i] if kk == 0 and c == 0 else None, xt, bank_free[p][c] if st else None]
                    b0 = s * UN + kk * w
                    if u["mode"] == "A":
                        W1, W2 = wh[:, b0 + 128 * c:b0 + 128 * c + 128], wl[:, b0 + 128 * c:b0 + 128 * c + 128]
                        pe(lambda e, bank=bank, W1=W1, x=x, st=st: e.matmul(bank[:, :], W1, x, start=st, stop=False),
                           *wt, inc=False)
                        t = pe(lambda e, bank=bank, W2=W2, x=x, sp=sp: e.matmul(bank[:, 0:256], W2, x[:, 0:256],
                                                                               start=False, stop=sp), inc=last)
                    else:
                        W1, W2 = wh[:, b0:b0 + 256], wl[:, b0:b0 + 256]
                        xh, xl = x[:, c * 128:c * 128 + 128], x[:, 256 + c * 128:384 + c * 128]
                        for m, (l, r) in enumerate([(xh, W1), (xh, W2), (xl, W1)]):
                            t = pe(lambda e, bank=bank, l=l, r=r, st=st, sp=sp, m=m: e.matmul(
                                bank[:, 0:256], l, r, start=st and m == 0, stop=sp and m == 2),
                                *wt, inc=last and m == 2)
            w_free[s] = [t]
            if u["post"]:
                for c in range(nb):
                    fr = []
                    u["post"](u["col"] * nb + c, banks[2 * p + c], t, fr)
                    bank_free[p][c] = fr
                pair[0] += 1
            step()
            if len(tasks) > 2:
                step()

    def X1k(k):
        return X1[:, k * 512:(k + 1) * 512], x1tok[k]

    def XGk(k):
        return XG[:, (k % 16) * 512:(k % 16 + 1) * 512], xgtok[k % 16]

    x1tok, xgtok = [[] for _ in range(16)], [[] for _ in range(16)]

    def to_X1(k, ap, tok):
        x1tok[k] = split_to(X1, k, ap, tok, x1free[0])
        return x1tok[k]

    x1free = [[]]

    kT = lambda i: a_(A_ATT["kT"] + 256 * i, 256)
    vv = lambda mt: a_(A_ATT["v"] + 512 * mt, 512)
    kT_tok, v_tok = [None] * 4, []

    def start():
        n = Norm(16)
        for k in range(16):
            n.add(memT[:, k * 256:(k + 1) * 256], t_mem)
        rs, rt = n.finish(D, 1e-5)
        normalise(rs, rt, [(memT[:, k * 256:(k + 1) * 256], t_mem) for k in range(16)], lambda k: P("mem_norm", k), to_X1)

        def first_norm():
            nx = Norm(16)
            for k in range(16):
                s, t = nx.square(hk(k), t_x[k])
                yield
                nx.total(s, t)
            yield
            n1[0] = nx.finish(D, 1e-5)
        tasks.append(("n1", first_norm()))

    n1 = [None]

    def post_k(ct, bank, tok, fr):
        kT_tok[ct] = evac(bank, tok, fr, kT(ct), None)

    def post_v(ct, bank, tok, fr):
        mt, col = ct % 2, ct // 2
        t = act(lambda e: e.activation(vv(mt)[:, col * 256:(col + 1) * 256], bank[:, 0:256], ACT.Copy), tok)
        v_tok.append(t)
        fr.append(t)

    for c in range(2):
        proj(T_["w_k"], c, range(4), X1k, post_k)
    for c in range(2):
        proj(T_["w_v"], c, range(4), X1k, post_v, mode="B")

    def begin_mix():
        drain("n1")
        for k in range(16):
            h[k] = t_x[k]
        x1free[0] = done()
        rs, rt = n1[0]
        normalise(rs, rt, [(hk(k), h[k]) for k in range(16)], lambda k: P("norm_mix", k), to_X1)

    def conv(src, out, ntap, off, wname, wi, nch, stok, ofree, bias=None):
        b = bias if bias is not None else 0.0
        t = act(lambda e: e.activation(out, src[:, off:off + 256], ACT.Identity, scale=P(wname, wi), bias=b),
                stok, ofree, t_par)
        for k in range(1, ntap):
            t = dve(lambda e, k=k: e.scalar_tensor_tensor(out, src[:, off + k:off + k + 256],
                                                          P(wname, k * nch + wi), out, ALU.mult, ALU.add), t, stok)
        return t

    am = A_MIX
    Uo, Co, Bo, Vo = ([a_(am[n] + 256 * i, 256) for i in range(2)] for n in "UCBV")
    cfree, bfree, vfree, ufree = [[], []], [[], []], [[], []], [[], []]
    u_tok, c_tok = [None, None], [None, None]

    def post_u(ct, bank, tok, fr):
        i = ct % 2
        u_tok[i] = evac(bank, tok, fr, Uo[i], ufree[i])

    def post_c(ct, bank, tok, fr):
        i, j = ct % 2, ct - 32
        s = TR.take()
        r = RR.take()
        t = evac(bank, tok, fr, s.ap, s.free)
        t = pool(lambda e: e.tensor_tensor(r.ap[:, 3:259], s.ap, Uo[i], ALU.mult), t, u_tok[i], r.free)
        TR.give(s, t)
        ufree[i] = [t]
        t = conv(r.ap, Co[i], 3, 1, "sc_w", j, 16, t, cfree[i])
        c_tok[i] = t
        RR.give(r, t)

    def sc_task(i, j, t):
        n = Norm(1)
        s, ts = n.square(Vo[i], t)
        yield
        n.total(s, ts)
        yield
        rs, rt = n.finish(128, 1e-5)
        yield

        def dst(_, ap, tok):
            xgtok[j] = split_to(XG, j, ap, tok, xgfree[0])
            return xgtok[j]
        normalise(rs, rt, [(Vo[i], t)], lambda k: P("sc_norm", j), dst)
        vfree[i] = xgtok[j]

    def post_b(ct, bank, tok, fr):
        i, j = ct % 2, ct - 16
        drain(f"sc{i}")
        s = TR.take()
        t = evac(bank, tok, fr, s.ap, s.free)
        t = pool(lambda e: e.tensor_tensor(Vo[i], s.ap, Co[i], ALU.mult), t, c_tok[i], vfree[i])
        TR.give(s, t)
        cfree[i] = [t]
        tasks.append((f"sc{i}", sc_task(i, j, t)))

    xgfree = [[]]

    def begin_sc():
        begin_mix()
        xgfree[0] = done()

    for j in range(8):
        proj(T_["w_sc"], j, range(4), X1k, post_u, pre=begin_sc if j == 0 else None)
        proj(T_["w_sc"], 16 + j, range(4), X1k, post_c)
        proj(T_["w_sc"], 8 + j, range(4), X1k, post_b)

    mask = a_(am["mask"], 384)
    s_mask = sem("d_mask")
    tm = {}
    dtb = [a_(am["dtb"] + 256 * i, 256, 32) for i in range(8)]
    dcol = a_(am["dcol"], 128)
    acs = dtb[5]
    eyeo = ones

    def dt_task(bank, tok, fr):
        ps = [bank[0:32, 0:256], bank[0:32, 256:512]]
        x, b1, b2, b3, b4, _, b6 = dtb[:7]
        t1 = act(lambda e: e.activation(b1, ps[1], ACT.Copy), tok)
        t2 = dve(lambda e: e.tensor_tensor(x, ps[0], b1, ALU.add), t1)
        fr.append(t2)
        t3 = dve(lambda e: e.tensor_scalar(x, x, P("dt_bias", p=32), None, ALU.add), t2, t_par)
        yield
        t4 = act(lambda e: e.activation(b1, x, ACT.Abs), t3)
        t5 = act(lambda e: e.activation(b1, b1, ACT.Exp, scale=-1.0), t4)
        t6 = dve(lambda e: e.tensor_scalar(b2, b1, 1.0, None, ALU.add), t5)
        t7 = act(lambda e: e.activation(b3, b2, ACT.Ln), t6)
        t8 = dve(lambda e: e.tensor_scalar(b4, b2, -1.0, None, ALU.add), t6)
        t9 = dve(lambda e: e.tensor_tensor(b4, b1, b4, ALU.subtract), t8)
        t10 = dve(lambda e: e.reciprocal(b6, b2), t6)
        t11 = dve(lambda e: e.tensor_tensor(b4, b4, b6, ALU.mult), t9, t10)
        t12 = dve(lambda e: e.tensor_tensor(b4, b4, b3, ALU.add), t11, t7)
        t13 = dve(lambda e: e.scalar_tensor_tensor(b4, x, 0.0, b4, ALU.max, ALU.add), t12)
        al = dtb[7]
        t14 = act(lambda e: e.activation(al[:, 0:1], P("a_log", p=32), ACT.Exp), t_par)
        t15 = dve(lambda e: e.tensor_scalar(b2, b4, al[:, 0:1], -1.0, ALU.mult, ALU.mult), t13, t14, t7)
        t16 = dve(lambda e: e.memset(b3, 1.0), t12)
        t17 = dve(lambda e: e.tensor_tensor_scan(acs, b3, b2, 0.0, ALU.mult, ALU.add), t15, t16)
        yield
        bk = AUX.take()
        for n, (src, tk) in enumerate([(acs, t17), (b4, t13)]):
            for st in range(2):
                o = 64 * n + 32 * st
                t = pe(lambda e, src=src, st=st, o=o: e.transpose(bk.ap[:, o:o + 32], src[:, 128 * st:128 * st + 128],
                                                                  ident[0:32, 0:32]), tk, bk.free, t_par)
        yield
        t = act(lambda e: e.activation(dcol, bk.ap[:, 0:128], ACT.Copy), t)
        AUX.give(bk, t)
        tm["dt"] = t
        tm["acs"] = t17

    def post_dt(ct, bank, tok, fr):
        tasks.append(("dt", dt_task(bank, tok, fr)))
        drain("dt")

    s_dec = [None]

    def post_xbc(dstf):
        def post(ct, bank, tok, fr):
            i = ct - 16
            out, ofree = dstf(i)
            r, s = RR.take(), TR.take()
            t = evac(bank, tok, fr, r.ap[:, 3:259], r.free)
            t = conv(r.ap, s.ap, 4, 0, "conv_w", i, 24, t, s.free, bias=P("conv_b", i))
            RR.give(r, t)
            t2 = act(lambda e: e.activation(out, s.ap, ACT.Silu), t, ofree)
            TR.give(s, t2)
            tm[("xbc", i)] = t2
            if 16 <= i < 24 and i >= 20:
                tasks.append(("cb", cb_task(i - 20)))
        return post

    def bc_dst(i):
        o = am["BT"] + 256 * (i - 16)
        return a_(o, 256), None

    def cb_task(g):
        yield
        bk = AUX.take()
        B, C = a_(am["BT"] + 256 * g, 256), a_(am["CT"] + 256 * g, 256)
        w = [tm[("xbc", 16 + g)], tm[("xbc", 20 + g)], bk.free]
        pe(lambda e: e.matmul(bk.ap[:, 0:256], B[:, 0:128], C[:, 0:256], start=True, stop=True), *w)
        t = pe(lambda e: e.matmul(bk.ap[:, 256:384], B[:, 128:256], C[:, 128:256], start=True, stop=True))
        yield
        t = dve(lambda e: e.tensor_tensor(a_(am["cbm"] + 384 * g, 384), bk.ap[:, 0:384], mask, ALU.mult), t, tm["mask"])
        AUX.give(bk, t)
        tm[("cb", g)] = t

    xsfree, zsfree = [[] for _ in range(8)], [[] for _ in range(8)]

    def XS(j):
        return a_(am["XS"] + 256 * (j % 8), 256)

    def ZS(j):
        return a_(am["ZS"] + 256 * (j % 8), 256)

    def post_z(ct, bank, tok, fr):
        j = ct
        s = TR.take()
        t = evac(bank, tok, fr, s.ap, s.free)
        t2 = act(lambda e: e.activation(ZS(j), s.ap, ACT.Silu), t, zsfree[j % 8])
        TR.give(s, t2)
        tm[("z", j)] = t2
        tasks.append((f"ssd{j // 4}", ssd_task(j)))

    dfree, mfree, xfree = [[]], [[]], [[]]
    gnorm = [None]

    def ssd_task(j):
        g = j // 4
        if j % 4 == 0:
            gnorm[0] = Norm(4)
        xs, xt = XS(j), tm[("xbc", j)]
        tb, bb = AUX.take(), AUX.take()
        for st in range(2):
            t1 = pe(lambda e, st=st: e.transpose(tb.ap[:, 128 * st:128 * st + 128], xs[:, 128 * st:128 * st + 128], ident[:, :]),
                    xt, tb.free, t_par)
        for hh in range(2):
            t2 = pe(lambda e, hh=hh: e.matmul(bb.ap[:, 256 * hh:256 * hh + 256],
                                              ident[0:32, 2 * j + hh:2 * j + hh + 1].to_broadcast([32, 128]), acs,
                                              start=True, stop=True), tm["acs"], bb.free)
        yield
        xdt = a_(am["xdt"], 256)
        t3 = None
        for st in range(2):
            o = xdt[:, 128 * st:128 * st + 128].rearrange("p (a b) -> p a b", a=2)
            i0 = tb.ap[:, 128 * st:128 * st + 128].rearrange("p (a b) -> p a b", a=2)
            c = 64 + 32 * st + 2 * j
            i1 = dcol[:, c:c + 2].unsqueeze(2).to_broadcast([128, 2, 64])
            t3 = dve(lambda e, o=o, i0=i0, i1=i1: e.tensor_tensor(o, i0, i1, ALU.mult), t1, tm["dt"], xfree[0])
        AUX.give(tb, t3)
        Dd, M = a_(am["D"], 768), a_(am["M"], 768)
        for hh in range(2):
            for st in range(2):
                o = Dd[:, 384 * hh + 256 * st:384 * hh + 256 + 128 * st]
                i0 = bb.ap[:, 256 * hh + 128 * st:256 * hh + 256]
                sc = dcol[:, 32 * st + 2 * j + hh:32 * st + 2 * j + hh + 1]
                t4 = dve(lambda e, o=o, i0=i0, sc=sc: e.tensor_scalar(o, i0, sc, 0.0, ALU.subtract, ALU.min),
                         t2, tm["dt"], dfree[0])
        AUX.give(bb, t4)
        t5 = act(lambda e: e.activation(Dd, Dd, ACT.Exp), t4)
        yield
        cb = a_(am["cbm"] + 384 * g, 384)
        for hh in range(2):
            t6 = pool(lambda e, hh=hh: e.tensor_tensor(M[:, 384 * hh:384 * hh + 384], Dd[:, 384 * hh:384 * hh + 384], cb,
                                                       ALU.mult), t5, tm[("cb", g)], mfree[0])
        dfree[0] = [t6]
        yield
        yb = AUX.take()
        for hh in range(2):
            o = yb.ap[64 * hh:64 * hh + 64, 0:256]
            o2 = yb.ap[64 * hh:64 * hh + 64, 128:256]
            pe(lambda e, o=o, hh=hh: e.matmul(o, xdt[:, 64 * hh:64 * hh + 64], M[:, 384 * hh:384 * hh + 256],
                                              start=True, stop=False), t6, t3, yb.free, inc=False)
            t7 = pe(lambda e, o2=o2, hh=hh: e.matmul(o2, xdt[:, 128 + 64 * hh:192 + 64 * hh],
                                                     M[:, 384 * hh + 256:384 * hh + 384], start=False, stop=True))
        mfree[0] = [t7]
        xfree[0] = [t7]
        yield
        t8 = dve(lambda e: e.scalar_tensor_tensor(xs, xs, P("d_skip", j), yb.ap[:, 0:256], ALU.mult, ALU.add), t7, t1, t_par)
        AUX.give(yb, t8)
        t9 = pool(lambda e: e.tensor_tensor(xs, xs, ZS(j), ALU.mult), t8, tm[("z", j)])
        zsfree[j % 8] = [t9]
        s, t10 = gnorm[0].square(xs, t9)
        tm[("y", j)] = t9
        yield
        gnorm[0].total(s, t10)
        if j % 4 == 3:
            yield
            rs, rt = gnorm[0].finish(512, 1e-5)
            yield
            n0 = 4 * g

            def dst(k, ap, tok):
                xgtok[n0 + k] = split_to(XG, n0 + k, ap, tok, xgfree[0])
                xsfree[(n0 + k) % 8] = xgtok[n0 + k]
                return xgtok[n0 + k]
            normalise(rs, rt, [(XS(n0 + k), tm[("y", n0 + k)]) for k in range(4)], lambda k: P("ssd_norm", n0 + k), dst)

    def xs_dst(i):
        return XS(i), xsfree[i % 8]

    def residual(norm=None):
        def post(ct, bank, tok, fr):
            t = dve(lambda e: e.tensor_tensor(hk(ct), hk(ct), bank[:, 0:256], ALU.add), tok, h[ct])
            t = dve(lambda e: e.tensor_tensor(hk(ct), hk(ct), bank[:, 256:512], ALU.add), t)
            fr.append(t)
            h[ct] = t
            if norm:
                def task():
                    if ct == 0:
                        cur[0] = Norm(16)
                    s, ts = cur[0].square(hk(ct), t)
                    yield
                    cur[0].total(s, ts)
                tasks.append(("res", task()))
        return post

    cur = [None]

    def next_norm(gain, eps=1e-5):
        drain()
        rs, rt = cur[0].finish(D, eps)
        x1free[0] = done()
        normalise(rs, rt, [(hk(k), h[k]) for k in range(16)], lambda k: P(gain, k), to_X1)

    def load_mask():
        tm["mask"] = dma("sp", s_mask, mask, T_["mask"])

    def pre_bc():
        load_mask()

    proj(T_["w_dt"], 0, range(2), X1k, post_dt, w=128, kn=8, pre=pre_bc)
    for c in range(4):
        proj(T_["w_zx"], 16 + c, range(4), X1k, post_xbc(bc_dst))

    def pre_wsc():
        drain("sc0")
        drain("sc1")
    for c in range(8):
        proj(T_["w_osc"], c, range(4), XGk, residual(), pre=pre_wsc if c == 0 else None)

    def pre_ssd():
        drain()
        xgfree[0] = done()
    for g in range(4):
        for c in range(2):
            proj(T_["w_zx"], 8 + 2 * g + c, range(4), X1k, post_xbc(xs_dst), pre=pre_ssd if g == c == 0 else None)
        for c in range(2):
            proj(T_["w_zx"], 2 * g + c, range(4), X1k, post_z)
    for c in range(8):
        proj(T_["w_ossd"], c, range(3), XGk, residual(), pre=(lambda: drain("ssd2")) if c == 0 else None)
    for c in range(8):
        proj(T_["w_ossd"], c, [3], XGk, residual(True), pre=(lambda: drain("ssd3")) if c == 0 else None)

    ax = A_XA
    SC = 128.0 ** -0.5
    pfree = [[]]

    def post_q(ct, bank, tok, fr):
        t = evac(bank, tok, fr, a_(ax["qT"] + 256 * ct, 256), pfree[0])
        tasks.append(("att", att_task(ct, t)))

    def att_task(hd, t):
        qT = a_(ax["qT"] + 256 * hd, 256)
        sb = AUX.take()
        for st in range(2):
            t = pe(lambda e, st=st: e.matmul(sb.ap[:, 256 * st:256 * st + 256], qT[:, 128 * st:128 * st + 128], kT(hd),
                                             start=True, stop=True), t, kT_tok[hd], sb.free)
        yield
        Pp, PT = a_(ax["P"] + 512 * hd, 512), a_(ax["PT"] + 512 * hd, 512)
        st_ = a_(ax["st"] + 16 * hd, 16)
        tt = []
        for st in range(2):
            mx, nb, sm, ri = (st_[:, 8 * st + i:8 * st + i + 1] for i in range(4))
            src = sb.ap[:, 256 * st:256 * st + 256]
            o = Pp[:, 256 * st:256 * st + 256]
            ta = dve(lambda e, mx=mx, src=src: e.tensor_reduce(mx, src, AX.X, ALU.max), t, pfree[0])
            tb = dve(lambda e, nb=nb, mx=mx: e.tensor_scalar(nb, mx, -SC, None, ALU.mult), ta)
            tt.append((tb, nb, sm, ri, src, o))
        tq = []
        for tb, nb, sm, ri, src, o in tt:
            tc = act(lambda e, nb=nb, sm=sm, src=src, o=o: e.activation(o, src, ACT.Exp, bias=nb, scale=SC, accum_out=sm),
                     tb, ta)
            td = dve(lambda e, sm=sm, ri=ri: e.reciprocal(ri, sm), tc)
            tq.append(dve(lambda e, o=o, ri=ri: e.tensor_scalar(o, o, ri, None, ALU.mult), td))
        AUX.give(sb, tc)
        yield
        pb = AUX.take()
        for mt in range(2):
            for st in range(2):
                t = pe(lambda e, mt=mt, st=st: e.transpose(pb.ap[:, 256 * mt + 128 * st:256 * mt + 128 * st + 128],
                                                           Pp[:, 256 * st + 128 * mt:256 * st + 128 * mt + 128], ident[:, :]),
                       tq, pb.free)
        yield
        t = act(lambda e: e.activation(PT, pb.ap[:, :], ACT.Copy), t)
        AUX.give(pb, t)
        yield
        ob = AUX.take()
        for mt in range(2):
            t = pe(lambda e, mt=mt: e.matmul(ob.ap[:, 0:256], vv(mt)[:, 128 * hd:128 * hd + 128],
                                             PT[:, 256 * mt:256 * mt + 256], start=(mt == 0), stop=(mt == 1)),
                   t, v_tok, ob.free)
        s = TR.take()
        t = act(lambda e: e.activation(s.ap, ob.ap[:, 0:256], ACT.Copy), t, s.free)
        AUX.give(ob, t)
        xgtok[hd] = split_to(XG, hd, s.ap, t, xgfree[0])
        TR.give(s, xgtok[hd])

    def pre_q():
        next_norm("norm_xa")
        pfree[0] = done()
        xgfree[0] = done()
    for c in range(2):
        proj(T_["w_q"], c, range(4), X1k, post_q, pre=pre_q if c == 0 else None)
    for c in range(8):
        proj(T_["w_o"], c, [0], XGk, residual(True), pre=(lambda: drain("att")) if c == 0 else None)

    af = A_FIL
    s_fil, s_f1 = sem("d_fil"), sem("d_f1")

    def sine(z, k, t):
        MAGIC = 12582912.0
        C1, C2, C3 = 6.28125, 0.0019350051879882812, 3.0199159819e-07
        t = dve(lambda e: e.tensor_scalar(k, z, 0.15915494309189535, MAGIC, ALU.mult, ALU.add), t)
        t = dve(lambda e: e.tensor_scalar(k, k, -MAGIC, None, ALU.add), t)
        for c in (C1, C2, C3):
            t = dve(lambda e, c=c: e.scalar_tensor_tensor(z, k, -c, z, ALU.mult, ALU.add), t)
        t = dve(lambda e: e.tensor_scalar(z, z, 3.1415925, -3.1415925, ALU.min, ALU.max), t)
        return act(lambda e: e.activation(z, z, ACT.Sin), t)

    def filter_task(fr):
        F, G, dec, w3, hf = (a_(af[n], w) for n, w in (("F", 1024), ("G", 1024), ("dec", 1536), ("w3", 1536), ("hf", 3072)))
        feat, w1, w2 = a_(af["feat"], 256, 33), a_(af["w1"], 64, 33), a_(af["w2"], 64, 64)
        z, kk, z2 = (a_(af["s"] + 256 * i, 256, 64) for i in range(3))
        K = a_(af["K"], 3840).rearrange("p (m c) -> p m c", m=5)
        dma("sp", s_f1, feat, T_["feat"], fr)
        dma("sp", s_f1, w1, T_["f_w1"], fr)
        dma("sp", s_f1, w2, T_["f_w2"], fr)
        t_f1 = dma("sp", s_f1, w3[0:64, :], T_["f_w3"], fr)
        dma("sp", s_fil, F, T_["dftF"], fr)
        dma("sp", s_fil, G, T_["dftG"], fr)
        t_fil = dma("sp", s_fil, dec, T_["decay"], fr)
        for _ in range(8):
            yield
        bk = AUX.take()
        t = pe(lambda e: e.matmul(bk.ap[0:64, 0:256], w1, feat, start=True, stop=True), t_f1, bk.free)
        yield
        t = dve(lambda e: e.tensor_scalar(z, bk.ap[0:64, 0:256], P("f_b1", p=64), P("f_fr1", p=64), ALU.add, ALU.mult), t, t_par)
        t = sine(z, kk, t)
        yield
        yield
        t = pe(lambda e: e.matmul(bk.ap[0:64, 0:256], w2, z, start=True, stop=True), t)
        yield
        t = dve(lambda e: e.tensor_scalar(z2, bk.ap[0:64, 0:256], P("f_b2", p=64), P("f_fr2", p=64), ALU.add, ALU.mult), t)
        AUX.give(bk, t)
        tz = sine(z2, kk, t)
        yield
        yield
        thf = []
        for st in range(2):
            for c in range(4):
                bk = AUX.take()
                t = pe(lambda e, st=st, c=c, bk=bk: e.matmul(bk.ap[:, 0:384], z2[:, 128 * st:128 * st + 128],
                                                             w3[0:64, 384 * c:384 * c + 384], start=True, stop=True), tz, bk.free)
                yield
                o = 1536 * st + 384 * c
                d = 768 * st + 384 * (c % 2)
                t = dve(lambda e, o=o, d=d, bk=bk: e.tensor_tensor(hf[:, o:o + 384], bk.ap[:, 0:384], dec[:, d:d + 384], ALU.mult),
                        t, t_fil)
                AUX.give(bk, t)
                thf.append(t)
                yield
        tk = {}
        for m in range(4):
            for c in range(2):
                bk = AUX.take()
                n = 0
                for st in range(2):
                    for mat, base in ((F, 0), (G, 768)):
                        lhs = mat[:, 512 * st + 128 * m:512 * st + 128 * m + 128]
                        rhs = hf[:, 1536 * st + base + 384 * c:1536 * st + base + 384 * c + 384]
                        t = pe(lambda e, lhs=lhs, rhs=rhs, n=n, bk=bk: e.matmul(bk.ap[:, 0:384], lhs, rhs, start=(n == 0), stop=(n == 3)),
                               thf, t_fil, bk.free)
                        n += 1
                yield
                tk[m, c] = act(lambda e, m=m, c=c, bk=bk: e.activation(K[:, m, 384 * c:384 * c + 384], bk.ap[:, 0:384], ACT.Copy), t)
                AUX.give(bk, tk[m, c])
        t = dve(lambda e: e.tensor_copy(K[:, 4, :], K[:, 0, :]), tk[0, 0], tk[0, 1])
        t = dve(lambda e: e.tensor_copy(K[0:1, 4, :], K[0:1, 2, :]), t, tk[2, 0], tk[2, 1])
        t = dve(lambda e: e.memset(K[0:1, 2, :], 0.0), t)
        tm["K"] = [t] + list(tk.values())
        tm["F"] = t_fil

    g_tok = [None, None]
    sgfree = [None, None]
    ffn_free = [[]]
    slot_free = [[] for _ in range(16)]
    SG = [None, None]

    def pre_ffn():
        next_norm("norm_ffn")
        fr = done()
        for i in range(16):
            slot_free[i] = fr
        tasks.append(("filter", filter_task(fr)))

    def post_gate(ct, bank, tok, fr):
        i = ct % 2
        s = TR.take()
        t = evac(bank, tok, fr, s.ap, s.free)
        g_tok[i] = act(lambda e: e.activation(s.ap, s.ap, ACT.Silu), t)
        SG[i] = s

    def post_up(ct, bank, tok, fr):
        i = ct % 2
        s = TR.take()
        t = evac(bank, tok, fr, s.ap, s.free)
        g = SG[i]
        t = dve(lambda e: e.tensor_tensor(s.ap, s.ap, g.ap, ALU.mult), t, g_tok[i])
        TR.give(g, t)
        xgtok[ct % 16] = split_to(XG, ct % 16, s.ap, t, slot_free[ct % 16])
        TR.give(s, xgtok[ct % 16])

    def after_down(kts, post):
        def p(ct, bank, tok, fr):
            post(ct, bank, tok, fr)
            if ct == 15:
                for k in kts:
                    slot_free[k % 16] = [tok]
        return p

    def ffn(Wg, Wu, Wd, pg, pu, pre):
        chunks = [list(range(8 * c, min(8 * c + 8, FT))) for c in range(6)]
        nextc = 0
        for p in range(FT // 2):
            proj(Wg, p, range(4), X1k, pg, pre=pre if p == 0 else None)
            proj(Wu, p, range(4), X1k, pu)
            done_t = 2 * p
            while nextc < 5 and chunks[nextc][-1] < done_t:
                kts = chunks[nextc]
                for c in range(8):
                    proj(Wd, c, [k // 4 for k in kts[::4]], XGk, after_down(kts, residual()))
                nextc += 1
        kts = chunks[5]
        for c in range(8):
            proj(Wd, c, [k // 4 for k in kts[::4]], XGk, after_down(kts, residual(True)))

    ffn(T_["w_gate"], T_["w_up"], T_["w_down"], post_gate, post_up, pre_ffn)

    ab, gb = A_B2, G_B2
    s_b2 = sem("d_b2")
    g_ = lambda off, n: Gf[:, off:off + n]

    def pre_b2():
        drain()
        rs, rt = cur[0].finish(D, 1e-5)
        x1free[0] = done()
        nn = Norm(16)
        pend = None
        for k in range(16):
            h[k] = dve(lambda e, k=k: e.scalar_tensor_tensor(hk(k), hk(k), P("norm_final", k), rs.ap, ALU.mult, ALU.mult), rt, h[k])
            nn.add(hk(k), h[k])
        TR.give(rs, h[15])
        rs2, rt2 = nn.finish(D, 1e-6)
        fr = x1free[0]
        for dst, name in ((a_(ab["IF"], 1024), "dftI"), (a_(ab["ws"], 768), "gm_ws"), (a_(ab["bs"], 768), "gm_bs"),
                          (a_(ab["wp"], 512), "pool_w"), (g_(gb["gain"], 1536), "gm_gb")):
            tm["b2"] = dma("sp", s_b2, dst, T_[name], fr)
        tm["b2free"] = fr
        normalise(rs2, rt2, [(hk(k), h[k]) for k in range(16)], lambda k: P("norm_mix_2", k), to_X1)

    def cconv(bank, tok, fr, out, ofree, wname, bname, i, nch):
        r = RR.take()
        t = evac(bank, tok, fr, r.ap[:, 3:259], r.free)
        t = conv(r.ap, out, 3, 2, wname, i, nch, t, ofree, bias=P(bname, i))
        RR.give(r, t)
        return t

    zT = lambda e: a_(ab["z"] + 256 * e, 256)
    ztoks = [None] * 6
    x0toks = [None] * 6

    def post_hv(ct, bank, tok, fr):
        e_ = ct - 16
        ztoks[e_] = cconv(bank, tok, fr, zT(e_), tm["b2free"], "hy_w", "hy_b", 12 + e_, 18)

    def post_hx1(ct, bank, tok, fr):
        e_ = ct - 10
        s = TR.take()
        t = cconv(bank, tok, fr, s.ap, s.free, "hy_w", "hy_b", 6 + e_, 18)
        ztoks[e_] = dve(lambda e: e.tensor_tensor(zT(e_), zT(e_), s.ap, ALU.mult), t, ztoks[e_])
        TR.give(s, ztoks[e_])
        if e_ == 5:
            tasks.append(("hyena", hyena_task()))

    def post_hx0(ct, bank, tok, fr):
        e_ = ct - 4
        x0toks[e_] = cconv(bank, tok, fr, a_(ab["x0"] + 256 * e_, 256), tm["b2free"], "hy_w", "hy_b", e_, 18)

    def transposes(src, toks, dst, fr):
        out = []
        for st in range(2):
            for c in range(2):
                bk = AUX.take()
                for i in range(3):
                    e_ = 3 * c + i
                    t = pe(lambda e, st=st, i=i, e_=e_, bk=bk: e.transpose(bk.ap[:, 128 * i:128 * i + 128],
                                                                          src(e_)[:, 128 * st:128 * st + 128], ident[:, :]),
                           toks[e_], bk.free)
                yield
                o = dst[:, 768 * st + 384 * c:768 * st + 384 * c + 384]
                t = act(lambda e, o=o, bk=bk: e.activation(o, bk.ap[:, 0:384], ACT.Copy), t, fr)
                AUX.give(bk, t)
                out.append(t)
        tm["tr"] = out

    def hyena_task():
        K = a_(ab["K"], 3840).rearrange("p (m c) -> p m c", m=5)
        F, IF = a_(ab["F"], 1024), a_(ab["IF"], 1024)
        zt, zf = g_(gb["zt"], 1536), g_(gb["zf"], 1536).rearrange("p (m c) -> p m c", m=4)
        ta, tb, tc = (a_(ab["t"] + 384 * i, 384) for i in range(3))
        yield from transposes(zT, ztoks, zt, tm["b2free"])
        tr = tm["tr"]
        zfree = tm["b2free"]
        tfree = None
        for hf in range(2):
            sl = slice(384 * hf, 384 * hf + 384)
            tf = []
            for m in range(4):
                bk = AUX.take()
                for st in range(2):
                    lhs = F[:, 512 * st + 128 * m:512 * st + 128 * m + 128]
                    rhs = zt[:, 768 * st + 384 * hf:768 * st + 384 * hf + 384]
                    t = pe(lambda e, lhs=lhs, rhs=rhs, st=st, bk=bk: e.matmul(bk.ap[:, 0:384], lhs, rhs, start=(st == 0), stop=(st == 1)),
                           tr, tm["F"], bk.free)
                yield
                t = act(lambda e, m=m, bk=bk: e.activation(zf[:, m, :], bk.ap[:, 0:384], ACT.Copy), t, zfree)
                AUX.give(bk, t)
                tf.append(t)
            if hf == 1:
                tm["zt_done"] = t
            ty = []
            for m in range(2):
                zr, zi, kr, ki = zf[:, m, :], zf[:, 2 + m, :], K[:, m, sl], K[:, 2 + m, sl]
                k2 = K[:, 4, sl] if m == 0 else K[:, 1, sl]
                w = [tf[m], tf[2 + m], tm["K"], tfree]
                t1 = dve(lambda e, zr=zr, kr=kr: e.tensor_tensor(ta, zr, kr, ALU.mult), *w)
                t2 = pool(lambda e, zi=zi, ki=ki: e.tensor_tensor(tb, zi, ki, ALU.mult), *w)
                t3 = dve(lambda e, zr=zr, ki=ki: e.tensor_tensor(tc, zr, ki, ALU.mult), *w)
                t4 = pool(lambda e, zi=zi, k2=k2: e.tensor_tensor(zi, zi, k2, ALU.mult), t2, *w)
                t5 = dve(lambda e, zr=zr: e.tensor_tensor(zr, ta, tb, ALU.subtract), t1, t2, t3)
                t6 = dve(lambda e, zi=zi: e.tensor_tensor(zi, zi, tc, ALU.add), t4, t3)
                tfree = [t5, t6]
                ty += [t5, t6]
                yield
            zfree = []
            for i in range(3):
                e_ = 3 * hf + i
                bk = AUX.take()
                for m in range(4):
                    t = pe(lambda e, m=m, i=i, bk=bk: e.matmul(bk.ap[:, 0:256], zf[:, m, 128 * i:128 * i + 128],
                                                              IF[:, 256 * m:256 * m + 256], start=(m == 0), stop=(m == 3)),
                           ty, tm["b2"], bk.free)
                zfree.append(t)
                yield
                t = dve(lambda e, e_=e_, bk=bk: e.scalar_tensor_tensor(zT(e_), zT(e_), P("hy_skip", e_), bk.ap[:, 0:256],
                                                                      ALU.mult, ALU.add), t)
                AUX.give(bk, t)
                ztoks[e_] = t
        tm["zf_done"] = t

    def hyena_out():
        drain("hyena")
        for e_ in range(6):
            x0 = a_(ab["x0"] + 256 * e_, 256)
            t = dve(lambda e, e_=e_, x0=x0: e.tensor_tensor(x0, x0, zT(e_), ALU.mult), ztoks[e_], x0toks[e_])
            xgtok[4 + e_] = split_to(XG, 4 + e_, x0, t, [tm["zt_done"], tm["zf_done"]])

    vg = lambda e: a_(ab["vg"] + 256 * e, 256)
    vgtok = [None] * 6

    def post_gv(ct, bank, tok, fr):
        e_ = ct - 28
        s = TR.take()
        t = evac(bank, tok, fr, s.ap, s.free)
        vgtok[e_] = act(lambda e: e.activation(vg(e_), s.ap, ACT.Gelu_apprx_tanh), t, tm["b2free"])
        TR.give(s, vgtok[e_])
        if e_ == 5:
            tasks.append(("gmlp", gmlp_task()))

    def gmlp_task():
        vt = g_(gb["vt"], 1536)
        gain, bias = g_(gb["gain"], 768), g_(gb["gain"] + 768, 768)
        ws, bs = a_(ab["ws"], 768), a_(ab["bs"], 768)
        yield from transposes(vg, vgtok, vt, tm["b2free"])
        tr = tm["tr"]
        tv = []
        sm = TR.take()
        for st in range(2):
            v = vt[:, 768 * st:768 * st + 768]
            stt = sm.ap[:, 32 * st:32 * st + 12]
            mv = sm.ap[:, 32 * st + 12:32 * st + 14]
            rr, u, y = (sm.ap[:, 32 * st + 14 + i:32 * st + 15 + i] for i in range(3))
            for c in range(2):
                t = dve(lambda e, c=c, v=v, stt=stt: e.bn_stats(stt[:, 6 * c:6 * c + 6], v[:, 384 * c:384 * c + 384]), tr, sm.free)
            t = dve(lambda e, mv=mv, stt=stt: e.bn_aggr(mv, stt), t)
            t1 = dve(lambda e, mv=mv, rr=rr: e.tensor_scalar(rr, mv[:, 1:2], 1e-5, None, ALU.add), t)
            t2 = act(lambda e, u=u, rr=rr: e.activation(u, rr, ACT.Ln), t1)
            t2 = act(lambda e, u=u, y=y: e.activation(y, u, ACT.Exp, scale=-0.5), t2)
            t3 = dve(lambda e, u=u, y=y: e.tensor_tensor(u, y, y, ALU.mult), t2)
            t3 = dve(lambda e, u=u, rr=rr: e.scalar_tensor_tensor(u, u, -0.5, rr, ALU.mult, ALU.mult), t3)
            t3 = dve(lambda e, u=u, y=y: e.scalar_tensor_tensor(y, u, 1.5, y, ALU.add, ALU.mult), t3)
            yield
            t4 = dve(lambda e, v=v, mv=mv, y=y: e.tensor_scalar(v, v, mv[:, 0:1], y, ALU.subtract, ALU.mult), t3)
            t5 = pool(lambda e, v=v: e.tensor_tensor(v, v, gain, ALU.mult), t4, tm["b2"])
            t6 = pool(lambda e, v=v: e.tensor_tensor(v, v, bias, ALU.add), t5)
            tv.append(t6)
            yield
        TR.give(sm, tv)
        tm["gain_done"] = tv
        for e_ in range(6):
            bk = AUX.take()
            for st in range(2):
                t = pe(lambda e, st=st, e_=e_, bk=bk: e.matmul(bk.ap[:, 128 * st:128 * st + 128],
                                                              vt[:, 768 * st + 128 * e_:768 * st + 128 * e_ + 128],
                                                              ws[:, 128 * e_:128 * e_ + 128], start=True, stop=True),
                       tv, tm["b2"], bk.free)
            yield
            o = vg(e_).rearrange("p (s q) -> p s q", s=2)
            i0 = bk.ap[:, 0:256].rearrange("p (s q) -> p s q", s=2)
            i1 = bs[:, 128 * e_:128 * e_ + 128].unsqueeze(1).to_broadcast([128, 2, 128])
            vgtok[e_] = dve(lambda e, o=o, i0=i0, i1=i1: e.tensor_tensor(o, i0, i1, ALU.add), t, tr)
            AUX.give(bk, vgtok[e_])
        tm["vt_done"] = t

    def pool_task(g, s, t0, pfr):
        half = 2 ** g
        w = 2 * half
        ce = a_(ab["rc"], 280)
        t = dve(lambda e: e.memset(ce[:, 0:9], 0.0), pfr)
        ta = dve(lambda e: e.tensor_tensor_scan(ce[:, 9:265], cones[0], s.ap, 0.0, ALU.mult, ALU.add), t0, pfr, cones[1])
        tb = dve(lambda e: e.tensor_scalar(ce[:, 265:273], ce[:, 0:8], ce[:, 264:265], None, ALU.add), t, ta)
        d = TR.take()
        tc = dve(lambda e: e.tensor_tensor(d.ap, ce[:, 8 + half:264 + half], ce[:, 8 - half:264 - half], ALU.subtract), tb, d.free)
        t1 = dve(lambda e: e.tensor_tensor(d.ap[:, 0:8], d.ap[:, 0:8], P("rcnt", 16 * g, 8), ALU.mult), tc)
        t2 = dve(lambda e: e.tensor_tensor(d.ap[:, 248:256], d.ap[:, 248:256], P("rcnt", 16 * g + 8, 8), ALU.mult), tc)
        t3 = dve(lambda e: e.scalar_tensor_tensor(d.ap, d.ap, 1.0 / w, s.ap, ALU.mult, ALU.subtract), t1, t2)
        TR.give(s, t3)
        pf[0] = [t3]
        yield
        bk = AUX.take()
        t = pe(lambda e: e.matmul(bk.ap[:, 0:256], a_(ab["wp"] + 128 * g, 128), d.ap, start=True, stop=True), t3, tm["b2"], bk.free)
        yield
        t = dve(lambda e: e.tensor_scalar(d.ap, bk.ap[:, 0:256], P("pool_b", g), P("pool_scale", g), ALU.add, ALU.mult), t)
        AUX.give(bk, t)
        xgtok[g] = split_to(XG, g, d.ap, t, tm["gain_done"])
        TR.give(d, xgtok[g])

    pf = [None]
    cones = [a_(ab["rc"] + 288, 256), None]

    def post_pool(ct, bank, tok, fr):
        s = TR.take()
        t = evac(bank, tok, fr, s.ap, s.free)
        if ct == 0:
            pf[0] = tm["b2free"]
            cones[1] = dve(lambda e: e.memset(cones[0], 1.0), pf[0])
        if ct % 2 == 0:
            drain("gmlp")
            hyena_out() if ct == 0 else None
        tasks.append(("pool", pool_task_late(ct, s, t)))

    def pool_task_late(ct, s, t):
        yield from pool_task(ct, s, t, pf[0])

    def post_gu(ct, bank, tok, fr):
        e_ = ct - 22
        if e_ == 0:
            drain()
        s = TR.take()
        t = evac(bank, tok, fr, s.ap, s.free)
        t = act(lambda e: e.activation(s.ap, s.ap, ACT.Gelu_apprx_tanh), t)
        t = dve(lambda e: e.tensor_tensor(s.ap, s.ap, vg(e_), ALU.mult), t, vgtok[e_])
        xgtok[10 + e_] = split_to(XG, 10 + e_, s.ap, t, [tm["vt_done"], tm["zf_done"]])
        TR.give(s, xgtok[10 + e_])

    W2 = T_["w_in_2"]
    first = True
    for base, n, post in ((8, 3, post_hv), (5, 3, post_hx1), (14, 3, post_gv), (2, 3, post_hx0), (0, 2, post_pool), (11, 3, post_gu)):
        for c in range(n):
            proj(W2, base + c, range(4), X1k, post, pre=pre_b2 if first else None)
            first = False
    for c in range(8):
        proj(T_["w_out_2"], c, range(4), XGk, residual(True), pre=drain if c == 0 else None)

    def pre_ffn2():
        next_norm("norm_ffn_2", 1e-6)
        fr = done()
        for i in range(16):
            slot_free[i] = fr

    def post_gate2(ct, bank, tok, fr):
        i = ct % 2
        s = TR.take()
        t = cconv(bank, tok, fr, s.ap, s.free, "fc_w", "fc_b", ct, 88)
        g_tok[i] = act(lambda e: e.activation(s.ap, s.ap, ACT.Silu), t)
        SG[i] = s

    def post_val2(ct, bank, tok, fr):
        i = ct % 2
        s = TR.take()
        t = cconv(bank, tok, fr, s.ap, s.free, "fc_w", "fc_b", FT + ct, 88)
        g = SG[i]
        t = pool(lambda e: e.tensor_tensor(s.ap, s.ap, g.ap, ALU.mult), t, g_tok[i])
        TR.give(g, t)
        xgtok[ct % 16] = split_to(XG, ct % 16, s.ap, t, slot_free[ct % 16])
        TR.give(s, xgtok[ct % 16])

    ffn(T_["w_gate_2"], T_["w_val_2"], T_["w_down_2"], post_gate2, post_val2, pre_ffn2)

    load_x()
    start()
    run()
    drain()
    rs, rt = cur[0].finish(D, 1e-6)
    s_out = [sem(f"d_out{i}") for i in range(4)]
    outs = []
    for k in range(16):
        t = dve(lambda e, k=k: e.scalar_tensor_tensor(hk(k), hk(k), P("norm_final_2", k), rs.ap, ALU.mult, ALU.mult), rt, h[k])
        if k % 4 == 3:
            i = k // 4
            outs.append(dma("sp", s_out[i], T_["out"][:, i * 1024:(i + 1) * 1024], hT[:, i * 1024:(i + 1) * 1024], t))

    with nc.Block() as block:
        @block.sync
        def _(eng):
            for waits, fn, _ in q["sp"].items:
                for s, v in waits:
                    eng.wait_ge(s, v)
                fn(eng)
            for s, v in outs:
                eng.wait_ge(s, v)

        @block.tensor
        def _(eng):
            q["pe"].play(eng)

        @block.vector
        def _(eng):
            q["dve"].play(eng)

        @block.scalar
        def _(eng):
            q["act"].play(eng)

        @block.gpsimd
        def _(eng):
            q["pool"].play(eng)

    for g in reversed(pguards):
        g.__exit__(None, None, None)
    slab.__exit__(None, None, None)
    for g in reversed(sems):
        g.__exit__(None, None, None)


def kernel(**inputs):
    import math
    import numpy as np
    import concourse.bacc as bacc
    from concourse.bass_utils import run_bass_kernel_spmd

    f = np.float32
    I = {k: np.asarray(v) for k, v in inputs.items()}

    def pack(w, n=256, k=4):
        r, c = w.shape
        return np.ascontiguousarray(w.reshape(r // (128 * k), k, 128, c // n, n).transpose(3, 0, 2, 1, 4)).reshape(
            c // n, r // (128 * k), 128, k * n)

    def cols(v):
        return v.reshape(-1, 128).T

    def taps(w):
        return w.reshape(-1, 128).T

    def pad(v):
        o = np.zeros((128, 1), f)
        o[:v.shape[0], 0] = v
        return o

    w_in = I["w_in"][0]
    arr = {}
    arr["w_zx"] = pack(w_in[:, 0:5120])
    wd = np.zeros((2048, 128), f)
    wd[:, 0:32] = w_in[:, 5120:5152]
    arr["w_dt"] = pack(wd, 128, 8)
    arr["w_sc"] = pack(w_in[:, 5152:])
    arr["w_ossd"] = pack(I["w_out"][0][0:2048])
    arr["w_osc"] = pack(I["w_out"][0][2048:])
    for n in ("w_q", "w_k", "w_v", "w_o", "w_gate", "w_up", "w_down"):
        arr[n] = pack(I[n][0])
    arr["w_in_2"] = pack(I["w_in_2"][0])
    arr["w_out_2"] = pack(I["w_out_2"][0])
    arr["w_gate_2"] = pack(I["ffn_w_up_2"][0][:, 0:5632])
    arr["w_val_2"] = pack(I["ffn_w_up_2"][0][:, 5632:])
    arr["w_down_2"] = pack(I["ffn_w_down_2"][0])

    def fm(x):
        return np.ascontiguousarray(x.T.reshape(-1, 128, 256).transpose(1, 0, 2)).reshape(128, -1)

    arr["xT"] = fm(I["x"][0])
    arr["memT"] = fm(I["mem"][0])
    rc = np.ones((4, 16), f)
    t = np.arange(256)
    for g, w in enumerate((2, 4, 8, 16)):
        cnt = np.minimum(t + w // 2 - 1, 255) - np.maximum(t - w // 2, 0) + 1
        full = (w / cnt).astype(f)
        rc[g, 0:8], rc[g, 8:16] = full[0:8], full[248:256]
    P = {
        "norm_mix": cols(I["norm_mix"][0]), "conv_w": taps(I["ssd_conv_w"][0]), "conv_b": cols(I["ssd_conv_b"][0]),
        "ssd_norm": cols(I["ssd_norm"][0]), "d_skip": cols(np.repeat(I["d_skip"][0], 64)),
        "sc_w": taps(I["sc_conv_w"][0]), "sc_norm": cols(I["sc_norm"][0]), "mem_norm": cols(I["mem_norm"]),
        "norm_xa": cols(I["norm_xa"][0]), "norm_ffn": cols(I["norm_ffn"][0]), "norm_final": cols(I["norm_final"]),
        "norm_mix_2": cols(I["norm_mix_2"][0]), "pool_b": cols(I["pool_b_2"][0].reshape(-1)),
        "pool_scale": cols(I["pool_scale_2"][0]), "hy_w": taps(I["hy_short_w_2"][0]), "hy_b": cols(I["hy_short_b_2"][0]),
        "hy_skip": cols(I["hy_skip_2"][0]), "norm_ffn_2": cols(I["norm_ffn_2"][0]), "fc_w": taps(I["ffn_conv_w_2"][0]),
        "fc_b": cols(I["ffn_conv_b_2"][0]), "norm_final_2": cols(I["norm_final_2"]), "dt_bias": pad(I["dt_bias"][0]),
        "a_log": pad(I["a_log"][0]), "f_b1": pad(I["hy_filt_b1_2"][0]), "f_fr1": pad(I["hy_filt_freq1_2"][0]),
        "f_b2": pad(I["hy_filt_b2_2"][0]), "f_fr2": pad(I["hy_filt_freq2_2"][0]),
        "rcnt": np.broadcast_to(rc.reshape(1, 64), (128, 64)),
    }
    arr["par"] = np.ascontiguousarray(np.concatenate([P[n] for n, _ in PARAMS], axis=1))
    arr["ident"] = np.eye(128, dtype=f)
    s_, l_ = np.arange(128)[:, None], np.arange(128)[None, :]
    tri = (l_ >= s_).astype(f)
    arr["mask"] = np.ascontiguousarray(np.concatenate([tri, np.ones((128, 128), f), tri], axis=1))

    n = np.arange(256)[:, None]
    b = np.arange(256)[None, :]
    ang = 2 * np.pi * ((n * b) % 512) / 512
    sgn = (1.0 - 2.0 * (n % 2))
    Fm = np.concatenate([np.cos(ang), -np.sin(ang)], axis=1)
    Fm[:, 256:257] = sgn
    Gm = np.concatenate([np.cos(ang), np.sin(ang)], axis=1)
    Gm[:, 256:257] = sgn
    Gm[0, :] = 0.0
    wgt = np.full((256, 1), 2.0)
    wgt[0] = 1.0
    Im = np.concatenate([wgt * np.cos(ang.T), -wgt * np.sin(ang.T)], axis=0) / 512
    Im[256, :] = sgn[:, 0] / 512

    def rows(m, k):
        return np.ascontiguousarray(m.astype(f).reshape(k, 128, -1).transpose(1, 0, 2)).reshape(128, -1)
    arr["dftF"], arr["dftG"], arr["dftI"] = rows(Fm, 2), rows(Gm, 2), rows(Im, 4)
    tt = np.linspace(0.0, 1.0, 256, dtype=f)[:, None]
    ww = (f(2.0 * math.pi) * np.arange(256, dtype=f)[:, None] / f(256)).astype(f)
    ff = np.linspace(1e-4, 15, 16, dtype=f)[None, :]
    arr["feat"] = np.ascontiguousarray(np.concatenate([tt, np.cos(ff * ww), -np.sin(ff * ww)], axis=1).astype(f).T)
    deltas = np.linspace(math.log(1e-2) / 1.5, math.log(1e-2) / 0.3, 768, dtype=f)
    arr["decay"] = rows(np.exp(-tt * np.abs(deltas)[None, :]), 2)
    arr["f_w1"], arr["f_w2"], arr["f_w3"] = (np.ascontiguousarray(I[f"hy_filt_w{i}_2"][0]) for i in (1, 2, 3))
    arr["gm_ws"] = np.ascontiguousarray(I["gm_w_s_2"][0].transpose(2, 0, 1)).reshape(128, 768)
    arr["gm_bs"] = np.ascontiguousarray(np.broadcast_to(I["gm_b_s_2"][0].reshape(1, 768), (128, 768)))
    arr["pool_w"] = np.ascontiguousarray(I["pool_w_2"][0].transpose(1, 0, 2)).reshape(128, 512)
    arr["gm_gb"] = np.ascontiguousarray(np.broadcast_to(
        np.concatenate([I["gm_ln_g_2"][0], I["gm_ln_b_2"][0]])[None, :], (128, 1536)))

    nc = bacc.Bacc("TRN2", target_bir_lowering=False, num_devices=1)
    T_ = {k: nc.dram_tensor(f"in_{k}", v.shape, mybir.dt.from_np(v.dtype), kind="ExternalInput").ap() for k, v in arr.items()}
    T_["out"] = nc.dram_tensor("out_0", (128, 4096), F32, kind="ExternalOutput").ap()
    program(nc, T_)
    r = run_bass_kernel_spmd(nc, [{f"in_{k}": v for k, v in arr.items()}], core_ids=[0])
    o = r.results[0]["out_0"]
    return np.ascontiguousarray(o.reshape(128, 16, 256).transpose(2, 1, 0)).reshape(1, 256, 2048)
```

```python
from collections import deque

import concourse.bass as bass
from concourse import mybir

F32 = mybir.dt.float32
F32R = mybir.dt.float32r
ALU = mybir.AluOpType
ACT = mybir.ActivationFunctionType
AX = mybir.AxisListType

L = 256
D = 2048
KT = 16
FT = 44
NRAW = 4
NT = 13
NR = 6
NA = 13824
NW = 4
UK = 4
UN = UK * 256
SPLIT_AHEAD = 3
LANE = 3

PARAMS = [
    ("norm_mix", 16), ("conv_w", 96), ("conv_b", 24), ("ssd_norm", 16), ("d_skip", 16),
    ("sc_w", 48), ("sc_norm", 16), ("mem_norm", 16), ("norm_xa", 16), ("norm_ffn", 16),
    ("norm_final", 16), ("norm_mix_2", 16), ("pool_b", 4), ("pool_scale", 4), ("hy_w", 54),
    ("hy_b", 18), ("hy_skip", 6), ("norm_ffn_2", 16), ("fc_w", 264), ("fc_b", 88),
    ("norm_final_2", 16), ("dt_bias", 1), ("a_log", 1), ("f_b1", 1), ("f_fr1", 1), ("f_b2", 1),
    ("f_fr2", 1), ("rcnt", 64),
]
POFF = {}
_o = 0
for _n, _c in PARAMS:
    POFF[_n] = _o
    _o += _c
NPAR = _o

MAP = {}
_o = 0
for _n, _c in [("hT", 4096), ("X1", 8192), ("XG", 8192), ("raw", NRAW * UN), ("wh", NW * UN), ("wl", NW * UN),
               ("par", NPAR), ("ident", 128), ("ones", 128), ("T", NT * 256), ("R", NR * 264), ("RS", 512), ("A", NA)]:
    MAP[_n] = _o
    _o += (_c + 7) // 8 * 8
NWORDS = _o

A_ATT = dict(kT=0, v=1024)
A_MIX = dict(XS=2048, ZS=4096, BT=6144, CT=7168, cbm=8192, mask=9728, dtb=10112, dcol=12160, D=(10112, 12288), M=(10880, 13056),
             xdt=(11648, 6144), U=12288, C=12800, V=13312, sq=2048, n0=2560, n1=3072, n2=3584)
A_MEM = 2048
A_XA = dict(qT=2048, P=3072, PT=5120, st=7168)
A_FIL = dict(K=0, F=3840, G=4864, dec=5888, w3=7424, hf=8960, feat=12032, w1=12288, w2=12352, s=12416)
A_B2 = dict(K=0, F=3840, IF=4864, z=5888, x0=7424, vg=8960, ws=10496, bs=11264, wp=12032, rc=12544)
G_B2 = dict(zt=2048, zf=5120, vt=6656, gain=0, t=3584)


class Queue:

    def __init__(self, name, sem):
        self.name, self.sem, self.n, self.items = name, sem, 0, []

    def add(self, fn, waits, inc):
        tok = None
        if inc:
            self.n += 1
            tok = (self.sem, self.n)
        self.items.append((flat(waits), fn, inc))
        return tok

    def play(self, eng):
        seen = {}
        for waits, fn, inc in self.items:
            for sem, val in waits:
                if seen.get(id(sem), 0) < val:
                    eng.wait_ge(sem, val)
                    seen[id(sem)] = val
            ins = fn(eng)
            if inc:
                ins.then_inc(self.sem, 1)


def flat(x):
    if x is None:
        return []
    if isinstance(x, tuple) and len(x) == 2 and isinstance(x[1], int):
        return [x]
    out = []
    for y in x:
        out += flat(y)
    return out


class Slot:
    def __init__(self, ap):
        self.ap, self.free = ap, []


class Ring:

    def __init__(self, aps):
        self.slots = deque(Slot(a) for a in aps)

    def take(self):
        assert self.slots, "no buffer left"
        return self.slots.popleft()

    def give(self, slot, *toks):
        slot.free = flat(toks)
        self.slots.append(slot)


def program(nc, T_):
    sems = []

    def sem(name):
        g = nc.semaphore(name)
        s = g.__enter__()
        sems.append(g)
        return s

    def at(name, words, dt=F32, base=None, off=0):
        b = MAP[base or name] + off
        return nc.alloc_sbuf_tensor_at(name, [128, words], dt, offset=4 * b + BASE)

    BASE = (nc.sbuf_base + 31) // 32 * 32
    slab = nc.sbuf_tensor("slab", [128, NWORDS + 8], F32)
    slab.__enter__()
    hT = at("hT", 4096)
    X1 = at("X1", 8192, F32R)
    XG = at("XG", 8192, F32R)
    Gf = at("Gf", 8192, F32, base="XG")
    raw = at("raw", NRAW * UN)
    wh = at("wh", NW * UN, F32R)
    wl = at("wl", NW * UN, F32R)
    par = at("par", NPAR)
    ident = at("ident", 128)
    ones = at("ones", 128)
    Tt = at("T", NT * 256)
    Rt = at("R", NR * 264)
    RS = at("RS", 512)
    A = at("A", NA)

    pguards = [nc.psum_tensor(f"ps{i}", [128, 512], F32) for i in range(8)]
    banks = [g.__enter__() for g in pguards]

    q = {n: Queue(n, sem("s_" + n)) for n in ("pe", "act", "dve", "pool", "sp")}

    def pe(fn, *w, inc=True):
        return q["pe"].add(fn, w, inc)

    def act(fn, *w):
        return q["act"].add(fn, w, True)

    def dve(fn, *w):
        return q["dve"].add(fn, w, True)

    def pool(fn, *w):
        return q["pool"].add(fn, w, True)

    dcount = {}

    def dma(queue, s, out, in_, *w):
        dcount[id(s)] = dcount.get(id(s), 0) + 16

        def fn(e):
            return e.dma_start(out, in_).then_inc(s, 16)
        q[queue].add(fn, w, False)
        return (s, dcount[id(s)])

    def done():
        return [(x.sem, x.n) for x in q.values() if x.n and x.name != "sp"]

    def P(name, i=0, n=1, p=128):
        return par[0:p, POFF[name] + i:POFF[name] + i + n]

    def a_(off, n, p=128):
        return A[0:p, off:off + n]

    TR = Ring([Tt[:, i * 256:(i + 1) * 256] for i in range(NT)])
    RR = Ring([Rt[:, i * 264:(i + 1) * 264] for i in range(NR)])
    AUX = Ring([banks[i][:, :] for i in range(4, 8)])

    s_par = sem("d_par")
    s_x, s_mem = ([sem(f"d_{n}{i}") for i in range(4)] for n in ("x", "m"))
    memT = A[:, A_MEM:A_MEM + 4096]
    dma("sp", s_par, par[:, :], T_["par"])
    t_par = dma("sp", s_par, ident[:, :], T_["ident"])
    t_mem, t_x = [], []
    for i in range(4):
        t = dma("sp", s_mem[i], memT[:, i * 1024:(i + 1) * 1024], T_["memT"][:, i * 1024:(i + 1) * 1024])
        t_mem.extend([t] * 4)
    t_ones = pool(lambda e: e.memset(ones[:, :], 1.0))
    t_pad = pool(lambda e: e.memset(Rt[:, :], 0.0))
    for s in RR.slots:
        s.free = [t_pad]

    def load_x():
        for i in range(4):
            t = dma("sp", s_x[i], hT[:, i * 1024:(i + 1) * 1024], T_["xT"][:, i * 1024:(i + 1) * 1024])
            t_x.extend([t] * 4)

    h = [[None] for _ in range(KT)]

    def hk(k):
        return hT[:, k * 256:(k + 1) * 256]

    def rsqrt(v, y, u, t, vfree=None):
        t1 = act(lambda e: e.activation(u, v, ACT.Ln), t, vfree)
        t2 = act(lambda e: e.activation(y, u, ACT.Exp, scale=-0.5), t1)
        yield
        t3 = dve(lambda e: e.tensor_tensor(u, y, y, ALU.mult), t2)
        t4 = dve(lambda e: e.scalar_tensor_tensor(u, u, -0.5, v, ALU.mult, ALU.mult), t3)
        return dve(lambda e: e.scalar_tensor_tensor(y, u, 1.5, y, ALU.add, ALU.mult), t4)

    def split(items):
        out = []
        for X, k, src, tok, free in items:
            hi = X[:, k * 512:k * 512 + 256]
            out.append([act(lambda e, hi=hi, src=src: e.activation(hi, src, ACT.Copy), tok, free)])
        yield
        for n, (X, k, src, tok, free) in enumerate(items):
            hi, lo = X[:, k * 512:k * 512 + 256], X[:, k * 512 + 256:k * 512 + 512]
            out[n].append(dve(lambda e, hi=hi, lo=lo, src=src: e.tensor_tensor(lo, src, hi.bitcast(F32), ALU.subtract),
                              out[n][0], free))
        return out

    class Norm:

        def __init__(self, n):
            self.n, self.i, self.bank, self.rs = n, 0, AUX.take(), None

        def pair(self, srcs, scales=(1.0, 1.0)):
            ss = []
            for (src, tok), sc in zip(srcs, scales):
                s = TR.take()
                ss.append((s, act(lambda e, s=s, src=src, sc=sc: e.activation(s.ap, src, ACT.Square, scale=sc), tok, s.free)))
            yield
            (s0, t0), (s1, t1) = ss
            t = dve(lambda e: e.tensor_tensor(s0.ap, s0.ap, s1.ap, ALU.add), t0, t1)
            TR.give(s1, t)
            yield
            i = self.i
            self.i += 1
            ps = self.bank.ap[:, 0:256]
            self.tok = pe(lambda e: e.matmul(ps, ones[:, :], s0.ap, start=(i == 0), stop=(i == self.n - 1)),
                          t, t_ones, self.bank.free if i == 0 else None)
            TR.give(s0, self.tok)

        def finish(self, n, eps, keep, kfree=None):
            assert self.i == self.n
            v, u = TR.take(), TR.take()
            ps = self.bank.ap[:, 0:256]
            t = dve(lambda e: e.tensor_scalar(v.ap, ps, 1.0 / n, eps, ALU.mult, ALU.add), self.tok, v.free)
            AUX.give(self.bank, t)
            t = yield from rsqrt(v.ap, keep, u.ap, t, [u.free, kfree])
            TR.give(v, t)
            TR.give(u, t)
            return t

    rs_now = {}

    def evac(pairs, tok, frees, scaled=True):
        ts = []
        for (bank, out, ofree), fr in zip(pairs, frees):
            tmp = TR.take()
            ts.append((tmp, act(lambda e, tmp=tmp, bank=bank: e.activation(tmp.ap, bank[:, 256:512], ACT.Copy), tok, tmp.free)))
        res = []
        for (bank, out, ofree), fr, (tmp, t) in zip(pairs, frees, ts):
            t = dve(lambda e, tmp=tmp, bank=bank, out=out: e.tensor_tensor(out, bank[:, 0:256], tmp.ap, ALU.add), t, ofree)
            TR.give(tmp, t)
            fr.append(t)
            res.append(t)
        if scaled:
            rs, rt, ri = scale()
            for n, (bank, out, ofree) in enumerate(pairs):
                res[n] = dve(lambda e, out=out: e.tensor_tensor(out, out, rs, ALU.mult), res[n], rt)
            scale_last[ri] = res
        return res

    units = []

    def proj(W, col, groups, X, post, w=256, kn=UK, mode="A", pre=None):
        n = len(groups)
        for i, g in enumerate(groups):
            units.append(dict(src=W[col, g], g=g, kn=kn, w=w, X=X, post=post if i == n - 1 else None,
                              start=i == 0, stop=i == n - 1, mode=mode, col=col, pre=pre if i == 0 else None))

    s_raw = [sem(f"d_raw{i}") for i in range(NRAW)]
    raw_free = [[] for _ in range(NRAW)]
    w_free = [[] for _ in range(NW)]
    bank_free = [[[], []], [[], []]]
    raw_tok, split_tok = {}, {}

    def load_unit(i):
        s = i % NRAW
        raw_tok[i] = dma("sp", s_raw[s], raw[:, s * UN:(s + 1) * UN], units[i]["src"], raw_free[s])

    def split_unit(i):
        s, r = i % NW, i % NRAW
        src, hi, lo = raw[:, r * UN:(r + 1) * UN], wh[:, s * UN:(s + 1) * UN], wl[:, s * UN:(s + 1) * UN]
        t1 = act(lambda e: e.activation(hi, src, ACT.Copy), raw_tok[i], w_free[s])
        t2 = dve(lambda e: e.tensor_tensor(lo, src, hi.bitcast(F32), ALU.subtract), t1, w_free[s])
        raw_free[r] = [t1, t2]
        split_tok[i] = [t1, t2]

    tasks = deque()
    chains = []

    def step():
        for c in list(tasks)[:2]:
            if c is not tasks[0] and tasks[0][2] < LANE:
                break
            c[2] += 1
            try:
                next(c[1])
            except StopIteration:
                tasks.remove(c)
                if not tasks:
                    break

    def advance():
        for c in list(chains):
            if c[2]:
                continue
            c[2] = True
            try:
                next(c[1])
                c[2] = False
            except StopIteration:
                chains.remove(c)

    def finish_chains(name=None):
        while any(name is None or c[0] == name for c in chains):
            for c in list(chains):
                if name is None or c[0] == name:
                    try:
                        next(c[1])
                    except StopIteration:
                        chains.remove(c)

    def chain(name, gen):
        c = [name, gen, True]
        chains.append(c)
        try:
            next(gen)
            c[2] = False
        except StopIteration:
            chains.remove(c)

    def drain(name=None):
        while any(name is None or c[0] == name for c in tasks):
            step()

    def drain_all():
        finish_chains()
        drain()
        finish_chains()

    def run():
        pair = [0]
        for j in range(min(NRAW, len(units))):
            load_unit(j)
        for j in range(SPLIT_AHEAD):
            split_unit(j)
            if j + NRAW < len(units):
                load_unit(j + NRAW)
        for i, u in enumerate(units):
            if i + SPLIT_AHEAD < len(units):
                split_unit(i + SPLIT_AHEAD)
                if i + SPLIT_AHEAD + NRAW < len(units):
                    load_unit(i + SPLIT_AHEAD + NRAW)
            if u["pre"]:
                u["pre"]()
            s, w, kn = i % NW, u["w"], u["kn"]
            p = pair[0] % 2
            nb = 2 if w == 256 else 1
            for kk in range(kn):
                k = u["g"] * kn + kk
                x, xt = u["X"](k)
                for c in range(nb):
                    bank = banks[2 * p + c]
                    st, sp = u["start"] and kk == 0, u["stop"] and kk == kn - 1
                    last = c == nb - 1 and kk == kn - 1
                    wt = [split_tok[i] if kk == 0 and c == 0 else None, xt, bank_free[p][c] if st else None]
                    b0 = s * UN + kk * w
                    if u["mode"] == "A":
                        W1, W2 = wh[:, b0 + 128 * c:b0 + 128 * c + 128], wl[:, b0 + 128 * c:b0 + 128 * c + 128]
                        pe(lambda e, bank=bank, W1=W1, x=x, st=st: e.matmul(bank[:, :], W1, x, start=st, stop=False),
                           *wt, inc=False)
                        t = pe(lambda e, bank=bank, W2=W2, x=x, sp=sp: e.matmul(bank[:, 0:256], W2, x[:, 0:256],
                                                                               start=False, stop=sp), inc=last)
                    else:
                        W1, W2 = wh[:, b0:b0 + 256], wl[:, b0:b0 + 256]
                        xh, xl = x[:, c * 128:c * 128 + 128], x[:, 256 + c * 128:384 + c * 128]
                        for m, (l, r) in enumerate([(xh, W1), (xh, W2), (xl, W1)]):
                            t = pe(lambda e, bank=bank, l=l, r=r, st=st, sp=sp, m=m: e.matmul(
                                bank[:, 0:256], l, r, start=st and m == 0, stop=sp and m == 2),
                                *wt, inc=last and m == 2)
            w_free[s] = [t]
            if u["post"]:
                fr = [[] for _ in range(nb)]
                chain(u["post"].__name__, u["post"]([u["col"] * nb + c for c in range(nb)],
                                                    [banks[2 * p + c] for c in range(nb)], t, fr))
                assert all(fr)
                for c in range(nb):
                    bank_free[p][c] = fr[c]
                pair[0] += 1
            advance()
            step()

    def X1k(k):
        while x1tok[k] is None:
            advance()
        return X1[:, k * 512:(k + 1) * 512], x1tok[k]

    def XGk(k):
        while xgtok[k % 16] is None:
            advance()
            step()
        return XG[:, (k % 16) * 512:(k % 16 + 1) * 512], xgtok[k % 16]

    x1tok, xgtok = [None] * 16, [None] * 16

    x1free = [[]]

    kT = lambda i: a_(A_ATT["kT"] + 256 * i, 256)
    vv = lambda mt: a_(A_ATT["v"] + 512 * mt, 512)
    kT_tok, v_tok = [None] * 4, []
    scale_buf = [RS[:, 0:256], RS[:, 256:512]]
    scale_n = [0]

    def new_scale():
        scale_n[0] += 1
        i = scale_n[0] % 2
        return scale_buf[i], i, scale_last[i]

    scale_last = [[], []]

    def scale():
        while rs_now["key"] not in res:
            advance()
        return res[rs_now["key"]]

    def gained(k, src, tok, gain, X, toks, free, src2=None):
        ss = [TR.take(), TR.take()]
        ts = []
        for i in range(2):
            g = [P(n, k + i) for n in gain]
            if len(g) == 1:
                ts.append(dve(lambda e, i=i, g=g: e.tensor_scalar(ss[i].ap, src[i], g[0], None, ALU.mult), tok[i], ss[i].free, t_par))
            else:
                ts.append(dve(lambda e, i=i, g=g: e.tensor_scalar(ss[i].ap, src[i], g[0], g[1], ALU.mult, ALU.mult),
                              tok[i], ss[i].free, t_par))
        yield
        out = yield from split([(X, k + i, ss[i].ap, ts[i], free) for i in range(2)])
        for i in range(2):
            toks[k + i] = out[i]
            TR.give(ss[i], out[i])

    def input_norm(src, tok, gain, X, toks, key):
        n = Norm(8)
        for k in range(0, 16, 2):
            s, t = [src(k), src(k + 1)], tok[k:k + 2]
            yield from gained(k, s, t, gain, X, toks, None)
            yield from n.pair(list(zip(s, t)))
        ap, i, fr = new_scale()
        t = yield from n.finish(D, 1e-5, ap, fr)
        res[key] = (ap, t, i)

    res = {}

    def use_scale(key):
        rs_now["key"] = key

    memc = a_(A_MEM + 4096, 2)

    def fast(gen, n):
        i = 0
        for _ in gen:
            i += 1
            if i % n == 0:
                yield

    def mem_task():
        yield from input_norm(lambda k: memT[:, k * 256:(k + 1) * 256], t_mem, ["mem_norm"], XG, xgtok, "mem")
        ap, tok, i = res["mem"]
        yield
        bk = AUX.take()
        for st in range(2):
            t = pe(lambda e, st=st: e.transpose(bk.ap[:, 128 * st:128 * st + 128], ap[:, 128 * st:128 * st + 128], ident[:, :]),
                   tok, bk.free, t_par)
        yield
        t = act(lambda e: e.activation(memc, bk.ap[:, 0:256:128], ACT.Copy), t)
        AUX.give(bk, t)
        tm["memc"] = t
        scale_last[i] = scale_last[i] + [t]

    def start():
        use_scale("mem")
        chain("mem", fast(mem_task(), 3))
        chain("n1", fast(input_norm(hk, t_x, ["norm_mix"], X1, x1tok, "x"), 3))

    def post_k(cts, bks, tok, frs):
        r = evac([(b, kT(ct), None) for ct, b in zip(cts, bks)], tok, frs)
        for ct, t in zip(cts, r):
            kT_tok[ct] = t
        yield

    def post_v(cts, bks, tok, frs):
        col = cts[0] // 2
        while "memc" not in tm:
            advance()
        for mt in range(2):
            t = act(lambda e, mt=mt: e.activation(vv(mt)[:, col * 256:(col + 1) * 256], bks[mt][:, 0:256], ACT.Copy,
                                                  scale=memc[:, mt:mt + 1]), tok, tm["memc"])
            v_tok.append(t)
            frs[mt].append(t)
        yield

    tm = {}
    for c in range(2):
        proj(T_["w_k"], c, range(4), XGk, post_k)
    for c in range(2):
        proj(T_["w_v"], c, range(4), XGk, post_v, mode="B")

    def begin_mix():
        for k in range(16):
            h[k] = t_x[k]
        use_scale("x")

    def conv(items, ntap, off, wname, nch, bname=None):
        ts = []
        for src, out, wi, stok, ofree in items:
            b = P(bname, wi) if bname else 0.0
            ts.append(act(lambda e, src=src, out=out, wi=wi, b=b: e.activation(
                out, src[:, off:off + 256], ACT.Identity, scale=P(wname, wi), bias=b), stok, ofree, t_par))
        yield
        for k in range(1, ntap):
            for n, (src, out, wi, stok, ofree) in enumerate(items):
                ts[n] = dve(lambda e, k=k, src=src, out=out, wi=wi: e.scalar_tensor_tensor(
                    out, src[:, off + k:off + k + 256], P(wname, k * nch + wi), out, ALU.mult, ALU.add), ts[n], stok)
        return ts

    am = A_MIX
    Uo, Co, Vo = ([a_(am[n] + 256 * i, 256) for i in range(2)] for n in "UCV")
    cfree, vfree, ufree = [None], [None], [None]
    u_tok, c_tok = [None, None], [None, None]

    def post_u(cts, bks, tok, frs):
        u_tok[:] = evac([(b, Uo[i], ufree[0]) for i, b in enumerate(bks)], tok, frs)
        yield

    def post_c(cts, bks, tok, frs):
        ss, rr = [TR.take() for _ in "ab"], [RR.take() for _ in "ab"]
        ts = evac([(b, s.ap, s.free) for b, s in zip(bks, ss)], tok, frs)
        yield
        for i in range(2):
            ts[i] = pool(lambda e, i=i: e.tensor_tensor(rr[i].ap[:, 3:259], ss[i].ap, Uo[i], ALU.mult),
                         ts[i], u_tok[i], rr[i].free)
            TR.give(ss[i], ts[i])
        ufree[0] = list(ts)
        yield
        j = cts[0] - 32
        ts = yield from conv([(rr[i].ap, Co[i], j + i, ts[i], cfree[0]) for i in range(2)], 3, 1, "sc_w", 16)
        c_tok[:] = ts
        for r, t in zip(rr, ts):
            RR.give(r, t)

    def post_b(cts, bks, tok, frs):
        j = cts[0] - 16
        finish_chains("post_c")
        ss = [TR.take() for _ in "ab"]
        ts = evac([(b, s.ap, s.free) for b, s in zip(bks, ss)], tok, frs)
        yield
        for i in range(2):
            ts[i] = pool(lambda e, i=i: e.tensor_tensor(Vo[i], ss[i].ap, Co[i], ALU.mult), ts[i], c_tok[i], vfree[0])
            TR.give(ss[i], ts[i])
        cfree[0] = list(ts)
        yield
        V, sq, v, u, y = (a_(am[n], 512) for n in ("V", "sq", "n0", "n1", "n2"))
        t = act(lambda e: e.activation(sq, V, ACT.Square), ts, scfree[0])
        yield
        bk = AUX.take()
        t = pe(lambda e: e.matmul(bk.ap[:, :], ones[:, :], sq, start=True, stop=True), t, bk.free)
        yield
        t = dve(lambda e: e.tensor_scalar(v, bk.ap[:, :], 1.0 / 128, 1e-5, ALU.mult, ALU.add), t, scfree[0])
        AUX.give(bk, t)
        t = yield from rsqrt(v, y, u, t, scfree[0])
        yield
        tt = [dve(lambda e, i=i: e.scalar_tensor_tensor(Vo[i], Vo[i], P("sc_norm", j + i), y[:, 256 * i:256 * i + 256],
                                                        ALU.mult, ALU.mult), t) for i in range(2)]
        scfree[0] = tt
        out = yield from split([(XG, j + i, Vo[i], tt[i], xgfree[0]) for i in range(2)])
        vfree[0] = out
        for i in range(2):
            xgtok[j + i] = out[i]

    scfree = [None]
    xgfree = [[]]

    def begin_sc():
        begin_mix()
        xgfree[0] = done()
        scfree[0] = xgfree[0]
        ufree[0] = xgfree[0]
        xgtok[:] = [None] * 16

    for j in range(8):
        proj(T_["w_sc"], j, range(4), X1k, post_u, pre=begin_sc if j == 0 else None)
        proj(T_["w_sc"], 16 + j, range(4), X1k, post_c)
        proj(T_["w_sc"], 8 + j, range(4), X1k, post_b)

    mask = a_(am["mask"], 384)
    s_mask = sem("d_mask")
    dtb = [a_(am["dtb"] + 256 * i, 256, 32) for i in range(8)]
    dcol = a_(am["dcol"], 128)
    acs = dtb[7]

    def post_dt(cts, bks, tok, frs):
        bank, fr = bks[0], frs[0]
        ps = [bank[0:32, 0:256], bank[0:32, 256:512]]
        x, b1, b2, b3, b4, al, b6 = dtb[:7]
        t1 = act(lambda e: e.activation(b1, ps[1], ACT.Copy), tok)
        t2 = dve(lambda e: e.tensor_tensor(x, ps[0], b1, ALU.add), t1)
        fr.append(t2)
        rs, rt, _ = scale()
        t2 = dve(lambda e: e.tensor_tensor(x, x, rs[0:32, :], ALU.mult), t2, rt)
        t3 = dve(lambda e: e.tensor_scalar(x, x, P("dt_bias", p=32), None, ALU.add), t2, t_par)
        yield
        t4 = act(lambda e: e.activation(b1, x, ACT.Abs), t3)
        t5 = act(lambda e: e.activation(b1, b1, ACT.Exp, scale=-1.0), t4)
        t6 = dve(lambda e: e.tensor_scalar(b2, b1, 1.0, None, ALU.add), t5)
        t7 = act(lambda e: e.activation(b3, b2, ACT.Ln), t6)
        t8 = dve(lambda e: e.tensor_scalar(b4, b2, -1.0, None, ALU.add), t6)
        t9 = dve(lambda e: e.tensor_tensor(b4, b1, b4, ALU.subtract), t8)
        t10 = dve(lambda e: e.reciprocal(b6, b2), t6)
        t11 = dve(lambda e: e.tensor_tensor(b4, b4, b6, ALU.mult), t9, t10)
        t12 = dve(lambda e: e.tensor_tensor(b4, b4, b3, ALU.add), t11, t7)
        t13 = dve(lambda e: e.scalar_tensor_tensor(b4, x, 0.0, b4, ALU.max, ALU.add), t12)
        t14 = act(lambda e: e.activation(al[:, 0:1], P("a_log", p=32), ACT.Exp), t_par)
        t15 = dve(lambda e: e.tensor_scalar(b2, b4, al[:, 0:1], -1.0, ALU.mult, ALU.mult), t13, t14, t7)
        t16 = dve(lambda e: e.memset(b3, 1.0), t12)
        t17 = dve(lambda e: e.tensor_tensor_scan(acs, b3, b2, 0.0, ALU.mult, ALU.add), t15, t16)
        yield
        bk = AUX.take()
        for n, (src, tk) in enumerate([(acs, t17), (b4, t13)]):
            for st in range(2):
                o = 64 * n + 32 * st
                t = pe(lambda e, src=src, st=st, o=o: e.transpose(bk.ap[:, o:o + 32], src[:, 128 * st:128 * st + 128],
                                                                  ident[0:32, 0:32]), tk, bk.free, t_par)
        yield
        t = act(lambda e: e.activation(dcol, bk.ap[:, 0:128], ACT.Copy), t)
        AUX.give(bk, t)
        tm["dt"] = t
        tm["acs"] = t17

    def post_xbc(dstf):
        def post(cts, bks, tok, frs):
            i0 = cts[0] - 16
            rr = [RR.take() for _ in "ab"]
            ts = evac([(b, r.ap[:, 3:259], r.free) for b, r in zip(bks, rr)], tok, frs)
            yield
            ss = [TR.take() for _ in "ab"]
            ts = yield from conv([(rr[i].ap, ss[i].ap, i0 + i, ts[i], ss[i].free) for i in range(2)], 4, 0, "conv_w", 24, "conv_b")
            yield
            for i in range(2):
                RR.give(rr[i], ts[i])
                out, ofree = dstf(i0 + i)
                t2 = act(lambda e, i=i, out=out: e.activation(out, ss[i].ap, ACT.Silu), ts[i], ofree)
                TR.give(ss[i], t2)
                tm[("xbc", i0 + i)] = t2
                if i0 + i >= 20:
                    tasks.append(["cb", cb_task(i0 + i - 20), 0])
        return post

    def bc_dst(i):
        o = am["BT"] + 256 * (i - 16)
        return a_(o, 256), None

    def cb_task(g):
        yield
        bk = AUX.take()
        B, C = a_(am["BT"] + 256 * g, 256), a_(am["CT"] + 256 * g, 256)
        w = [tm[("xbc", 16 + g)], tm[("xbc", 20 + g)], bk.free]
        pe(lambda e: e.matmul(bk.ap[:, 0:256], B[:, 0:128], C[:, 0:256], start=True, stop=True), *w)
        t = pe(lambda e: e.matmul(bk.ap[:, 256:384], B[:, 128:256], C[:, 128:256], start=True, stop=True))
        yield
        t = dve(lambda e: e.tensor_tensor(a_(am["cbm"] + 384 * g, 384), bk.ap[:, 0:384], mask, ALU.mult), t, tm["mask"])
        AUX.give(bk, t)
        tm[("cb", g)] = t

    xsfree, zsfree = [[] for _ in range(8)], [[] for _ in range(8)]

    def XS(j):
        return a_(am["XS"] + 256 * (j % 8), 256)

    def ZS(j):
        return a_(am["ZS"] + 256 * (j % 8), 256)

    def post_z(cts, bks, tok, frs):
        drain(f"ssd{cts[0] // 4 - 2}")
        r = evac([(b, ZS(j), zsfree[j % 8]) for j, b in zip(cts, bks)], tok, frs)
        yield
        for j, t in zip(cts, r):
            tm[("z", j)] = act(lambda e, j=j: e.activation(ZS(j), ZS(j), ACT.Silu), t)
            tasks.append([f"ssd{j // 4}", ssd_task(j), 0])

    dfree, mfree, xfree = [None, None], [None, None], [None, None]
    gacc = {}

    def ssd_task(j):
        g, q_ = j // 4, j % 2
        xs, xt = XS(j), tm[("xbc", j)]
        tb, bb = AUX.take(), AUX.take()
        for st in range(2):
            t1 = pe(lambda e, st=st: e.transpose(tb.ap[:, 128 * st:128 * st + 128], xs[:, 128 * st:128 * st + 128], ident[:, :]),
                    xt, tb.free, t_par)
        for hh in range(2):
            t2 = pe(lambda e, hh=hh: e.matmul(bb.ap[:, 256 * hh:256 * hh + 256],
                                              ident[0:32, 2 * j + hh:2 * j + hh + 1].to_broadcast([32, 128]), acs,
                                              start=True, stop=True), tm["acs"], bb.free)
        yield
        xdt = a_(am["xdt"][q_], 256)
        for st in range(2):
            o = xdt[:, 128 * st:128 * st + 128].rearrange("p (a b) -> p a b", a=2)
            i0 = tb.ap[:, 128 * st:128 * st + 128].rearrange("p (a b) -> p a b", a=2)
            c = 64 + 32 * st + 2 * j
            i1 = dcol[:, c:c + 2].unsqueeze(2).to_broadcast([128, 2, 64])
            t3 = dve(lambda e, o=o, i0=i0, i1=i1: e.tensor_tensor(o, i0, i1, ALU.mult), t1, tm["dt"], xfree[q_])
        Dd, M = a_(am["D"][q_], 768), a_(am["M"][q_], 768)
        for hh in range(2):
            for st in range(2):
                o = Dd[:, 384 * hh + 256 * st:384 * hh + 256 + 128 * st]
                i0 = bb.ap[:, 256 * hh + 128 * st:256 * hh + 256]
                sc = dcol[:, 32 * st + 2 * j + hh:32 * st + 2 * j + hh + 1]
                t4 = dve(lambda e, o=o, i0=i0, sc=sc: e.tensor_scalar(o, i0, sc, 0.0, ALU.subtract, ALU.min),
                         t2, tm["dt"], dfree[q_])
        AUX.give(bb, t4)
        t5 = act(lambda e: e.activation(Dd, Dd, ACT.Exp), t4)
        yield
        cb = a_(am["cbm"] + 384 * g, 384)
        for hh in range(2):
            t6 = pool(lambda e, hh=hh: e.tensor_tensor(M[:, 384 * hh:384 * hh + 384], Dd[:, 384 * hh:384 * hh + 384], cb,
                                                       ALU.mult), t5, tm[("cb", g)], mfree[q_])
        dfree[q_] = [t6]
        yield
        yo = tb.ap[:, 256:512]
        for hh in range(2):
            o = yo[64 * hh:64 * hh + 64, 0:256]
            o2 = yo[64 * hh:64 * hh + 64, 128:256]
            pe(lambda e, o=o, hh=hh: e.matmul(o, xdt[:, 64 * hh:64 * hh + 64], M[:, 384 * hh:384 * hh + 256],
                                              start=True, stop=False), t6, t3, inc=False)
            t7 = pe(lambda e, o2=o2, hh=hh: e.matmul(o2, xdt[:, 128 + 64 * hh:192 + 64 * hh],
                                                     M[:, 384 * hh + 256:384 * hh + 384], start=False, stop=True))
        mfree[q_] = [t7]
        xfree[q_] = [t7]
        yield
        t8 = dve(lambda e: e.scalar_tensor_tensor(xs, xs, P("d_skip", j), yo, ALU.mult, ALU.add), t7, t1, t_par)
        AUX.give(tb, t8)
        t9 = pool(lambda e: e.tensor_tensor(xs, xs, ZS(j), ALU.mult), t8, tm[("z", j)])
        zsfree[j % 8] = [t9]
        tm[("y", j)] = t9
        yield
        s = TR.take()
        t = act(lambda e: e.activation(s.ap, xs, ACT.Square), t9, s.free)
        while j % 4 and gacc.get("n") != j:
            yield
        if j % 4 == 0:
            gacc["s"], gacc["t"] = s, t
        else:
            acc = gacc["s"]
            gacc["t"] = pool(lambda e: e.tensor_tensor(acc.ap, acc.ap, s.ap, ALU.add), t, gacc["t"])
            TR.give(s, gacc["t"])
        gacc["n"] = j + 1
        if j % 4 == 3:
            yield
            bk = AUX.take()
            acc = gacc["s"]
            t = pe(lambda e: e.matmul(bk.ap[:, 0:256], ones[:, :], acc.ap, start=True, stop=True), gacc["t"], bk.free)
            yield
            v, rs = TR.take(), TR.take()
            t = dve(lambda e: e.tensor_scalar(v.ap, bk.ap[:, 0:256], 1.0 / 512, 1e-5, ALU.mult, ALU.add), t, v.free)
            AUX.give(bk, t)
            rt = yield from rsqrt(v.ap, rs.ap, acc.ap, t, rs.free)
            TR.give(acc, rt)
            TR.give(v, rt)
            yield
            for n0 in (4 * g, 4 * g + 2):
                ts = [dve(lambda e, i=i: e.scalar_tensor_tensor(XS(i), XS(i), P("ssd_norm", i), rs.ap, ALU.mult, ALU.mult), rt)
                      for i in (n0, n0 + 1)]
                out = yield from split([(XG, n0 + i, XS(n0 + i), ts[i], xgfree[0]) for i in range(2)])
                for i in range(2):
                    xgtok[n0 + i] = out[i]
                    xsfree[(n0 + i) % 8] = out[i]
            TR.give(rs, ts)

    def xs_dst(i):
        drain(f"ssd{i // 4 - 2}")
        return XS(i), xsfree[i % 8]

    def residual(norm=None):
        def post(cts, bks, tok, frs):
            k = cts[0]
            for o in (0, 256):
                for i, b in enumerate(bks):
                    h[k + i] = dve(lambda e, i=i, b=b, o=o: e.tensor_tensor(hk(k + i), hk(k + i), b[:, o:o + 256], ALU.add),
                                   tok, h[k + i])
            for i in range(2):
                frs[i].append(h[k + i])
            yield
            if norm:
                gains, key, eps = norm
                if k == 0:
                    cur[0] = Norm(8)
                    x1free[0] = done()
                src, tk = [hk(k), hk(k + 1)], h[k:k + 2]
                if k == 0:
                    x1tok[:] = [None] * 16 if gains else x1tok
                    if key == "fin":
                        cur2[0] = Norm(8)
                if gains:
                    yield from gained(k, src, tk, gains, X1, x1tok, x1free[0])
                yield from cur[0].pair(list(zip(src, tk)))
                if key == "fin":
                    yield from cur2[0].pair(list(zip(src, tk)), [P(gains[0], k), P(gains[0], k + 1)])
                if k == 14:
                    while cur[0].i < 8 or (key == "fin" and cur2[0].i < 8):
                        yield
                    ap, si, fr = new_scale()
                    rt = yield from cur[0].finish(D, eps, ap, fr)
                    if key == "fin":
                        yield from second_norm(gains[0], ap, rt)
                    else:
                        res[key] = (ap, rt, si)
        return post

    def second_norm(gain, r1, rt):
        bank, n2 = cur2[0].bank, cur2[0]
        v, u, y = TR.take(), TR.take(), TR.take()
        t = dve(lambda e: e.scalar_tensor_tensor(v.ap, bank.ap[:, 0:256], 1.0 / D, r1, ALU.mult, ALU.mult), n2.tok, rt, v.free)
        AUX.give(bank, t)
        t = dve(lambda e: e.tensor_tensor(v.ap, v.ap, r1, ALU.mult), t)
        t = dve(lambda e: e.tensor_scalar(v.ap, v.ap, 1e-6, None, ALU.add), t)
        t = yield from rsqrt(v.ap, y.ap, u.ap, t, [u.free, y.free])
        ap, si, fr = new_scale()
        t = dve(lambda e: e.tensor_tensor(ap, r1, y.ap, ALU.mult), t, fr)
        for s in (v, u, y):
            TR.give(s, t)
        res["fin"] = (ap, t, si)
        for k in range(16):
            h[k] = dve(lambda e, k=k: e.scalar_tensor_tensor(hk(k), hk(k), P(gain, k), r1, ALU.mult, ALU.mult), rt, h[k], x1tok[k])
            if k % 4 == 3:
                yield
        scale_last[1 - si] = h[15]

    cur, cur2 = [None], [None]

    def begin(key):
        use_scale(key)

    def pre_bc():
        tm["mask"] = dma("sp", s_mask, mask, T_["mask"])

    proj(T_["w_dt"], 0, range(2), X1k, post_dt, w=128, kn=8, pre=pre_bc)
    for c in range(4):
        proj(T_["w_zx"], 16 + c, range(4), X1k, post_xbc(bc_dst))

    for c in range(8):
        proj(T_["w_osc"], c, range(4), XGk, residual())

    def pre_ssd():
        drain_all()
        xgfree[0] = done()
        dfree[:] = mfree[:] = xfree[:] = [xgfree[0]] * 2
        for i in range(8):
            xsfree[i] = zsfree[i] = xgfree[0]
        xgtok[:] = [None] * 16
    for g in range(4):
        for c in range(2):
            proj(T_["w_zx"], 8 + 2 * g + c, range(4), X1k, post_xbc(xs_dst), pre=pre_ssd if g == c == 0 else None)
        for c in range(2):
            proj(T_["w_zx"], 2 * g + c, range(4), X1k, post_z)
    for c in range(8):
        proj(T_["w_ossd"], c, range(3), XGk, residual())
    for c in range(8):
        proj(T_["w_ossd"], c, [3], XGk, residual((["norm_xa"], "xa", 1e-5)))

    ax = A_XA
    SC = 128.0 ** -0.5
    pfree = [[]]

    def post_q(cts, bks, tok, frs):
        r = evac([(b, a_(ax["qT"] + 256 * ct, 256), pfree[0]) for ct, b in zip(cts, bks)], tok, frs)
        yield
        for ct, t in zip(cts, r):
            chain("att", att_task(ct, t))

    def att_task(hd, t):
        qT = a_(ax["qT"] + 256 * hd, 256)
        sb = AUX.take()
        for st in range(2):
            t = pe(lambda e, st=st: e.matmul(sb.ap[:, 256 * st:256 * st + 256], qT[:, 128 * st:128 * st + 128], kT(hd),
                                             start=True, stop=True), t, kT_tok[hd], sb.free)
        yield
        Pp, PT = a_(ax["P"] + 512 * hd, 512), a_(ax["PT"] + 512 * hd, 512)
        st_ = a_(ax["st"] + 16 * hd, 16)
        tt = []
        for st in range(2):
            mx, nb, sm, ri = (st_[:, 8 * st + i:8 * st + i + 1] for i in range(4))
            src = sb.ap[:, 256 * st:256 * st + 256]
            o = Pp[:, 256 * st:256 * st + 256]
            ta = dve(lambda e, mx=mx, src=src: e.tensor_reduce(mx, src, AX.X, ALU.max), t, pfree[0])
            tb = dve(lambda e, nb=nb, mx=mx: e.tensor_scalar(nb, mx, -SC, None, ALU.mult), ta)
            tt.append((tb, nb, sm, ri, src, o))
        tq = []
        for tb, nb, sm, ri, src, o in tt:
            tc = act(lambda e, nb=nb, sm=sm, src=src, o=o: e.activation(o, src, ACT.Exp, bias=nb, scale=SC, accum_out=sm),
                     tb, ta)
            td = dve(lambda e, sm=sm, ri=ri: e.reciprocal(ri, sm), tc)
            tq.append(dve(lambda e, o=o, ri=ri: e.tensor_scalar(o, o, ri, None, ALU.mult), td))
        AUX.give(sb, tc)
        yield
        pb = AUX.take()
        for mt in range(2):
            for st in range(2):
                t = pe(lambda e, mt=mt, st=st: e.transpose(pb.ap[:, 256 * mt + 128 * st:256 * mt + 128 * st + 128],
                                                           Pp[:, 256 * st + 128 * mt:256 * st + 128 * mt + 128], ident[:, :]),
                       tq, pb.free)
        yield
        t = act(lambda e: e.activation(PT, pb.ap[:, :], ACT.Copy), t)
        AUX.give(pb, t)
        yield
        ob = AUX.take()
        for mt in range(2):
            t = pe(lambda e, mt=mt: e.matmul(ob.ap[:, 0:256], vv(mt)[:, 128 * hd:128 * hd + 128],
                                             PT[:, 256 * mt:256 * mt + 256], start=(mt == 0), stop=(mt == 1)),
                   t, v_tok, ob.free)
        s = TR.take()
        t = act(lambda e: e.activation(s.ap, ob.ap[:, 0:256], ACT.Copy), t, s.free)
        AUX.give(ob, t)
        [xgtok[hd]] = yield from split([(XG, hd, s.ap, t, xgfree[0])])
        TR.give(s, xgtok[hd])

    def pre_q():
        begin("xa")
        pfree[0] = done()
        xgfree[0] = pfree[0]
        xgtok[:] = [None] * 16
    for c in range(2):
        proj(T_["w_q"], c, range(4), X1k, post_q, pre=pre_q if c == 0 else None)
    for c in range(8):
        proj(T_["w_o"], c, [0], XGk, residual((["norm_ffn"], "ffn", 1e-5)))

    af = A_FIL
    s_fil, s_f1 = sem("d_fil"), sem("d_f1")

    def sine(z, k, t):
        MAGIC = 12582912.0
        C1, C2, C3 = 6.28125, 0.0019350051879882812, 3.0199159819e-07
        t = dve(lambda e: e.tensor_scalar(k, z, 0.15915494309189535, MAGIC, ALU.mult, ALU.add), t)
        t = dve(lambda e: e.tensor_scalar(k, k, -MAGIC, None, ALU.add), t)
        for c in (C1, C2, C3):
            t = dve(lambda e, c=c: e.scalar_tensor_tensor(z, k, -c, z, ALU.mult, ALU.add), t)
        t = dve(lambda e: e.tensor_scalar(z, z, 3.1415925, -3.1415925, ALU.min, ALU.max), t)
        return act(lambda e: e.activation(z, z, ACT.Sin), t)

    def filter_task(fr):
        F, G, dec, w3, hf = (a_(af[n], w) for n, w in (("F", 1024), ("G", 1024), ("dec", 1536), ("w3", 1536), ("hf", 3072)))
        feat, w1, w2 = a_(af["feat"], 256, 33), a_(af["w1"], 64, 33), a_(af["w2"], 64, 64)
        z, kk, z2 = (a_(af["s"] + 256 * i, 256, 64) for i in range(3))
        K = a_(af["K"], 3840).rearrange("p (m c) -> p m c", m=5)
        dma("sp", s_f1, feat, T_["feat"], fr)
        dma("sp", s_f1, w1, T_["f_w1"], fr)
        dma("sp", s_f1, w2, T_["f_w2"], fr)
        t_f1 = dma("sp", s_f1, w3[0:64, :], T_["f_w3"], fr)
        dma("sp", s_fil, F, T_["dftF"], fr)
        dma("sp", s_fil, G, T_["dftG"], fr)
        t_fil = dma("sp", s_fil, dec, T_["decay"], fr)
        for _ in range(8):
            yield
        bk = AUX.take()
        t = pe(lambda e: e.matmul(bk.ap[0:64, 0:256], w1, feat, start=True, stop=True), t_f1, bk.free)
        yield
        t = dve(lambda e: e.tensor_scalar(z, bk.ap[0:64, 0:256], P("f_b1", p=64), P("f_fr1", p=64), ALU.add, ALU.mult), t, t_par)
        t = sine(z, kk, t)
        yield
        yield
        t = pe(lambda e: e.matmul(bk.ap[0:64, 0:256], w2, z, start=True, stop=True), t)
        yield
        t = dve(lambda e: e.tensor_scalar(z2, bk.ap[0:64, 0:256], P("f_b2", p=64), P("f_fr2", p=64), ALU.add, ALU.mult), t)
        AUX.give(bk, t)
        tz = sine(z2, kk, t)
        yield
        yield
        thf = []
        for st in range(2):
            for c in range(4):
                bk = AUX.take()
                t = pe(lambda e, st=st, c=c, bk=bk: e.matmul(bk.ap[:, 0:384], z2[:, 128 * st:128 * st + 128],
                                                             w3[0:64, 384 * c:384 * c + 384], start=True, stop=True), tz, bk.free)
                yield
                o = 1536 * st + 384 * c
                d = 768 * st + 384 * (c % 2)
                t = dve(lambda e, o=o, d=d, bk=bk: e.tensor_tensor(hf[:, o:o + 384], bk.ap[:, 0:384], dec[:, d:d + 384], ALU.mult),
                        t, t_fil)
                AUX.give(bk, t)
                thf.append(t)
                yield
        tk = {}
        for m in range(4):
            for c in range(2):
                bk = AUX.take()
                n = 0
                for st in range(2):
                    for mat, base in ((F, 0), (G, 768)):
                        lhs = mat[:, 512 * st + 128 * m:512 * st + 128 * m + 128]
                        rhs = hf[:, 1536 * st + base + 384 * c:1536 * st + base + 384 * c + 384]
                        t = pe(lambda e, lhs=lhs, rhs=rhs, n=n, bk=bk: e.matmul(bk.ap[:, 0:384], lhs, rhs, start=(n == 0), stop=(n == 3)),
                               thf, t_fil, bk.free)
                        n += 1
                yield
                tk[m, c] = act(lambda e, m=m, c=c, bk=bk: e.activation(K[:, m, 384 * c:384 * c + 384], bk.ap[:, 0:384], ACT.Copy), t)
                AUX.give(bk, tk[m, c])
        t = dve(lambda e: e.tensor_copy(K[:, 4, :], K[:, 0, :]), tk[0, 0], tk[0, 1])
        t = dve(lambda e: e.tensor_copy(K[0:1, 4, :], K[0:1, 2, :]), t, tk[2, 0], tk[2, 1])
        t = dve(lambda e: e.memset(K[0:1, 2, :], 0.0), t)
        tm["K"] = [t] + list(tk.values())
        tm["F"] = t_fil

    g_tok = [None, None]
    sgfree = [None, None]
    ffn_free = [[]]
    slot_free = [[] for _ in range(16)]
    SG = [None, None]

    def pre_ffn():
        begin("ffn")
        fr = done()
        for i in range(16):
            slot_free[i] = fr
        tasks.append(["filter", filter_task(fr), 0])

    def post_gate(cts, bks, tok, frs):
        ss = [TR.take() for _ in "ab"]
        ts = evac([(b, s.ap, s.free) for b, s in zip(bks, ss)], tok, frs)
        yield
        for i in range(2):
            g_tok[i] = act(lambda e, i=i: e.activation(ss[i].ap, ss[i].ap, ACT.Silu), ts[i])
            SG[i] = ss[i]

    def product(cts, ss, ts, gate):
        gg = list(SG)
        for i in range(2):
            ts[i] = gate(lambda e, i=i: e.tensor_tensor(ss[i].ap, ss[i].ap, gg[i].ap, ALU.mult), ts[i], g_tok[i])
            TR.give(gg[i], ts[i])
        yield
        k = cts[0]
        out = yield from split([(XG, (k + i) % 16, ss[i].ap, ts[i], slot_free[(k + i) % 16]) for i in range(2)])
        for i in range(2):
            xgtok[(k + i) % 16] = out[i]
            made.add(k + i)
            TR.give(ss[i], out[i])

    def post_up(cts, bks, tok, frs):
        ss = [TR.take() for _ in "ab"]
        ts = evac([(b, s.ap, s.free) for b, s in zip(bks, ss)], tok, frs)
        yield
        yield from product(cts, ss, ts, dve)

    def after_down(kts, post):
        def p(cts, bks, tok, frs):
            if cts[1] == 15:
                for k in kts:
                    slot_free[k % 16] = [tok]
            yield from post(cts, bks, tok, frs)
        return p

    made = set()

    def ready(kts):
        def f():
            while not all(k in made for k in kts):
                advance()
        return f

    def ffn(Wg, Wu, Wd, pg, pu, pre, norm):
        chunks = [list(range(8 * c, min(8 * c + 8, FT))) for c in range(6)]
        nextc = 0
        for p in range(FT // 2):
            proj(Wg, p, range(4), X1k, pg, pre=pre if p == 0 else None)
            proj(Wu, p, range(4), X1k, pu)
            done_t = 2 * p
            while nextc < 5 and chunks[nextc][-1] < done_t:
                kts = chunks[nextc]
                for c in range(8):
                    proj(Wd, c, [k // 4 for k in kts[::4]], XGk, after_down(kts, residual()),
                         pre=ready(kts) if c == 0 else None)
                nextc += 1
        kts = chunks[5]
        for c in range(8):
            proj(Wd, c, [k // 4 for k in kts[::4]], XGk, after_down(kts, residual(norm)), pre=ready(kts) if c == 0 else None)

    ffn(T_["w_gate"], T_["w_up"], T_["w_down"], post_gate, post_up, pre_ffn,
        (["norm_final", "norm_mix_2"], "fin", 1e-5))

    ab, gb = A_B2, G_B2
    s_b2 = sem("d_b2")
    g_ = lambda off, n: Gf[:, off:off + n]

    def pre_b2():
        drain_tasks()
        begin("fin")
        fr = done()
        for dst, name in ((a_(ab["IF"], 1024), "dftI"), (a_(ab["ws"], 768), "gm_ws"), (a_(ab["bs"], 768), "gm_bs"),
                          (a_(ab["wp"], 512), "pool_w"), (g_(gb["gain"], 1536), "gm_gb")):
            tm["b2"] = dma("sp", s_b2, dst, T_[name], fr)
        tm["b2free"] = fr
        xgtok[:] = [None] * 16

    def drain_tasks():
        drain()

    def cconv(bks, tok, frs, outs, wis, wname, bname, nch):
        rr = [RR.take() for _ in "ab"]
        ts = evac([(b, r.ap[:, 3:259], r.free) for b, r in zip(bks, rr)], tok, frs)
        yield
        ts = yield from conv([(rr[i].ap, outs[i][0], wis[i], ts[i], outs[i][1]) for i in range(2)], 3, 2, wname, nch, bname)
        for r, t in zip(rr, ts):
            RR.give(r, t)
        return ts

    zT = lambda e: a_(ab["z"] + 256 * e, 256)
    ztoks = [None] * 6
    x0toks = [None] * 6

    def post_hv(cts, bks, tok, frs):
        e0 = cts[0] - 16
        ztoks[e0:e0 + 2] = yield from cconv(bks, tok, frs, [(zT(e0 + i), tm["b2free"]) for i in range(2)],
                                            [12 + e0, 13 + e0], "hy_w", "hy_b", 18)

    def post_hx1(cts, bks, tok, frs):
        e0 = cts[0] - 10
        ss = [TR.take() for _ in "ab"]
        ts = yield from cconv(bks, tok, frs, [(s.ap, s.free) for s in ss], [6 + e0, 7 + e0], "hy_w", "hy_b", 18)
        for i in range(2):
            ztoks[e0 + i] = dve(lambda e, i=i: e.tensor_tensor(zT(e0 + i), zT(e0 + i), ss[i].ap, ALU.mult), ts[i], ztoks[e0 + i])
            TR.give(ss[i], ztoks[e0 + i])
        if e0 == 4:
            tasks.append(["hyena", hyena_task(), 0])

    def post_hx0(cts, bks, tok, frs):
        e0 = cts[0] - 4
        x0toks[e0:e0 + 2] = yield from cconv(bks, tok, frs, [(a_(ab["x0"] + 256 * (e0 + i), 256), tm["b2free"]) for i in range(2)],
                                             [e0, e0 + 1], "hy_w", "hy_b", 18)

    def transposes(src, toks, dst, fr):
        out = []
        for st in range(2):
            for c in range(2):
                bk = AUX.take()
                for i in range(3):
                    e_ = 3 * c + i
                    t = pe(lambda e, st=st, i=i, e_=e_, bk=bk: e.transpose(bk.ap[:, 128 * i:128 * i + 128],
                                                                          src(e_)[:, 128 * st:128 * st + 128], ident[:, :]),
                           toks[e_], bk.free)
                yield
                o = dst[:, 768 * st + 384 * c:768 * st + 384 * c + 384]
                t = act(lambda e, o=o, bk=bk: e.activation(o, bk.ap[:, 0:384], ACT.Copy), t, fr)
                AUX.give(bk, t)
                out.append(t)
        tm["tr"] = out

    def hyena_task():
        K = a_(ab["K"], 3840).rearrange("p (m c) -> p m c", m=5)
        F, IF = a_(ab["F"], 1024), a_(ab["IF"], 1024)
        zt, zf = g_(gb["zt"], 1536), g_(gb["zf"], 1536).rearrange("p (m c) -> p m c", m=4)
        ta, tb, tc = (g_(gb["t"] + 384 * i, 384) for i in range(3))
        yield from transposes(zT, ztoks, zt, tm["b2free"])
        tr = tm["tr"]
        zfree = tm["b2free"]
        tfree = None
        for hf in range(2):
            sl = slice(384 * hf, 384 * hf + 384)
            tf = []
            for m in range(4):
                bk = AUX.take()
                for st in range(2):
                    lhs = F[:, 512 * st + 128 * m:512 * st + 128 * m + 128]
                    rhs = zt[:, 768 * st + 384 * hf:768 * st + 384 * hf + 384]
                    t = pe(lambda e, lhs=lhs, rhs=rhs, st=st, bk=bk: e.matmul(bk.ap[:, 0:384], lhs, rhs, start=(st == 0), stop=(st == 1)),
                           tr, tm["F"], bk.free)
                yield
                t = act(lambda e, m=m, bk=bk: e.activation(zf[:, m, :], bk.ap[:, 0:384], ACT.Copy), t, zfree)
                AUX.give(bk, t)
                tf.append(t)
            if hf == 1:
                tm["zt_done"] = t
            ty = []
            for m in range(2):
                zr, zi, kr, ki = zf[:, m, :], zf[:, 2 + m, :], K[:, m, sl], K[:, 2 + m, sl]
                k2 = K[:, 4, sl] if m == 0 else K[:, 1, sl]
                w = [tf[m], tf[2 + m], tm["K"], tfree]
                t1 = dve(lambda e, zr=zr, kr=kr: e.tensor_tensor(ta, zr, kr, ALU.mult), *w)
                t2 = pool(lambda e, zi=zi, ki=ki: e.tensor_tensor(tb, zi, ki, ALU.mult), *w)
                t3 = dve(lambda e, zr=zr, ki=ki: e.tensor_tensor(tc, zr, ki, ALU.mult), *w)
                t4 = pool(lambda e, zi=zi, k2=k2: e.tensor_tensor(zi, zi, k2, ALU.mult), t2, *w)
                t5 = dve(lambda e, zr=zr: e.tensor_tensor(zr, ta, tb, ALU.subtract), t1, t2, t3)
                t6 = dve(lambda e, zi=zi: e.tensor_tensor(zi, zi, tc, ALU.add), t4, t3)
                tfree = [t5, t6]
                ty += [t5, t6]
                yield
            zfree = []
            for i in range(3):
                e_ = 3 * hf + i
                bk = AUX.take()
                for m in range(4):
                    t = pe(lambda e, m=m, i=i, bk=bk: e.matmul(bk.ap[:, 0:256], zf[:, m, 128 * i:128 * i + 128],
                                                              IF[:, 256 * m:256 * m + 256], start=(m == 0), stop=(m == 3)),
                           ty, tm["b2"], bk.free)
                zfree.append(t)
                yield
                t = dve(lambda e, e_=e_, bk=bk: e.scalar_tensor_tensor(zT(e_), zT(e_), P("hy_skip", e_), bk.ap[:, 0:256],
                                                                      ALU.mult, ALU.add), t)
                AUX.give(bk, t)
                ztoks[e_] = t
        tm["zf_done"] = t

    def hyena_out():
        for e0 in (0, 2, 4):
            items = []
            for e_ in (e0, e0 + 1):
                x0 = a_(ab["x0"] + 256 * e_, 256)
                t = dve(lambda e, e_=e_, x0=x0: e.tensor_tensor(x0, x0, zT(e_), ALU.mult), ztoks[e_], x0toks[e_])
                items.append((XG, 4 + e_, x0, t, [tm["zt_done"], tm["zf_done"]]))
            out = yield from split(items)
            xgtok[4 + e0:6 + e0] = out
            yield

    vg = lambda e: a_(ab["vg"] + 256 * e, 256)
    vgtok = [None] * 6

    def post_gv(cts, bks, tok, frs):
        e0 = cts[0] - 28
        ss = [TR.take() for _ in "ab"]
        ts = evac([(b, s.ap, s.free) for b, s in zip(bks, ss)], tok, frs)
        yield
        for i in range(2):
            vgtok[e0 + i] = act(lambda e, i=i: e.activation(vg(e0 + i), ss[i].ap, ACT.Gelu_apprx_tanh), ts[i], tm["b2free"])
            TR.give(ss[i], vgtok[e0 + i])
        if e0 == 4:
            tasks.append(["gmlp", gmlp_task(), 0])

    def gmlp_task():
        vt = g_(gb["vt"], 1536)
        gain, bias = g_(gb["gain"], 768), g_(gb["gain"] + 768, 768)
        ws, bs = a_(ab["ws"], 768), a_(ab["bs"], 768)
        yield from transposes(vg, vgtok, vt, tm["b2free"])
        tr = tm["tr"]
        tv = []
        sm = TR.take()
        for st in range(2):
            v = vt[:, 768 * st:768 * st + 768]
            stt = sm.ap[:, 32 * st:32 * st + 12]
            mv = sm.ap[:, 32 * st + 12:32 * st + 14]
            rr, u, y = (sm.ap[:, 32 * st + 14 + i:32 * st + 15 + i] for i in range(3))
            for c in range(2):
                t = dve(lambda e, c=c, v=v, stt=stt: e.bn_stats(stt[:, 6 * c:6 * c + 6], v[:, 384 * c:384 * c + 384]), tr, sm.free)
            t = dve(lambda e, mv=mv, stt=stt: e.bn_aggr(mv, stt), t)
            t1 = dve(lambda e, mv=mv, rr=rr: e.tensor_scalar(rr, mv[:, 1:2], 1e-5, None, ALU.add), t)
            t2 = act(lambda e, u=u, rr=rr: e.activation(u, rr, ACT.Ln), t1)
            t2 = act(lambda e, u=u, y=y: e.activation(y, u, ACT.Exp, scale=-0.5), t2)
            t3 = dve(lambda e, u=u, y=y: e.tensor_tensor(u, y, y, ALU.mult), t2)
            t3 = dve(lambda e, u=u, rr=rr: e.scalar_tensor_tensor(u, u, -0.5, rr, ALU.mult, ALU.mult), t3)
            t3 = dve(lambda e, u=u, y=y: e.scalar_tensor_tensor(y, u, 1.5, y, ALU.add, ALU.mult), t3)
            yield
            t4 = dve(lambda e, v=v, mv=mv, y=y: e.tensor_scalar(v, v, mv[:, 0:1], y, ALU.subtract, ALU.mult), t3)
            t5 = pool(lambda e, v=v: e.tensor_tensor(v, v, gain, ALU.mult), t4, tm["b2"])
            t6 = pool(lambda e, v=v: e.tensor_tensor(v, v, bias, ALU.add), t5)
            tv.append(t6)
            yield
        TR.give(sm, tv)
        tm["gain_done"] = tv
        for e_ in range(6):
            bk = AUX.take()
            for st in range(2):
                t = pe(lambda e, st=st, e_=e_, bk=bk: e.matmul(bk.ap[:, 128 * st:128 * st + 128],
                                                              vt[:, 768 * st + 128 * e_:768 * st + 128 * e_ + 128],
                                                              ws[:, 128 * e_:128 * e_ + 128], start=True, stop=True),
                       tv, tm["b2"], bk.free)
            yield
            o = vg(e_).rearrange("p (s q) -> p s q", s=2)
            i0 = bk.ap[:, 0:256].rearrange("p (s q) -> p s q", s=2)
            i1 = bs[:, 128 * e_:128 * e_ + 128].unsqueeze(1).to_broadcast([128, 2, 128])
            vgtok[e_] = dve(lambda e, o=o, i0=i0, i1=i1: e.tensor_tensor(o, i0, i1, ALU.add), t, tr)
            AUX.give(bk, vgtok[e_])
        tm["vt_done"] = t

    def pool_task(g, s, t0, pfr):
        half = 2 ** g
        w = 2 * half
        ce = a_(ab["rc"], 280)
        t = dve(lambda e: e.memset(ce[:, 0:9], 0.0), pfr)
        ta = dve(lambda e: e.tensor_tensor_scan(ce[:, 9:265], cones[0], s.ap, 0.0, ALU.mult, ALU.add), t0, pfr, cones[1])
        tb = dve(lambda e: e.tensor_scalar(ce[:, 265:273], ce[:, 0:8], ce[:, 264:265], None, ALU.add), t, ta)
        d = TR.take()
        tc = dve(lambda e: e.tensor_tensor(d.ap, ce[:, 8 + half:264 + half], ce[:, 8 - half:264 - half], ALU.subtract), tb, d.free)
        t1 = dve(lambda e: e.tensor_tensor(d.ap[:, 0:8], d.ap[:, 0:8], P("rcnt", 16 * g, 8), ALU.mult), tc)
        t2 = dve(lambda e: e.tensor_tensor(d.ap[:, 248:256], d.ap[:, 248:256], P("rcnt", 16 * g + 8, 8), ALU.mult), tc)
        t3 = dve(lambda e: e.scalar_tensor_tensor(d.ap, d.ap, 1.0 / w, s.ap, ALU.mult, ALU.subtract), t1, t2)
        TR.give(s, t3)
        pf[0] = [t3]
        yield
        bk = AUX.take()
        t = pe(lambda e: e.matmul(bk.ap[:, 0:256], a_(ab["wp"] + 128 * g, 128), d.ap, start=True, stop=True), t3, tm["b2"], bk.free)
        yield
        t = dve(lambda e: e.tensor_scalar(d.ap, bk.ap[:, 0:256], P("pool_b", g), P("pool_scale", g), ALU.add, ALU.mult), t)
        AUX.give(bk, t)
        [xgtok[g]] = yield from split([(XG, g, d.ap, t, tm["gain_done"])])
        TR.give(d, xgtok[g])

    pf = [None]
    cones = [a_(ab["rc"] + 288, 256), None]

    def post_pool(cts, bks, tok, frs):
        ss = [TR.take() for _ in "ab"]
        ts = evac([(b, s.ap, s.free) for b, s in zip(bks, ss)], tok, frs)
        if cts[0] == 0:
            pf[0] = tm["b2free"]
            cones[1] = dve(lambda e: e.memset(cones[0], 1.0), pf[0])
            tasks.append(["hout", hyena_out(), 0])
        for ct, s, t in zip(cts, ss, ts):
            tasks.append(["pool", pool_task_late(ct, s, t), 0])
        yield

    def pool_task_late(ct, s, t):
        yield from pool_task(ct, s, t, pf[0])

    def post_gu(cts, bks, tok, frs):
        e0 = cts[0] - 22
        ss = [TR.take() for _ in "ab"]
        ts = evac([(b, s.ap, s.free) for b, s in zip(bks, ss)], tok, frs)
        yield
        ts = [act(lambda e, i=i: e.activation(ss[i].ap, ss[i].ap, ACT.Gelu_apprx_tanh), ts[i]) for i in range(2)]
        yield
        drain("gmlp")
        ts = [dve(lambda e, i=i: e.tensor_tensor(ss[i].ap, ss[i].ap, vg(e0 + i), ALU.mult), ts[i], vgtok[e0 + i]) for i in range(2)]
        out = yield from split([(XG, 10 + e0 + i, ss[i].ap, ts[i], [tm["vt_done"], tm["zf_done"]]) for i in range(2)])
        for i in range(2):
            xgtok[10 + e0 + i] = out[i]
            TR.give(ss[i], out[i])

    W2 = T_["w_in_2"]
    first = True
    for base, n, post in ((8, 3, post_hv), (5, 3, post_hx1), (14, 3, post_gv), (2, 3, post_hx0), (0, 2, post_pool), (11, 3, post_gu)):
        for c in range(n):
            proj(W2, base + c, range(4), X1k, post, pre=pre_b2 if first else None)
            first = False
    for c in range(8):
        proj(T_["w_out_2"], c, range(4), XGk, residual((["norm_ffn_2"], "ffn2", 1e-6)))

    def pre_ffn2():
        begin("ffn2")
        made.clear()
        fr = done()
        for i in range(16):
            slot_free[i] = fr

    def post_gate2(cts, bks, tok, frs):
        ss = [TR.take() for _ in "ab"]
        ts = yield from cconv(bks, tok, frs, [(s.ap, s.free) for s in ss], cts, "fc_w", "fc_b", 88)
        yield
        for i in range(2):
            g_tok[i] = act(lambda e, i=i: e.activation(ss[i].ap, ss[i].ap, ACT.Silu), ts[i])
            SG[i] = ss[i]

    def post_val2(cts, bks, tok, frs):
        ss = [TR.take() for _ in "ab"]
        ts = yield from cconv(bks, tok, frs, [(s.ap, s.free) for s in ss], [FT + c for c in cts], "fc_w", "fc_b", 88)
        yield
        yield from product(cts, ss, ts, dve)

    ffn(T_["w_gate_2"], T_["w_val_2"], T_["w_down_2"], post_gate2, post_val2, pre_ffn2,
        (None, "out", 1e-6))

    load_x()
    start()
    run()
    drain_all()
    rs_ap, rt, _ = res["out"]
    s_out = [sem(f"d_out{i}") for i in range(4)]
    outs = []
    for k in range(16):
        t = dve(lambda e, k=k: e.scalar_tensor_tensor(hk(k), hk(k), P("norm_final_2", k), rs_ap, ALU.mult, ALU.mult), rt, h[k])
        if k % 4 == 3:
            i = k // 4
            outs.append(dma("sp", s_out[i], T_["out"][:, i * 1024:(i + 1) * 1024], hT[:, i * 1024:(i + 1) * 1024], t))

    with nc.Block() as block:
        @block.sync
        def _(eng):
            for waits, fn, _ in q["sp"].items:
                for s, v in waits:
                    eng.wait_ge(s, v)
                fn(eng)
            for s, v in outs:
                eng.wait_ge(s, v)

        @block.tensor
        def _(eng):
            q["pe"].play(eng)

        @block.vector
        def _(eng):
            q["dve"].play(eng)

        @block.scalar
        def _(eng):
            q["act"].play(eng)

        @block.gpsimd
        def _(eng):
            q["pool"].play(eng)

    for g in reversed(pguards):
        g.__exit__(None, None, None)
    slab.__exit__(None, None, None)
    for g in reversed(sems):
        g.__exit__(None, None, None)


def kernel(**inputs):
    import math
    import numpy as np
    import concourse.bacc as bacc
    from concourse.bass_utils import run_bass_kernel_spmd

    f = np.float32
    I = {k: np.asarray(v) for k, v in inputs.items()}

    def pack(w, n=256, k=4):
        r, c = w.shape
        return np.ascontiguousarray(w.reshape(r // (128 * k), k, 128, c // n, n).transpose(3, 0, 2, 1, 4)).reshape(
            c // n, r // (128 * k), 128, k * n)

    def cols(v):
        return v.reshape(-1, 128).T

    def taps(w):
        return w.reshape(-1, 128).T

    def pad(v):
        o = np.zeros((128, 1), f)
        o[:v.shape[0], 0] = v
        return o

    w_in = I["w_in"][0]
    arr = {}
    arr["w_zx"] = pack(w_in[:, 0:5120])
    wd = np.zeros((2048, 128), f)
    wd[:, 0:32] = w_in[:, 5120:5152]
    arr["w_dt"] = pack(wd, 128, 8)
    arr["w_sc"] = pack(w_in[:, 5152:])
    arr["w_ossd"] = pack(I["w_out"][0][0:2048])
    arr["w_osc"] = pack(I["w_out"][0][2048:])
    for n in ("w_q", "w_k", "w_v", "w_o", "w_gate", "w_up", "w_down"):
        arr[n] = pack(I[n][0])
    arr["w_in_2"] = pack(I["w_in_2"][0])
    arr["w_out_2"] = pack(I["w_out_2"][0])
    arr["w_gate_2"] = pack(I["ffn_w_up_2"][0][:, 0:5632])
    arr["w_val_2"] = pack(I["ffn_w_up_2"][0][:, 5632:])
    arr["w_down_2"] = pack(I["ffn_w_down_2"][0])

    def fm(x):
        return np.ascontiguousarray(x.T.reshape(-1, 128, 256).transpose(1, 0, 2)).reshape(128, -1)

    arr["xT"] = fm(I["x"][0])
    arr["memT"] = fm(I["mem"][0])
    rc = np.ones((4, 16), f)
    t = np.arange(256)
    for g, w in enumerate((2, 4, 8, 16)):
        cnt = np.minimum(t + w // 2 - 1, 255) - np.maximum(t - w // 2, 0) + 1
        full = (w / cnt).astype(f)
        rc[g, 0:8], rc[g, 8:16] = full[0:8], full[248:256]
    P = {
        "norm_mix": cols(I["norm_mix"][0]), "conv_w": taps(I["ssd_conv_w"][0]), "conv_b": cols(I["ssd_conv_b"][0]),
        "ssd_norm": cols(I["ssd_norm"][0]), "d_skip": cols(np.repeat(I["d_skip"][0], 64)),
        "sc_w": taps(I["sc_conv_w"][0]), "sc_norm": cols(I["sc_norm"][0]), "mem_norm": cols(I["mem_norm"]),
        "norm_xa": cols(I["norm_xa"][0]), "norm_ffn": cols(I["norm_ffn"][0]), "norm_final": cols(I["norm_final"]),
        "norm_mix_2": cols(I["norm_mix_2"][0]), "pool_b": cols(I["pool_b_2"][0].reshape(-1)),
        "pool_scale": cols(I["pool_scale_2"][0]), "hy_w": taps(I["hy_short_w_2"][0]), "hy_b": cols(I["hy_short_b_2"][0]),
        "hy_skip": cols(I["hy_skip_2"][0]), "norm_ffn_2": cols(I["norm_ffn_2"][0]), "fc_w": taps(I["ffn_conv_w_2"][0]),
        "fc_b": cols(I["ffn_conv_b_2"][0]), "norm_final_2": cols(I["norm_final_2"]), "dt_bias": pad(I["dt_bias"][0]),
        "a_log": pad(I["a_log"][0]), "f_b1": pad(I["hy_filt_b1_2"][0]), "f_fr1": pad(I["hy_filt_freq1_2"][0]),
        "f_b2": pad(I["hy_filt_b2_2"][0]), "f_fr2": pad(I["hy_filt_freq2_2"][0]),
        "rcnt": np.broadcast_to(rc.reshape(1, 64), (128, 64)),
    }
    arr["par"] = np.ascontiguousarray(np.concatenate([P[n] for n, _ in PARAMS], axis=1))
    arr["ident"] = np.eye(128, dtype=f)
    s_, l_ = np.arange(128)[:, None], np.arange(128)[None, :]
    tri = (l_ >= s_).astype(f)
    arr["mask"] = np.ascontiguousarray(np.concatenate([tri, np.ones((128, 128), f), tri], axis=1))

    n = np.arange(256)[:, None]
    b = np.arange(256)[None, :]
    ang = 2 * np.pi * ((n * b) % 512) / 512
    sgn = (1.0 - 2.0 * (n % 2))
    Fm = np.concatenate([np.cos(ang), -np.sin(ang)], axis=1)
    Fm[:, 256:257] = sgn
    Gm = np.concatenate([np.cos(ang), np.sin(ang)], axis=1)
    Gm[:, 256:257] = sgn
    Gm[0, :] = 0.0
    wgt = np.full((256, 1), 2.0)
    wgt[0] = 1.0
    Im = np.concatenate([wgt * np.cos(ang.T), -wgt * np.sin(ang.T)], axis=0) / 512
    Im[256, :] = sgn[:, 0] / 512

    def rows(m, k):
        return np.ascontiguousarray(m.astype(f).reshape(k, 128, -1).transpose(1, 0, 2)).reshape(128, -1)
    arr["dftF"], arr["dftG"], arr["dftI"] = rows(Fm, 2), rows(Gm, 2), rows(Im, 4)
    tt = np.linspace(0.0, 1.0, 256, dtype=f)[:, None]
    ww = (f(2.0 * math.pi) * np.arange(256, dtype=f)[:, None] / f(256)).astype(f)
    ff = np.linspace(1e-4, 15, 16, dtype=f)[None, :]
    arr["feat"] = np.ascontiguousarray(np.concatenate([tt, np.cos(ff * ww), -np.sin(ff * ww)], axis=1).astype(f).T)
    deltas = np.linspace(math.log(1e-2) / 1.5, math.log(1e-2) / 0.3, 768, dtype=f)
    arr["decay"] = rows(np.exp(-tt * np.abs(deltas)[None, :]), 2)
    arr["f_w1"], arr["f_w2"], arr["f_w3"] = (np.ascontiguousarray(I[f"hy_filt_w{i}_2"][0]) for i in (1, 2, 3))
    arr["gm_ws"] = np.ascontiguousarray(I["gm_w_s_2"][0].transpose(2, 0, 1)).reshape(128, 768)
    arr["gm_bs"] = np.ascontiguousarray(np.broadcast_to(I["gm_b_s_2"][0].reshape(1, 768), (128, 768)))
    arr["pool_w"] = np.ascontiguousarray(I["pool_w_2"][0].transpose(1, 0, 2)).reshape(128, 512)
    arr["gm_gb"] = np.ascontiguousarray(np.broadcast_to(
        np.concatenate([I["gm_ln_g_2"][0], I["gm_ln_b_2"][0]])[None, :], (128, 1536)))

    nc = bacc.Bacc("TRN2", target_bir_lowering=False, num_devices=1)
    T_ = {k: nc.dram_tensor(f"in_{k}", v.shape, mybir.dt.from_np(v.dtype), kind="ExternalInput").ap() for k, v in arr.items()}
    T_["out"] = nc.dram_tensor("out_0", (128, 4096), F32, kind="ExternalOutput").ap()
    program(nc, T_)
    r = run_bass_kernel_spmd(nc, [{f"in_{k}": v for k, v in arr.items()}], core_ids=[0])
    o = r.results[0]["out_0"]
    return np.ascontiguousarray(o.reshape(128, 16, 256).transpose(2, 1, 0)).reshape(1, 256, 2048)
```

```python
from collections import deque

import concourse.bass as bass
from concourse import mybir

F32 = mybir.dt.float32
F32R = mybir.dt.float32r
ALU = mybir.AluOpType
ACT = mybir.ActivationFunctionType
AX = mybir.AxisListType

L = 256
D = 2048
KT = 16
FT = 44
NRAW = 4
NT = 13
NR = 6
NA = 13824
NW = 4
UK = 4
UN = UK * 256
SPLIT_AHEAD = 3
LANE = 3
LAG = 4

PARAMS = [
    ("norm_mix", 16), ("conv_w", 96), ("conv_b", 24), ("ssd_norm", 16), ("d_skip", 16),
    ("sc_w", 48), ("sc_norm", 16), ("mem_norm", 16), ("norm_xa", 16), ("norm_ffn", 16),
    ("norm_final", 16), ("norm_mix_2", 16), ("pool_b", 4), ("pool_scale", 4), ("hy_w", 54),
    ("hy_b", 18), ("hy_skip", 6), ("norm_ffn_2", 16), ("fc_w", 264), ("fc_b", 88),
    ("norm_final_2", 16), ("dt_bias", 1), ("a_log", 1), ("f_b1", 1), ("f_fr1", 1), ("f_b2", 1),
    ("f_fr2", 1), ("rcnt", 64),
]
POFF = {}
_o = 0
for _n, _c in PARAMS:
    POFF[_n] = _o
    _o += _c
NPAR = _o

MAP = {}
_o = 0
for _n, _c in [("hT", 4096), ("X1", 8192), ("XG", 8192), ("raw", NRAW * UN), ("wh", NW * UN), ("wl", NW * UN),
               ("par", NPAR), ("ident", 128), ("ones", 128), ("gg", 16), ("root", 1), ("T", NT * 256), ("R", NR * 264), ("RS", 512), ("A", NA)]:
    MAP[_n] = _o
    _o += (_c + 7) // 8 * 8
NWORDS = _o

A_ATT = dict(kT=0, v=1024)
A_MIX = dict(XS=2048, ZS=4096, BT=6144, CT=7168, cbm=8192, mask=9728, dtb=10112, dcol=12160, D=(10112, 12288), M=(10880, 13056),
             xdt=(11648, 6144), U=12288, C=12800, V=13312, sq=2048, n0=2560, n1=3072, n2=3584)
A_MEM = 2048
A_XA = dict(qT=2048, P=3072, PT=5120, st=7168)
A_FIL = dict(K=0, F=3840, G=4864, dec=5888, w3=7424, hf=8960, feat=12032, w1=12288, w2=12352, s=12416)
A_B2 = dict(K=0, F=3840, IF=4864, z=5888, x0=7424, vg=8960, ws=10496, bs=11264, wp=12032, rc=12544)
G_B2 = dict(zt=2048, zf=5120, vt=6656, gain=0, t=3584)


class Queue:

    def __init__(self, name, sem):
        self.name, self.sem, self.n, self.items = name, sem, 0, []

    def add(self, fn, waits, inc):
        tok = None
        if inc:
            self.n += 1
            tok = (self.sem, self.n)
        self.items.append((flat(waits), fn, inc))
        return tok

    def play(self, eng):
        seen = {}
        for waits, fn, inc in self.items:
            for sem, val in waits:
                if seen.get(id(sem), 0) < val:
                    eng.wait_ge(sem, val)
                    seen[id(sem)] = val
            ins = fn(eng)
            if inc:
                ins.then_inc(self.sem, 1)


def flat(x):
    if x is None:
        return []
    if isinstance(x, tuple) and len(x) == 2 and isinstance(x[1], int):
        return [x]
    out = []
    for y in x:
        out += flat(y)
    return out


class Slot:
    def __init__(self, ap):
        self.ap, self.free = ap, []


class Ring:

    def __init__(self, aps):
        self.slots = deque(Slot(a) for a in aps)

    def take(self):
        assert self.slots, "no buffer left"
        return self.slots.popleft()

    def give(self, slot, *toks):
        slot.free = flat(toks)
        self.slots.append(slot)


def program(nc, T_):
    sems = []

    def sem(name):
        g = nc.semaphore(name)
        s = g.__enter__()
        sems.append(g)
        return s

    def at(name, words, dt=F32, base=None, off=0):
        b = MAP[base or name] + off
        return nc.alloc_sbuf_tensor_at(name, [128, words], dt, offset=4 * b + BASE)

    BASE = (nc.sbuf_base + 31) // 32 * 32
    slab = nc.sbuf_tensor("slab", [128, NWORDS + 8], F32)
    slab.__enter__()
    hT = at("hT", 4096)
    X1 = at("X1", 8192, F32R)
    XG = at("XG", 8192, F32R)
    Gf = at("Gf", 8192, F32, base="XG")
    raw = at("raw", NRAW * UN)
    wh = at("wh", NW * UN, F32R)
    wl = at("wl", NW * UN, F32R)
    par = at("par", NPAR)
    ident = at("ident", 128)
    ones = at("ones", 128)
    gg = at("gg", 16)
    root = at("root", 1)
    Tt = at("T", NT * 256)
    Rt = at("R", NR * 264)
    RS = at("RS", 512)
    A = at("A", NA)

    pguards = [nc.psum_tensor(f"ps{i}", [128, 512], F32) for i in range(8)]
    banks = [g.__enter__() for g in pguards]

    q = {n: Queue(n, sem("s_" + n)) for n in ("pe", "act", "dve", "pool", "sp")}

    def pe(fn, *w, inc=True):
        return q["pe"].add(fn, w, inc)

    def act(fn, *w):
        return q["act"].add(fn, w, True)

    def dve(fn, *w):
        return q["dve"].add(fn, w, True)

    def pool(fn, *w):
        return q["pool"].add(fn, w, True)

    dcount = {}

    def dma(queue, s, out, in_, *w):
        dcount[id(s)] = dcount.get(id(s), 0) + 16

        def fn(e):
            return e.dma_start(out, in_).then_inc(s, 16)
        q[queue].add(fn, w, False)
        return (s, dcount[id(s)])

    def done():
        return [(x.sem, x.n) for x in q.values() if x.n and x.name != "sp"]

    def P(name, i=0, n=1, p=128):
        return par[0:p, POFF[name] + i:POFF[name] + i + n]

    def a_(off, n, p=128):
        return A[0:p, off:off + n]

    TR = Ring([Tt[:, i * 256:(i + 1) * 256] for i in range(NT)])
    RR = Ring([Rt[:, i * 264:(i + 1) * 264] for i in range(NR)])
    AUX = Ring([banks[i][:, :] for i in range(4, 8)])

    s_par = sem("d_par")
    s_x, s_mem = ([sem(f"d_{n}{i}") for i in range(4)] for n in ("x", "m"))
    memT = A[:, A_MEM:A_MEM + 4096]
    t_mem, t_x = ([(s, 16) for s in ss for _ in range(4)] for ss in (s_mem, s_x))
    t_par = (s_par, 16)
    s_id = sem("d_id")
    t_id = (s_id, 16)

    def load_mem(i):
        dma("sp", s_mem[i], memT[:, i * 1024:(i + 1) * 1024], T_["memT"][:, i * 1024:(i + 1) * 1024])
    t_ones = pool(lambda e: e.memset(ones[:, :], 1.0))
    t_pad = pool(lambda e: e.memset(Rt[:, :], 0.0))
    for s in RR.slots:
        s.free = [t_pad]

    dve(lambda e: e.tensor_tensor(gg[:, :], P("norm_final", 0, 16), P("norm_mix_2", 0, 16), ALU.mult), t_par)

    def load_x(i):
        dma("sp", s_x[i], hT[:, i * 1024:(i + 1) * 1024], T_["xT"][:, i * 1024:(i + 1) * 1024])

    h = [[None] for _ in range(KT)]

    def hk(k):
        return hT[:, k * 256:(k + 1) * 256]

    def rsqrt(v, y, u, t, vfree=None, wide=False):
        if wide:
            t1 = act(lambda e: e.activation(u, v, ACT.Ln), t, vfree)
            t2 = act(lambda e: e.activation(y, u, ACT.Exp, scale=-0.5), t1, vfree)
            yield
        else:
            t1 = act(lambda e: e.activation(u, v, ACT.Sqrt), t, vfree)
            yield
            t2 = dve(lambda e: e.reciprocal(y, u), t1, vfree)
        t3 = dve(lambda e: e.tensor_tensor(u, y, y, ALU.mult), t2)
        t4 = dve(lambda e: e.scalar_tensor_tensor(u, u, -0.5, v, ALU.mult, ALU.mult), t3)
        return dve(lambda e: e.scalar_tensor_tensor(y, u, 1.5, y, ALU.add, ALU.mult), t4)

    def split(items):
        out = []
        for X, k, src, tok, free, *g in items:
            hi = X[:, k * 512:k * 512 + 256]
            sc = g[0] if g else 1.0
            out.append([act(lambda e, hi=hi, src=src, sc=sc: e.activation(hi, src, ACT.Copy, scale=sc), tok, free,
                            t_par if g else None)])
        yield
        for n, (X, k, src, tok, free, *g) in enumerate(items):
            hi, lo = X[:, k * 512:k * 512 + 256], X[:, k * 512 + 256:k * 512 + 512]
            if g:
                fn = lambda e, hi=hi, lo=lo, src=src, g=g[0]: e.scalar_tensor_tensor(lo, src, g, hi.bitcast(F32), ALU.mult, ALU.subtract)
            else:
                fn = lambda e, hi=hi, lo=lo, src=src: e.tensor_tensor(lo, src, hi.bitcast(F32), ALU.subtract)
            out[n].append(dve(fn, out[n][0], tok, free))
        return out

    root_tok = [None]

    class Norm:

        def __init__(self, n):
            self.n, self.i, self.bank, self.acc, self.atok = n, 0, AUX.take(), None, None

        def pair(self, srcs, scales=(1.0, 1.0)):
            ss = []
            for (src, tok), sc in zip(srcs, scales):
                s = TR.take()
                ss.append((s, act(lambda e, s=s, src=src, sc=sc: e.activation(s.ap, src, ACT.Square, scale=sc), tok, s.free)))
            yield
            i = self.i
            self.i += 1
            (s0, t0), (s1, t1) = ss
            if i == self.n - 2:
                root_tok[0] = act(lambda e: e.activation(root[:, :], ones[:, 0:1], ACT.Sqrt), t_ones, root_tok[0])
            if i < self.n - 1:
                t = pool(lambda e: e.tensor_tensor(s0.ap, s0.ap, s1.ap, ALU.add), t0, t1)
                TR.give(s1, t)
                if self.acc is None:
                    self.acc, self.atok = s0, t
                else:
                    acc = self.acc
                    self.atok = pool(lambda e: e.tensor_tensor(acc.ap, acc.ap, s0.ap, ALU.add), t, self.atok)
                    TR.give(s0, self.atok)
                return
            t = dve(lambda e: e.tensor_tensor(s0.ap, s0.ap, s1.ap, ALU.add), t0, t1)
            TR.give(s1, t)
            ps, acc = self.bank.ap[:, 0:256], self.acc
            yield
            t1 = pe(lambda e: e.matmul(ps, ones[:, :], acc.ap, start=True, stop=False), self.atok, t_ones, self.bank.free)
            yield
            self.tok = pe(lambda e: e.matmul(ps, ones[:, :], s0.ap, start=False, stop=True), t)
            TR.give(acc, t1)
            TR.give(s0, self.tok)

        def finish(self, n, eps, keep, kfree=None):
            assert self.i == self.n
            v, u = TR.take(), TR.take()
            ps = self.bank.ap[:, 0:256]
            t = dve(lambda e: e.tensor_scalar(v.ap, ps, 1.0 / n, eps, ALU.mult, ALU.add), self.tok, v.free)
            AUX.give(self.bank, t)
            t = yield from rsqrt(v.ap, keep, u.ap, t, [u.free, kfree])
            TR.give(v, t)
            TR.give(u, t)
            return t

    rs_now = {}

    def evac(pairs, tok, frees):
        key = rs_now["key"]
        ts = []
        for (bank, out, ofree), fr in zip(pairs, frees):
            tmp = TR.take()
            ts.append((tmp, act(lambda e, tmp=tmp, bank=bank: e.activation(tmp.ap, bank[:, 256:512], ACT.Copy), tok, tmp.free)))
        out_t = []
        for (bank, out, ofree), fr, (tmp, t) in zip(pairs, frees, ts):
            t = dve(lambda e, tmp=tmp, bank=bank, out=out: e.tensor_tensor(out, bank[:, 0:256], tmp.ap, ALU.add), t, ofree)
            TR.give(tmp, t)
            fr.append(t)
            out_t.append(t)
        while key not in res:
            yield
        rs, rt, ri = res[key]
        for n, (bank, out, ofree) in enumerate(pairs):
            out_t[n] = dve(lambda e, out=out: e.tensor_tensor(out, out, rs, ALU.mult), out_t[n], rt)
        scale_last[ri] = out_t
        return out_t

    units = []

    def proj(W, col, groups, X, post, w=256, kn=UK, mode="A", pre=None):
        n = len(groups)
        for i, g in enumerate(groups):
            units.append(dict(src=W[col, g], g=g, kn=kn, w=w, X=X, post=post if i == n - 1 else None,
                              start=i == 0, stop=i == n - 1, mode=mode, col=col, pre=pre if i == 0 else None))

    s_raw = [sem(f"d_raw{i}") for i in range(NRAW)]
    raw_free = [[] for _ in range(NRAW)]
    w_free = [[] for _ in range(NW)]
    bank_free = [[[()], [()]], [[()], [()]]]
    raw_tok, split_tok = {}, {}

    def load_unit(i):
        s = i % NRAW
        raw_tok[i] = dma("sp", s_raw[s], raw[:, s * UN:(s + 1) * UN], units[i]["src"], raw_free[s])

    def split_unit(i):
        s, r = i % NW, i % NRAW
        src, hi, lo = raw[:, r * UN:(r + 1) * UN], wh[:, s * UN:(s + 1) * UN], wl[:, s * UN:(s + 1) * UN]
        t1 = act(lambda e: e.activation(hi, src, ACT.Copy), raw_tok[i], w_free[s])
        t2 = dve(lambda e: e.tensor_tensor(lo, src, hi.bitcast(F32), ALU.subtract), t1, w_free[s])
        raw_free[r] = [t1, t2]
        split_tok[i] = [t1, t2]

    tasks = deque()
    chains = []

    def step():
        before = None
        for c in list(tasks)[:3]:
            if before is not None and before - c[2] < LANE:
                break
            c[2] += 1
            before = c[2]
            try:
                next(c[1])
            except StopIteration:
                tasks.remove(c)
                before = 1 << 20
                if not tasks:
                    break

    def advance():
        for c in list(chains):
            if c[2] or c not in chains:
                continue
            c[2] = True
            try:
                next(c[1])
                c[2] = False
            except StopIteration:
                chains.remove(c)

    def finish_chains(name=None):
        while any(name is None or c[0] == name for c in chains):
            for c in list(chains):
                if name is None or c[0] == name:
                    try:
                        next(c[1])
                    except StopIteration:
                        chains.remove(c)

    def chain(name, gen):
        c = [name, gen, True]
        chains.append(c)
        try:
            next(gen)
            c[2] = False
        except StopIteration:
            chains.remove(c)

    def drain(name=None):
        while any(name is None or c[0] == name for c in tasks):
            step()

    def drain_all():
        finish_chains()
        drain()
        finish_chains()

    def run():
        pair = [0]
        for j in range(NRAW):
            load_mem(j)
            load_unit(j)
            if j == 0:
                dma("sp", s_par, par[:, :], T_["par"])
        dma("sp", s_id, ident[:, :], T_["ident"])
        n_split = 0
        for i, u in enumerate(units):
            while n_split < min(i + 1 + (i > 0) + 2 * (i > 4), i + 1 + SPLIT_AHEAD, len(units)):
                split_unit(n_split)
                if n_split + NRAW < len(units):
                    load_unit(n_split + NRAW)
                if n_split < 4:
                    load_x(n_split)
                n_split += 1
            if i == 0:
                start()
            if i == 4:
                start_x()
            if u["pre"]:
                u["pre"]()
            s, w, kn = i % NW, u["w"], u["kn"]
            p = pair[0] % 2
            nb = 2 if w == 256 else 1
            while u["start"] and not all(bank_free[p]):
                advance()
            for kk in range(kn):
                k = u["g"] * kn + kk
                x, xt = u["X"](k)
                for c in range(nb):
                    bank = banks[2 * p + c]
                    st, sp = u["start"] and kk == 0, u["stop"] and kk == kn - 1
                    last = c == nb - 1 and kk == kn - 1
                    wt = [split_tok[i] if kk == 0 and c == 0 else None, xt, bank_free[p][c] if st else None]
                    b0 = s * UN + kk * w
                    if u["mode"] == "A":
                        W1, W2 = wh[:, b0 + 128 * c:b0 + 128 * c + 128], wl[:, b0 + 128 * c:b0 + 128 * c + 128]
                        pe(lambda e, bank=bank, W1=W1, x=x, st=st: e.matmul(bank[:, :], W1, x, start=st, stop=False),
                           *wt, inc=False)
                        t = pe(lambda e, bank=bank, W2=W2, x=x, sp=sp: e.matmul(bank[:, 0:256], W2, x[:, 0:256],
                                                                               start=False, stop=sp), inc=last)
                    else:
                        W1, W2 = wh[:, b0:b0 + 256], wl[:, b0:b0 + 256]
                        xh, xl = x[:, c * 128:c * 128 + 128], x[:, 256 + c * 128:384 + c * 128]
                        for m, (l, r) in enumerate([(xh, W1), (xh, W2), (xl, W1)]):
                            t = pe(lambda e, bank=bank, l=l, r=r, st=st, sp=sp, m=m: e.matmul(
                                bank[:, 0:256], l, r, start=st and m == 0, stop=sp and m == 2),
                                *wt, inc=last and m == 2)
            w_free[s] = [t]
            if u["post"]:
                fr = [[] for _ in range(nb)]
                chain(u["post"].__name__, u["post"]([u["col"] * nb + c for c in range(nb)],
                                                    [banks[2 * p + c] for c in range(nb)], t, fr))
                for c in range(nb):
                    bank_free[p][c] = fr[c]
                pair[0] += 1
            advance()
            step()

    def X1k(k):
        while x1tok[k] is None:
            advance()
        return X1[:, k * 512:(k + 1) * 512], x1tok[k]

    def XGk(k):
        while xgtok[k % 16] is None:
            advance()
            step()
        return XG[:, (k % 16) * 512:(k % 16 + 1) * 512], xgtok[k % 16]

    x1tok, xgtok = [None] * 16, [None] * 16

    x1free = [[]]

    kT = lambda i: a_(A_ATT["kT"] + 256 * i, 256)
    vv = lambda mt: a_(A_ATT["v"] + 512 * mt, 512)
    kT_tok, v_tok = [None] * 4, []
    scale_buf = [RS[:, 0:256], RS[:, 256:512]]
    scale_n = [0]

    def new_scale():
        scale_n[0] += 1
        i = scale_n[0] % 2
        return scale_buf[i], i, scale_last[i]

    scale_last = [[], []]

    def gained(k, src, tok, gain, X, toks, free):
        out = yield from split([(X, k + i, src[i], tok[i], free, gain(k + i)) for i in range(2)])
        for i in range(2):
            toks[k + i] = out[i]

    def input_norm(src, tok, gain, X, toks, key):
        n = Norm(8)
        for k in range(0, 16 + LAG, 2):
            if k < 16:
                yield from gained(k, [src(k), src(k + 1)], tok[k:k + 2], gain, X, toks, None)
            if k >= LAG:
                yield from n.pair([(src(k - LAG + i), tok[k - LAG + i]) for i in range(2)])
        ap, i, fr = new_scale()
        t = yield from n.finish(D, 1e-5, ap, fr)
        res[key] = (ap, t, i)

    res = {}

    def use_scale(key):
        rs_now["key"] = key

    memc = a_(A_MEM + 4096, 2)

    def fast(gen, n):
        i = 0
        for _ in gen:
            i += 1
            if i % n == 0:
                yield

    def mem_task():
        yield from input_norm(lambda k: memT[:, k * 256:(k + 1) * 256], t_mem, lambda k: P("mem_norm", k), XG, xgtok, "mem")
        ap, tok, i = res["mem"]
        yield
        yield
        yield
        bk = AUX.take()
        for st in range(2):
            t = pe(lambda e, st=st: e.transpose(bk.ap[:, 128 * st:128 * st + 128], ap[:, 128 * st:128 * st + 128], ident[:, :]),
                   tok, bk.free, t_id)
        yield
        t = act(lambda e: e.activation(memc, bk.ap[:, 0:256:128], ACT.Copy), t)
        AUX.give(bk, t)
        tm["memc"] = t
        scale_last[i] = scale_last[i] + [t]

    def start_x():
        chain("n1", fast(input_norm(hk, t_x, lambda k: P("norm_mix", k), X1, x1tok, "x"), 2))

    def start():
        use_scale("mem")
        chain("mem", fast(mem_task(), 2))

    def post_k(cts, bks, tok, frs):
        r = yield from evac([(b, kT(ct), None) for ct, b in zip(cts, bks)], tok, frs)
        for ct, t in zip(cts, r):
            kT_tok[ct] = t
        yield

    def post_v(cts, bks, tok, frs):
        col = cts[0] // 2
        while "memc" not in tm:
            yield
        for mt in range(2):
            t = act(lambda e, mt=mt: e.activation(vv(mt)[:, col * 256:(col + 1) * 256], bks[mt][:, 0:256], ACT.Copy,
                                                  scale=memc[:, mt:mt + 1]), tok, tm["memc"])
            v_tok.append(t)
            frs[mt].append(t)
        yield

    tm = {}
    for c in range(2):
        proj(T_["w_k"], c, range(4), XGk, post_k)
    for c in range(2):
        proj(T_["w_v"], c, range(4), XGk, post_v, mode="B")

    def begin_mix():
        for k in range(16):
            h[k] = t_x[k]
        use_scale("x")

    def conv(items, ntap, off, wname, nch, bname=None):
        ts = []
        for src, out, wi, stok, ofree in items:
            b = P(bname, wi) if bname else 0.0
            ts.append(act(lambda e, src=src, out=out, wi=wi, b=b: e.activation(
                out, src[:, off:off + 256], ACT.Identity, scale=P(wname, wi), bias=b), stok, ofree, t_par))
        yield
        for k in range(1, ntap):
            for n, (src, out, wi, stok, ofree) in enumerate(items):
                ts[n] = dve(lambda e, k=k, src=src, out=out, wi=wi: e.scalar_tensor_tensor(
                    out, src[:, off + k:off + k + 256], P(wname, k * nch + wi), out, ALU.mult, ALU.add), ts[n], stok)
        return ts

    am = A_MIX
    Uo, Co, Vo = ([a_(am[n] + 256 * i, 256) for i in range(2)] for n in "UCV")
    cfree, vfree, ufree = [None], [None], [None]
    u_tok, c_tok = [None, None], [None, None]

    def post_u(cts, bks, tok, frs):
        u_tok[:] = yield from evac([(b, Uo[i], ufree[0]) for i, b in enumerate(bks)], tok, frs)
        yield

    def post_c(cts, bks, tok, frs):
        ss, rr = [TR.take() for _ in "ab"], [RR.take() for _ in "ab"]
        ts = yield from evac([(b, s.ap, s.free) for b, s in zip(bks, ss)], tok, frs)
        yield
        for i in range(2):
            ts[i] = pool(lambda e, i=i: e.tensor_tensor(rr[i].ap[:, 3:259], ss[i].ap, Uo[i], ALU.mult),
                         ts[i], u_tok[i], rr[i].free)
            TR.give(ss[i], ts[i])
        ufree[0] = list(ts)
        yield
        j = cts[0] - 32
        ts = yield from conv([(rr[i].ap, Co[i], j + i, ts[i], cfree[0]) for i in range(2)], 3, 1, "sc_w", 16)
        c_tok[:] = ts
        for r, t in zip(rr, ts):
            RR.give(r, t)

    def post_b(cts, bks, tok, frs):
        j = cts[0] - 16
        finish_chains("post_c")
        ss = [TR.take() for _ in "ab"]
        ts = yield from evac([(b, s.ap, s.free) for b, s in zip(bks, ss)], tok, frs)
        yield
        for i in range(2):
            ts[i] = pool(lambda e, i=i: e.tensor_tensor(Vo[i], ss[i].ap, Co[i], ALU.mult), ts[i], c_tok[i], vfree[0])
            TR.give(ss[i], ts[i])
        cfree[0] = list(ts)
        yield
        V, sq, v, u, y = (a_(am[n], 512) for n in ("V", "sq", "n0", "n1", "n2"))
        t = act(lambda e: e.activation(sq, V, ACT.Square), ts, scfree[0])
        yield
        bk = AUX.take()
        t = pe(lambda e: e.matmul(bk.ap[:, :], ones[:, :], sq, start=True, stop=True), t, bk.free)
        yield
        t = dve(lambda e: e.tensor_scalar(v, bk.ap[:, :], 1.0 / 128, 1e-5, ALU.mult, ALU.add), t, scfree[0])
        AUX.give(bk, t)
        t = yield from rsqrt(v, y, u, t, scfree[0], wide=True)
        yield
        tt = [dve(lambda e, i=i: e.scalar_tensor_tensor(Vo[i], Vo[i], P("sc_norm", j + i), y[:, 256 * i:256 * i + 256],
                                                        ALU.mult, ALU.mult), t) for i in range(2)]
        scfree[0] = tt
        out = yield from split([(XG, j + i, Vo[i], tt[i], xgfree[0]) for i in range(2)])
        vfree[0] = out
        for i in range(2):
            xgtok[j + i] = out[i]

    scfree = [None]
    xgfree = [[]]

    def begin_sc():
        begin_mix()
        xgfree[0] = done()
        scfree[0] = xgfree[0]
        ufree[0] = xgfree[0]
        xgtok[:] = [None] * 16

    mask = a_(am["mask"], 384)
    s_mask = sem("d_mask")
    dtb = [a_(am["dtb"] + 256 * i, 256, 32) for i in range(8)]
    dcol = a_(am["dcol"], 128)
    acs = dtb[7]

    def post_dt(cts, bks, tok, frs):
        bank, fr = bks[0], frs[0]
        ps = [bank[0:32, 0:256], bank[0:32, 256:512]]
        x, b1, b2, b3, b4, al, b6 = dtb[:7]
        t1 = act(lambda e: e.activation(b1, ps[1], ACT.Copy), tok)
        t2 = dve(lambda e: e.tensor_tensor(x, ps[0], b1, ALU.add), t1)
        fr.append(t2)
        key = rs_now["key"]
        while key not in res:
            yield
        rs, rt, _ = res[key]
        t2 = dve(lambda e: e.tensor_tensor(x, x, rs[0:32, :], ALU.mult), t2, rt)
        t3 = dve(lambda e: e.tensor_scalar(x, x, P("dt_bias", p=32), None, ALU.add), t2, t_par)
        yield
        t4 = act(lambda e: e.activation(b1, x, ACT.Abs), t3)
        t5 = act(lambda e: e.activation(b1, b1, ACT.Exp, scale=-1.0), t4)
        t14 = act(lambda e: e.activation(al[:, 0:1], P("a_log", p=32), ACT.Exp), t_par)
        yield
        t6 = dve(lambda e: e.tensor_scalar(b2, b1, 1.0, None, ALU.add), t5)
        yield
        t7 = act(lambda e: e.activation(b3, b2, ACT.Ln), t6)
        t8 = dve(lambda e: e.tensor_scalar(b4, b2, -1.0, None, ALU.add), t6)
        t9 = dve(lambda e: e.tensor_tensor(b4, b1, b4, ALU.subtract), t8)
        t10 = dve(lambda e: e.reciprocal(b6, b2), t6)
        t11 = dve(lambda e: e.tensor_tensor(b4, b4, b6, ALU.mult), t9, t10)
        yield
        t12 = dve(lambda e: e.tensor_tensor(b4, b4, b3, ALU.add), t11, t7)
        t13 = dve(lambda e: e.scalar_tensor_tensor(b4, x, 0.0, b4, ALU.max, ALU.add), t12)
        t15 = dve(lambda e: e.tensor_scalar(b2, b4, al[:, 0:1], -1.0, ALU.mult, ALU.mult), t13, t14, t7)
        t16 = dve(lambda e: e.memset(b3, 1.0), t12)
        t17 = dve(lambda e: e.tensor_tensor_scan(acs, b3, b2, 0.0, ALU.mult, ALU.add), t15, t16)
        yield
        yield
        yield
        bk = AUX.take()
        for n, (src, tk) in enumerate([(acs, t17), (b4, t13)]):
            for st in range(2):
                o = 64 * n + 32 * st
                t = pe(lambda e, src=src, st=st, o=o: e.transpose(bk.ap[:, o:o + 32], src[:, 128 * st:128 * st + 128],
                                                                  ident[0:32, 0:32]), tk, bk.free, t_id)
        yield
        t = act(lambda e: e.activation(dcol, bk.ap[:, 0:128], ACT.Copy), t)
        AUX.give(bk, t)
        tm["dt"] = t
        tm["acs"] = t17

    def post_xbc(dstf):
        def post(cts, bks, tok, frs):
            i0 = cts[0] - 16
            rr = [RR.take() for _ in "ab"]
            ts = yield from evac([(b, r.ap[:, 3:259], r.free) for b, r in zip(bks, rr)], tok, frs)
            yield
            ss = [TR.take() for _ in "ab"]
            ts = yield from conv([(rr[i].ap, ss[i].ap, i0 + i, ts[i], ss[i].free) for i in range(2)], 4, 0, "conv_w", 24, "conv_b")
            yield
            for i in range(2):
                RR.give(rr[i], ts[i])
                out, ofree = dstf(i0 + i)
                t2 = act(lambda e, i=i, out=out: e.activation(out, ss[i].ap, ACT.Silu), ts[i], ofree)
                TR.give(ss[i], t2)
                tm[("xbc", i0 + i)] = t2
                if i0 + i >= 20:
                    tasks.append(["cb", cb_task(i0 + i - 20), 0])
        return post

    def bc_dst(i):
        o = am["BT"] + 256 * (i - 16)
        return a_(o, 256), None

    def cb_task(g):
        yield
        yield
        yield
        bk = AUX.take()
        B, C = a_(am["BT"] + 256 * g, 256), a_(am["CT"] + 256 * g, 256)
        w = [tm[("xbc", 16 + g)], tm[("xbc", 20 + g)], bk.free]
        pe(lambda e: e.matmul(bk.ap[:, 0:256], B[:, 0:128], C[:, 0:256], start=True, stop=True), *w)
        t = pe(lambda e: e.matmul(bk.ap[:, 256:384], B[:, 128:256], C[:, 128:256], start=True, stop=True))
        yield
        t = dve(lambda e: e.tensor_tensor(a_(am["cbm"] + 384 * g, 384), bk.ap[:, 0:384], mask, ALU.mult), t, tm["mask"])
        AUX.give(bk, t)
        tm[("cb", g)] = t

    xsfree, zsfree = [[] for _ in range(8)], [[] for _ in range(8)]

    def XS(j):
        return a_(am["XS"] + 256 * (j % 8), 256)

    def ZS(j):
        return a_(am["ZS"] + 256 * (j % 8), 256)

    def post_z(cts, bks, tok, frs):
        drain(f"ssd{cts[0] // 4 - 2}")
        r = yield from evac([(b, ZS(j), zsfree[j % 8]) for j, b in zip(cts, bks)], tok, frs)
        yield
        for j, t in zip(cts, r):
            tm[("z", j)] = act(lambda e, j=j: e.activation(ZS(j), ZS(j), ACT.Silu), t)
            tasks.append([f"ssd{j // 4}", ssd_task(j), 0])

    dfree, mfree, xfree = [None, None], [None, None], [None, None]
    gacc = {}

    def ssd_task(j):
        g, q_ = j // 4, j % 2
        xs, xt = XS(j), tm[("xbc", j)]
        tb, bb = AUX.take(), AUX.take()
        for st in range(2):
            t1 = pe(lambda e, st=st: e.transpose(tb.ap[:, 128 * st:128 * st + 128], xs[:, 128 * st:128 * st + 128], ident[:, :]),
                    xt, tb.free, t_id)
        for hh in range(2):
            t2 = pe(lambda e, hh=hh: e.matmul(bb.ap[:, 256 * hh:256 * hh + 256],
                                              ident[0:32, 2 * j + hh:2 * j + hh + 1].to_broadcast([32, 128]), acs,
                                              start=True, stop=True), tm["acs"], bb.free)
        yield
        xdt = a_(am["xdt"][q_], 256)
        for st in range(2):
            o = xdt[:, 128 * st:128 * st + 128].rearrange("p (a b) -> p a b", a=2)
            i0 = tb.ap[:, 128 * st:128 * st + 128].rearrange("p (a b) -> p a b", a=2)
            c = 64 + 32 * st + 2 * j
            i1 = dcol[:, c:c + 2].unsqueeze(2).to_broadcast([128, 2, 64])
            t3 = dve(lambda e, o=o, i0=i0, i1=i1: e.tensor_tensor(o, i0, i1, ALU.mult), t1, tm["dt"], xfree[q_])
        Dd, M = a_(am["D"][q_], 768), a_(am["M"][q_], 768)
        for hh in range(2):
            for st in range(2):
                o = Dd[:, 384 * hh + 256 * st:384 * hh + 256 + 128 * st]
                i0 = bb.ap[:, 256 * hh + 128 * st:256 * hh + 256]
                sc = dcol[:, 32 * st + 2 * j + hh:32 * st + 2 * j + hh + 1]
                t4 = act(lambda e, o=o, i0=i0, sc=sc: e.activation(o, i0, ACT.Relu, scale=-1.0, bias=sc),
                         t2, tm["dt"], dfree[q_])
        AUX.give(bb, t4)
        t5 = act(lambda e: e.activation(Dd, Dd, ACT.Exp, scale=-1.0), t4)
        yield
        cb = a_(am["cbm"] + 384 * g, 384)
        t6s = []
        for hh in range(2):
            t6 = (pool, dve)[hh](lambda e, hh=hh: e.tensor_tensor(M[:, 384 * hh:384 * hh + 384], Dd[:, 384 * hh:384 * hh + 384], cb,
                                                       ALU.mult), t5, tm[("cb", g)], mfree[q_])
            t6s.append(t6)
        dfree[q_] = t6 = t6s
        yield
        yield
        yo = tb.ap[:, 256:512]
        for hh in range(2):
            o = yo[64 * hh:64 * hh + 64, 0:256]
            o2 = yo[64 * hh:64 * hh + 64, 128:256]
            pe(lambda e, o=o, hh=hh: e.matmul(o, xdt[:, 64 * hh:64 * hh + 64], M[:, 384 * hh:384 * hh + 256],
                                              start=True, stop=False), t6, t3, inc=False)
            t7 = pe(lambda e, o2=o2, hh=hh: e.matmul(o2, xdt[:, 128 + 64 * hh:192 + 64 * hh],
                                                     M[:, 384 * hh + 256:384 * hh + 384], start=False, stop=True))
        mfree[q_] = [t7]
        xfree[q_] = [t7]
        yield
        t8 = dve(lambda e: e.scalar_tensor_tensor(xs, xs, P("d_skip", j), yo, ALU.mult, ALU.add), t7, t1, t_par)
        AUX.give(tb, t8)
        yield
        t9 = pool(lambda e: e.tensor_tensor(xs, xs, ZS(j), ALU.mult), t8, tm[("z", j)])
        zsfree[j % 8] = [t9]
        tm[("y", j)] = t9
        yield
        s = TR.take()
        t = act(lambda e: e.activation(s.ap, xs, ACT.Square), t9, s.free)
        while j % 4 and gacc.get("n") != j:
            yield
        if j % 4 == 0:
            gacc["s"], gacc["t"] = s, t
        else:
            acc = gacc["s"]
            gacc["t"] = pool(lambda e: e.tensor_tensor(acc.ap, acc.ap, s.ap, ALU.add), t, gacc["t"])
            TR.give(s, gacc["t"])
        gacc["n"] = j + 1
        if j % 4 == 3:
            chain(f"norm{g}", ssd_norm_task(g, gacc["s"], gacc["t"]))

    def ssd_norm_task(g, acc, t):
        yield
        bk = AUX.take()
        t = pe(lambda e: e.matmul(bk.ap[:, 0:256], ones[:, :], acc.ap, start=True, stop=True), t, bk.free)
        yield
        v, rs = TR.take(), TR.take()
        t = dve(lambda e: e.tensor_scalar(v.ap, bk.ap[:, 0:256], 1.0 / 512, 1e-5, ALU.mult, ALU.add), t, v.free)
        AUX.give(bk, t)
        rt = yield from rsqrt(v.ap, rs.ap, acc.ap, t, rs.free)
        TR.give(acc, rt)
        TR.give(v, rt)
        yield
        while ("osc", g // 2) not in tm:
            yield
        for n0 in (4 * g, 4 * g + 2):
            ts = [dve(lambda e, i=i: e.scalar_tensor_tensor(XS(i), XS(i), P("ssd_norm", i), rs.ap, ALU.mult, ALU.mult), rt)
                  for i in (n0, n0 + 1)]
            out = yield from split([(XG, n0 + i, XS(n0 + i), ts[i], xgfree[0]) for i in range(2)])
            for i in range(2):
                xgtok[n0 + i] = out[i]
                xsfree[(n0 + i) % 8] = out[i]
        TR.give(rs, ts)

    def xs_dst(i):
        drain(f"ssd{i // 4 - 2}")
        finish_chains(f"norm{i // 4 - 2}")
        return XS(i), xsfree[i % 8]

    def residual(norm=None):
        def post(cts, bks, tok, frs):
            k = cts[0]
            for i, b in enumerate(bks):
                if norm and (k == 14 or i == 1):
                    for o in (0, 256):
                        h[k + i] = dve(lambda e, i=i, b=b, o=o: e.tensor_tensor(hk(k + i), hk(k + i), b[:, o:o + 256], ALU.add),
                                       tok, h[k + i])
                    frs[i].append(h[k + i])
                    continue
                s = TR.take()
                t1 = act(lambda e, s=s, b=b: e.activation(s.ap, b[:, 256:512], ACT.Copy), tok, s.free)
                t2 = dve(lambda e, i=i, b=b: e.tensor_tensor(hk(k + i), hk(k + i), b[:, 0:256], ALU.add), t1, h[k + i])
                h[k + i] = pool(lambda e, i=i, s=s: e.tensor_tensor(hk(k + i), hk(k + i), s.ap, ALU.add), t1, t2)
                TR.give(s, h[k + i])
                frs[i] += [t1, t2]
            yield
            if norm:
                gains, key, eps = norm
                if k == 0:
                    cur[0] = Norm(8)
                    x1free[0] = done()
                src, tk = [hk(k), hk(k + 1)], h[k:k + 2]
                if k < 14:
                    yield
                if k == 0:
                    x1tok[:] = [None] * 16 if gains else x1tok
                    if key == "fin":
                        cur2[0] = Norm(8)
                if gains:
                    yield from gained(k, src, tk, gains, X1, x1tok, x1free[0])
                yield from cur[0].pair(list(zip(src, tk)))
                if key == "fin":
                    yield from cur2[0].pair(list(zip(src, tk)), [P("norm_final", k), P("norm_final", k + 1)])
                if key == "out":
                    for i in range(2):
                        h[k + i] = act(lambda e, i=i: e.activation(hk(k + i), hk(k + i), ACT.Copy, scale=P("norm_final_2", k + i)),
                                       h[k + i])
                if k == 14:
                    while cur[0].i < 8 or (key == "fin" and cur2[0].i < 8):
                        yield
                    ap, si, fr = new_scale()
                    rt = yield from cur[0].finish(D, eps, ap, fr)
                    if key == "fin":
                        yield from second_norm("norm_final", ap, rt)
                    else:
                        res[key] = (ap, rt, si)
        return post

    def second_norm(gain, r1, rt):
        bank, n2 = cur2[0].bank, cur2[0]
        v, u, y = TR.take(), TR.take(), TR.take()
        t = dve(lambda e: e.scalar_tensor_tensor(v.ap, bank.ap[:, 0:256], 1.0 / D, r1, ALU.mult, ALU.mult), n2.tok, rt, v.free)
        AUX.give(bank, t)
        t = dve(lambda e: e.tensor_tensor(v.ap, v.ap, r1, ALU.mult), t)
        t = dve(lambda e: e.tensor_scalar(v.ap, v.ap, 1e-6, None, ALU.add), t)
        yield
        t = yield from rsqrt(v.ap, y.ap, u.ap, t, [u.free, y.free])
        ap, si, fr = new_scale()
        t = dve(lambda e: e.tensor_tensor(ap, r1, y.ap, ALU.mult), t, fr)
        for s in (v, u, y):
            TR.give(s, t)
        res["fin"] = (ap, t, si)
        yield
        yield
        for k in range(16):
            t = act(lambda e, k=k: e.activation(hk(k), hk(k), ACT.Copy, scale=P(gain, k)), h[k], x1tok[k])
            h[k] = pool(lambda e, k=k: e.tensor_tensor(hk(k), hk(k), r1, ALU.mult), rt, t)
            if k % 2 == 1:
                yield
        scale_last[1 - si] = h[15]

    cur, cur2 = [None], [None]

    def begin(key):
        use_scale(key)

    proj(T_["w_dt"], 0, range(2), X1k, post_dt, w=128, kn=8, pre=begin_sc)
    for j in range(8):
        proj(T_["w_sc"], j, range(4), X1k, post_u)
        proj(T_["w_sc"], 16 + j, range(4), X1k, post_c)
        proj(T_["w_sc"], 8 + j, range(4), X1k, post_b)

    def pre_bc():
        tm["mask"] = dma("sp", s_mask, mask, T_["mask"])

    for c in range(4):
        proj(T_["w_zx"], 16 + c, range(4), X1k, post_xbc(bc_dst), pre=pre_bc if c == 0 else None)

    def pre_ssd():
        finish_chains()
        fr = done()
        dfree[:] = mfree[:] = xfree[:] = [fr] * 2
        for i in range(8):
            xsfree[i] = zsfree[i] = fr

    def pre_half(i):
        def f():
            xgfree[0] = done()
            xgtok[8 * i:8 * i + 8] = [None] * 8
            tm["osc", i] = True
        return f

    for g in range(4):
        for c in range(2):
            proj(T_["w_zx"], 8 + 2 * g + c, range(4), X1k, post_xbc(xs_dst),
                 pre=pre_ssd if g == c == 0 else pre_half(0) if g == 2 and c == 0 else None)
        for c in range(2):
            proj(T_["w_zx"], 2 * g + c, range(4), X1k, post_z)
        if g == 1:
            for c in range(8):
                proj(T_["w_osc"], c, [0, 1], XGk, residual())
    for c in range(8):
        proj(T_["w_osc"], c, [2, 3], XGk, residual())
    for c in range(8):
        proj(T_["w_ossd"], c, [0, 1], XGk, residual(), pre=pre_half(1) if c == 0 else None)
    for c in range(8):
        proj(T_["w_ossd"], c, [2, 3], XGk, residual((lambda k: P("norm_xa", k), "xa", 1e-5)))

    ax = A_XA
    SC = 128.0 ** -0.5
    pfree = [[]]

    def post_q(cts, bks, tok, frs):
        r = yield from evac([(b, a_(ax["qT"] + 256 * ct, 256), pfree[0]) for ct, b in zip(cts, bks)], tok, frs)
        yield
        for ct, t in zip(cts, r):
            chain("att", att_task(ct, t))

    def att_task(hd, t):
        yield
        qT = a_(ax["qT"] + 256 * hd, 256)
        sb = AUX.take()
        for st in range(2):
            t = pe(lambda e, st=st: e.matmul(sb.ap[:, 256 * st:256 * st + 256], qT[:, 128 * st:128 * st + 128], kT(hd),
                                             start=True, stop=True), t, kT_tok[hd], sb.free)
        yield
        Pp, PT = a_(ax["P"] + 512 * hd, 512), a_(ax["PT"] + 512 * hd, 512)
        st_ = a_(ax["st"] + 16 * hd, 16)
        tt = []
        for st in range(2):
            mx, nb, sm, ri = (st_[:, 8 * st + i:8 * st + i + 1] for i in range(4))
            src = sb.ap[:, 256 * st:256 * st + 256]
            o = Pp[:, 256 * st:256 * st + 256]
            ta = dve(lambda e, mx=mx, src=src: e.tensor_reduce(mx, src, AX.X, ALU.max), t, pfree[0])
            tb = dve(lambda e, nb=nb, mx=mx: e.tensor_scalar(nb, mx, -SC, None, ALU.mult), ta)
            tt.append((tb, nb, sm, ri, src, o))
        tq, tcs = [], []
        for tb, nb, sm, ri, src, o in tt:
            tc = act(lambda e, nb=nb, sm=sm, src=src, o=o: e.activation(o, src, ACT.Exp, bias=nb, scale=SC, accum_out=sm),
                     tb, ta)
            tcs.append(tc)
        for (tb, nb, sm, ri, src, o), tc in zip(tt, tcs):
            td = dve(lambda e, sm=sm, ri=ri: e.reciprocal(ri, sm), tc)
            tq.append(dve(lambda e, o=o, ri=ri: e.tensor_scalar(o, o, ri, None, ALU.mult), td))
        AUX.give(sb, tc)
        yield
        pb = AUX.take()
        for mt in range(2):
            for st in range(2):
                t = pe(lambda e, mt=mt, st=st: e.transpose(pb.ap[:, 256 * mt + 128 * st:256 * mt + 128 * st + 128],
                                                           Pp[:, 256 * st + 128 * mt:256 * st + 128 * mt + 128], ident[:, :]),
                       tq, pb.free)
        yield
        t = act(lambda e: e.activation(PT, pb.ap[:, :], ACT.Copy), t)
        AUX.give(pb, t)
        yield
        ob = AUX.take()
        for mt in range(2):
            t = pe(lambda e, mt=mt: e.matmul(ob.ap[:, 0:256], vv(mt)[:, 128 * hd:128 * hd + 128],
                                             PT[:, 256 * mt:256 * mt + 256], start=(mt == 0), stop=(mt == 1)),
                   t, v_tok, ob.free)
        s = TR.take()
        t = act(lambda e: e.activation(s.ap, ob.ap[:, 0:256], ACT.Copy), t, s.free)
        AUX.give(ob, t)
        [xgtok[hd]] = yield from split([(XG, hd, s.ap, t, xgfree[0])])
        TR.give(s, xgtok[hd])

    def pre_q():
        begin("xa")
        pfree[0] = done()
        xgfree[0] = pfree[0]
        xgtok[:] = [None] * 16
    for c in range(2):
        proj(T_["w_q"], c, range(4), X1k, post_q, pre=pre_q if c == 0 else None)
    for c in range(8):
        proj(T_["w_o"], c, [0], XGk, residual((lambda k: P("norm_ffn", k), "ffn", 1e-5)))

    af = A_FIL
    s_fil, s_f1 = sem("d_fil"), sem("d_f1")

    def sine(z, k, t):
        MAGIC = 12582912.0
        C1, C2, C3 = 6.28125, 0.0019350051879882812, 3.0199159819e-07
        t = dve(lambda e: e.tensor_scalar(k, z, 0.15915494309189535, MAGIC, ALU.mult, ALU.add), t)
        t = dve(lambda e: e.tensor_scalar(k, k, -MAGIC, None, ALU.add), t)
        for c in (C1, C2, C3):
            t = dve(lambda e, c=c: e.scalar_tensor_tensor(z, k, -c, z, ALU.mult, ALU.add), t)
        t = dve(lambda e: e.tensor_scalar(z, z, 3.1415925, -3.1415925, ALU.min, ALU.max), t)
        return act(lambda e: e.activation(z, z, ACT.Sin), t)

    def filter_task(fr):
        F, dec, w3, hf = (a_(af[n], w) for n, w in (("F", 1024), ("dec", 1536), ("w3", 1536), ("hf", 3072)))
        feat, w1, w2 = a_(af["feat"], 256, 33), a_(af["w1"], 64, 33), a_(af["w2"], 64, 64)
        z, kk, z2 = (a_(af["s"] + 256 * i, 256, 64) for i in range(3))
        K = a_(af["K"], 3840).rearrange("p (m c) -> p m c", m=5)
        dma("sp", s_f1, feat, T_["feat"], fr)
        dma("sp", s_f1, w1, T_["f_w1"], fr)
        dma("sp", s_f1, w2, T_["f_w2"], fr)
        t_f1 = dma("sp", s_f1, w3[0:64, :], T_["f_w3"], fr)
        dma("sp", s_fil, F, T_["dftF"], fr)
        t_fil = dma("sp", s_fil, dec, T_["decay"], fr)
        for _ in range(8):
            yield
        bk = AUX.take()
        t = pe(lambda e: e.matmul(bk.ap[0:64, 0:256], w1, feat, start=True, stop=True), t_f1, bk.free)
        yield
        t = dve(lambda e: e.tensor_scalar(z, bk.ap[0:64, 0:256], P("f_b1", p=64), P("f_fr1", p=64), ALU.add, ALU.mult), t, t_par)
        t = sine(z, kk, t)
        yield
        yield
        yield
        t = pe(lambda e: e.matmul(bk.ap[0:64, 0:256], w2, z, start=True, stop=True), t)
        yield
        t = dve(lambda e: e.tensor_scalar(z2, bk.ap[0:64, 0:256], P("f_b2", p=64), P("f_fr2", p=64), ALU.add, ALU.mult), t)
        AUX.give(bk, t)
        tz = sine(z2, kk, t)
        yield
        yield
        yield
        thf = []
        for st in range(2):
            for c in range(4):
                bk = AUX.take()
                t = pe(lambda e, st=st, c=c, bk=bk: e.matmul(bk.ap[:, 0:384], z2[:, 128 * st:128 * st + 128],
                                                             w3[0:64, 384 * c:384 * c + 384], start=True, stop=True), tz, bk.free)
                yield
                o = 1536 * st + 384 * c
                d = 768 * st + 384 * (c % 2)
                t = dve(lambda e, o=o, d=d, bk=bk: e.tensor_tensor(hf[:, o:o + 384], bk.ap[:, 0:384], dec[:, d:d + 384], ALU.mult),
                        t, t_fil)
                AUX.give(bk, t)
                thf.append(t)
                yield
        t0 = dve(lambda e: e.memset(hf[0:1, 768:1536], 0.0), thf)
        yield
        tsum = []
        for st in range(2):
            fw, bw = hf[:, 1536 * st:1536 * st + 768], hf[:, 1536 * st + 768:1536 * st + 1536]
            hs = dec[:, 768 * st:768 * st + 768]
            t = dve(lambda e, fw=fw, bw=bw, hs=hs: e.tensor_tensor(hs, fw, bw, ALU.add), t0)
            tsum.append(dve(lambda e, fw=fw, bw=bw: e.tensor_tensor(fw, fw, bw, ALU.subtract), t))
            yield
        yield
        tk = {}
        for m in range(5):
            lo, n = (128 * m, 128) if m < 4 else (256, 1)
            for c in range(2):
                bk = AUX.take()
                for st in range(2):
                    lhs = F[:, 512 * st + lo:512 * st + lo + n]
                    src = hf[:, 1536 * st:1536 * st + 768] if m in (2, 3) else dec[:, 768 * st:768 * st + 768]
                    rhs = src[:, 384 * c:384 * c + 384]
                    t = pe(lambda e, lhs=lhs, rhs=rhs, st=st, n=n, bk=bk: e.matmul(bk.ap[0:n, 0:384], lhs, rhs, start=(st == 0),
                                                                                  stop=(st == 1)),
                           tsum, t_fil, bk.free)
                yield
                if m == 4 and c == 0:
                    tc = dve(lambda e: e.tensor_copy(K[:, 4, :], K[:, 0, :]), tk[0, 0], tk[0, 1])
                tk[m, c] = act(lambda e, m=m, c=c, n=n, bk=bk: e.activation(K[0:n, m, 384 * c:384 * c + 384], bk.ap[0:n, 0:384],
                                                                            ACT.Copy), t, tc if m == 4 else None)
                AUX.give(bk, tk[m, c])
        t = dve(lambda e: e.memset(K[0:1, 2, :], 0.0), tk[2, 0], tk[2, 1])
        tm["K"] = [t] + list(tk.values())
        tm["F"] = t_fil

    g_tok = [None, None]
    sgfree = [None, None]
    ffn_free = [[]]
    slot_free = [[] for _ in range(16)]
    SG = [None, None]

    def pre_ffn():
        begin("ffn")
        fr = done()
        for i in range(16):
            slot_free[i] = fr
        tasks.append(["filter", filter_task(fr), 0])

    def post_gate(cts, bks, tok, frs):
        ss = [TR.take() for _ in "ab"]
        ts = yield from evac([(b, s.ap, s.free) for b, s in zip(bks, ss)], tok, frs)
        yield
        for i in range(2):
            g_tok[i] = act(lambda e, i=i: e.activation(ss[i].ap, ss[i].ap, ACT.Silu), ts[i])
            SG[i] = ss[i]

    def product(cts, ss, ts, gate):
        gg = list(SG)
        for i in range(2):
            ts[i] = gate(lambda e, i=i: e.tensor_tensor(ss[i].ap, ss[i].ap, gg[i].ap, ALU.mult), ts[i], g_tok[i])
            TR.give(gg[i], ts[i])
        yield
        k = cts[0]
        out = yield from split([(XG, (k + i) % 16, ss[i].ap, ts[i], slot_free[(k + i) % 16]) for i in range(2)])
        for i in range(2):
            xgtok[(k + i) % 16] = out[i]
            made.add(k + i)
            TR.give(ss[i], out[i])

    def post_up(cts, bks, tok, frs):
        ss = [TR.take() for _ in "ab"]
        ts = yield from evac([(b, s.ap, s.free) for b, s in zip(bks, ss)], tok, frs)
        yield
        yield from product(cts, ss, ts, dve)

    def after_down(kts, post):
        def p(cts, bks, tok, frs):
            if cts[1] == 15:
                for k in kts:
                    slot_free[k % 16] = [tok]
            yield from post(cts, bks, tok, frs)
        return p

    made = set()

    def ready(kts):
        def f():
            while not all(k in made for k in kts):
                advance()
        return f

    def ffn(Wg, Wu, Wd, pg, pu, pre, norm):
        chunks = [list(range(8 * c, 8 * c + 8)) for c in range(4)] + [list(range(32, 36)), list(range(36, 44))]
        nextc = 0
        for p in range(FT // 2):
            proj(Wg, p, range(4), X1k, pg, pre=pre if p == 0 else None)
            proj(Wu, p, range(4), X1k, pu)
            done_t = 2 * p
            while nextc < 4 and chunks[nextc][-1] < done_t:
                kts = chunks[nextc]
                for c in range(8):
                    proj(Wd, c, [k // 4 for k in kts[::4]], XGk, after_down(kts, residual()),
                         pre=ready(kts) if c == 0 else None)
                nextc += 1
        kts = chunks[4]
        for c in range(8):
            proj(Wd, c, [8], XGk, after_down(kts, residual()), pre=ready(kts) if c == 0 else None)
        kts = chunks[5]
        for c in range(8):
            proj(Wd, c, [k // 4 for k in kts[::4]], XGk, after_down(kts, residual(norm)), pre=ready(kts) if c == 0 else None)

    ffn(T_["w_gate"], T_["w_up"], T_["w_down"], post_gate, post_up, pre_ffn,
        (lambda k: gg[:, k:k + 1], "fin", 1e-5))

    ab, gb = A_B2, G_B2
    s_b2 = sem("d_b2")
    g_ = lambda off, n: Gf[:, off:off + n]

    def pre_b2():
        drain()
        begin("fin")
        fr = done()
        for dst, name in ((a_(ab["IF"], 1024), "dftI"), (a_(ab["ws"], 768), "gm_ws"), (a_(ab["bs"], 768), "gm_bs"),
                          (a_(ab["wp"], 512), "pool_w"), (g_(gb["gain"], 1536), "gm_gb")):
            tm["b2"] = dma("sp", s_b2, dst, T_[name], fr)
        tm["b2free"] = fr
        xgtok[:] = [None] * 16

    def cconv(bks, tok, frs, outs, wis, wname, bname, nch):
        rr = [RR.take() for _ in "ab"]
        ts = yield from evac([(b, r.ap[:, 3:259], r.free) for b, r in zip(bks, rr)], tok, frs)
        yield
        ts = yield from conv([(rr[i].ap, outs[i][0], wis[i], ts[i], outs[i][1]) for i in range(2)], 3, 2, wname, nch, bname)
        for r, t in zip(rr, ts):
            RR.give(r, t)
        return ts

    zT = lambda e: a_(ab["z"] + 256 * e, 256)
    ztoks = [None] * 6
    x0toks = [None] * 6

    def post_hv(cts, bks, tok, frs):
        e0 = cts[0] - 16
        ztoks[e0:e0 + 2] = yield from cconv(bks, tok, frs, [(zT(e0 + i), tm["b2free"]) for i in range(2)],
                                            [12 + e0, 13 + e0], "hy_w", "hy_b", 18)

    def post_hx1(cts, bks, tok, frs):
        e0 = cts[0] - 10
        ss = [TR.take() for _ in "ab"]
        ts = yield from cconv(bks, tok, frs, [(s.ap, s.free) for s in ss], [6 + e0, 7 + e0], "hy_w", "hy_b", 18)
        for i in range(2):
            ztoks[e0 + i] = dve(lambda e, i=i: e.tensor_tensor(zT(e0 + i), zT(e0 + i), ss[i].ap, ALU.mult), ts[i], ztoks[e0 + i])
            TR.give(ss[i], ztoks[e0 + i])
        if e0 == 4:
            tasks.append(["hyena", hyena_task(), 0])

    def post_hx0(cts, bks, tok, frs):
        e0 = cts[0] - 4
        x0toks[e0:e0 + 2] = yield from cconv(bks, tok, frs, [(a_(ab["x0"] + 256 * (e0 + i), 256), tm["b2free"]) for i in range(2)],
                                             [e0, e0 + 1], "hy_w", "hy_b", 18)

    def transposes(src, toks, dst, fr):
        out = []
        for st in range(2):
            for c in range(2):
                bk = AUX.take()
                for i in range(3):
                    e_ = 3 * c + i
                    t = pe(lambda e, st=st, i=i, e_=e_, bk=bk: e.transpose(bk.ap[:, 128 * i:128 * i + 128],
                                                                          src(e_)[:, 128 * st:128 * st + 128], ident[:, :]),
                           toks[e_], bk.free)
                yield
                o = dst[:, 768 * st + 384 * c:768 * st + 384 * c + 384]
                t = act(lambda e, o=o, bk=bk: e.activation(o, bk.ap[:, 0:384], ACT.Copy), t, fr)
                AUX.give(bk, t)
                out.append(t)
        tm["tr"] = out

    def hyena_task():
        K = a_(ab["K"], 3840).rearrange("p (m c) -> p m c", m=5)
        F, IF = a_(ab["F"], 1024), a_(ab["IF"], 1024)
        zt, zf = g_(gb["zt"], 1536), g_(gb["zf"], 1536).rearrange("p (m c) -> p m c", m=4)
        ta, tb, tc = (g_(gb["t"] + 384 * i, 384) for i in range(3))
        yield
        yield from transposes(zT, ztoks, zt, tm["b2free"])
        yield
        tr = tm["tr"]
        zfree = tm["b2free"]
        tfree = None
        for hf in range(2):
            sl = slice(384 * hf, 384 * hf + 384)
            tf = []
            for m in range(4):
                bk = AUX.take()
                for st in range(2):
                    lhs = F[:, 512 * st + 128 * m:512 * st + 128 * m + 128]
                    rhs = zt[:, 768 * st + 384 * hf:768 * st + 384 * hf + 384]
                    t = pe(lambda e, lhs=lhs, rhs=rhs, st=st, bk=bk: e.matmul(bk.ap[:, 0:384], lhs, rhs, start=(st == 0), stop=(st == 1)),
                           tr, tm["F"], bk.free)
                yield
                t = act(lambda e, m=m, bk=bk: e.activation(zf[:, m, :], bk.ap[:, 0:384], ACT.Copy), t, zfree)
                AUX.give(bk, t)
                tf.append(t)
            if hf == 1:
                tm["zt_done"] = t
            ty = []
            for m in range(2):
                zr, zi, kr, ki = zf[:, m, :], zf[:, 2 + m, :], K[:, m, sl], K[:, 2 + m, sl]
                k2 = K[:, 4, sl] if m == 0 else K[:, 1, sl]
                w = [tf[m], tf[2 + m], tm["K"], tfree]
                t1 = dve(lambda e, zr=zr, kr=kr: e.tensor_tensor(ta, zr, kr, ALU.mult), *w)
                t2 = pool(lambda e, zi=zi, ki=ki: e.tensor_tensor(tb, zi, ki, ALU.mult), *w)
                t3 = dve(lambda e, zr=zr, ki=ki: e.tensor_tensor(tc, zr, ki, ALU.mult), *w)
                t4 = pool(lambda e, zi=zi, k2=k2: e.tensor_tensor(zi, zi, k2, ALU.mult), t2, *w)
                yield
                t5 = dve(lambda e, zr=zr: e.tensor_tensor(zr, ta, tb, ALU.subtract), t1, t2, t3)
                t6 = dve(lambda e, zi=zi: e.tensor_tensor(zi, zi, tc, ALU.add), t4, t3)
                tfree = [t5, t6]
                ty += [t5, t6]
                yield
            yield
            zfree = []
            for i in range(3):
                e_ = 3 * hf + i
                bk = AUX.take()
                for m in range(4):
                    t = pe(lambda e, m=m, i=i, bk=bk: e.matmul(bk.ap[:, 0:256], zf[:, m, 128 * i:128 * i + 128],
                                                              IF[:, 256 * m:256 * m + 256], start=(m == 0), stop=(m == 3)),
                           ty, tm["b2"], bk.free)
                zfree.append(t)
                yield
                t = dve(lambda e, e_=e_, bk=bk: e.scalar_tensor_tensor(zT(e_), zT(e_), P("hy_skip", e_), bk.ap[:, 0:256],
                                                                      ALU.mult, ALU.add), t)
                AUX.give(bk, t)
                ztoks[e_] = t
        tm["zf_done"] = t

    def hyena_out():
        while "zf_done" not in tm:
            yield
        for e0 in (0, 2, 4):
            items = []
            for e_ in (e0, e0 + 1):
                x0 = a_(ab["x0"] + 256 * e_, 256)
                t = dve(lambda e, e_=e_, x0=x0: e.tensor_tensor(x0, x0, zT(e_), ALU.mult), ztoks[e_], x0toks[e_])
                items.append((XG, 4 + e_, x0, t, [tm["zt_done"], tm["zf_done"]]))
            out = yield from split(items)
            xgtok[4 + e0:6 + e0] = out
            yield

    vg = lambda e: a_(ab["vg"] + 256 * e, 256)
    vgtok = [None] * 6

    def post_gv(cts, bks, tok, frs):
        e0 = cts[0] - 28
        ss = [TR.take() for _ in "ab"]
        ts = yield from evac([(b, s.ap, s.free) for b, s in zip(bks, ss)], tok, frs)
        yield
        for i in range(2):
            vgtok[e0 + i] = act(lambda e, i=i: e.activation(vg(e0 + i), ss[i].ap, ACT.Gelu_apprx_tanh), ts[i], tm["b2free"])
            TR.give(ss[i], vgtok[e0 + i])
        if e0 == 4:
            tasks.append(["gmlp", gmlp_task(), 0])

    def gmlp_task():
        vt = g_(gb["vt"], 1536)
        gain, bias = g_(gb["gain"], 768), g_(gb["gain"] + 768, 768)
        ws, bs = a_(ab["ws"], 768), a_(ab["bs"], 768)
        yield from transposes(vg, vgtok, vt, tm["b2free"])
        tr = tm["tr"]
        tv = []
        sm = TR.take()
        for st in range(2):
            v = vt[:, 768 * st:768 * st + 768]
            stt = sm.ap[:, 32 * st:32 * st + 12]
            mv = sm.ap[:, 32 * st + 12:32 * st + 14]
            rr, u, y = (sm.ap[:, 32 * st + 14 + i:32 * st + 15 + i] for i in range(3))
            for c in range(2):
                t = dve(lambda e, c=c, v=v, stt=stt: e.bn_stats(stt[:, 6 * c:6 * c + 6], v[:, 384 * c:384 * c + 384]), tr, sm.free)
            t = dve(lambda e, mv=mv, stt=stt: e.bn_aggr(mv, stt), t)
            t1 = dve(lambda e, mv=mv, rr=rr: e.tensor_scalar(rr, mv[:, 1:2], 1e-5, None, ALU.add), t)
            t2 = act(lambda e, u=u, rr=rr: e.activation(u, rr, ACT.Sqrt), t1)
            yield
            t2 = dve(lambda e, u=u, y=y: e.reciprocal(y, u), t2)
            t3 = dve(lambda e, u=u, y=y: e.tensor_tensor(u, y, y, ALU.mult), t2)
            t3 = dve(lambda e, u=u, rr=rr: e.scalar_tensor_tensor(u, u, -0.5, rr, ALU.mult, ALU.mult), t3)
            t3 = dve(lambda e, u=u, y=y: e.scalar_tensor_tensor(y, u, 1.5, y, ALU.add, ALU.mult), t3)
            yield
            t4 = dve(lambda e, v=v, mv=mv, y=y: e.tensor_scalar(v, v, mv[:, 0:1], y, ALU.subtract, ALU.mult), t3)
            t5 = pool(lambda e, v=v: e.tensor_tensor(v, v, gain, ALU.mult), t4, tm["b2"])
            t6 = pool(lambda e, v=v: e.tensor_tensor(v, v, bias, ALU.add), t5)
            tv.append(t6)
            yield
        TR.give(sm, tv)
        tm["gain_done"] = tv
        for _ in range(3):
            yield
        for e_ in range(6):
            bk = AUX.take()
            for st in range(2):
                t = pe(lambda e, st=st, e_=e_, bk=bk: e.matmul(bk.ap[:, 128 * st:128 * st + 128],
                                                              vt[:, 768 * st + 128 * e_:768 * st + 128 * e_ + 128],
                                                              ws[:, 128 * e_:128 * e_ + 128], start=True, stop=True),
                       tv, tm["b2"], bk.free)
            yield
            o = vg(e_).rearrange("p (s q) -> p s q", s=2)
            i0 = bk.ap[:, 0:256].rearrange("p (s q) -> p s q", s=2)
            i1 = bs[:, 128 * e_:128 * e_ + 128].unsqueeze(1).to_broadcast([128, 2, 128])
            vgtok[e_] = dve(lambda e, o=o, i0=i0, i1=i1: e.tensor_tensor(o, i0, i1, ALU.add), t, tr)
            AUX.give(bk, vgtok[e_])
        tm["vt_done"] = t

    def pool_task(g, s, t0, pfr):
        half = 2 ** g
        w = 2 * half
        ce = a_(ab["rc"], 280)
        t = dve(lambda e: e.memset(ce[:, 0:9], 0.0), pfr)
        ta = dve(lambda e: e.tensor_tensor_scan(ce[:, 9:265], cones[0], s.ap, 0.0, ALU.mult, ALU.add), t0, pfr, cones[1])
        tb = dve(lambda e: e.tensor_scalar(ce[:, 265:273], ce[:, 0:8], ce[:, 264:265], None, ALU.add), t, ta)
        d = TR.take()
        tc = dve(lambda e: e.tensor_tensor(d.ap, ce[:, 8 + half:264 + half], ce[:, 8 - half:264 - half], ALU.subtract), tb, d.free)
        t1 = dve(lambda e: e.tensor_tensor(d.ap[:, 0:8], d.ap[:, 0:8], P("rcnt", 16 * g, 8), ALU.mult), tc)
        t2 = dve(lambda e: e.tensor_tensor(d.ap[:, 248:256], d.ap[:, 248:256], P("rcnt", 16 * g + 8, 8), ALU.mult), tc)
        t3 = dve(lambda e: e.scalar_tensor_tensor(d.ap, d.ap, 1.0 / w, s.ap, ALU.mult, ALU.subtract), t1, t2)
        TR.give(s, t3)
        pf[0] = [t3]
        yield
        yield
        yield
        bk = AUX.take()
        t = pe(lambda e: e.matmul(bk.ap[:, 0:256], a_(ab["wp"] + 128 * g, 128), d.ap, start=True, stop=True), t3, tm["b2"], bk.free)
        yield
        t = dve(lambda e: e.tensor_scalar(d.ap, bk.ap[:, 0:256], P("pool_b", g), P("pool_scale", g), ALU.add, ALU.mult), t)
        AUX.give(bk, t)
        while "gain_done" not in tm:
            yield
        [xgtok[g]] = yield from split([(XG, g, d.ap, t, tm["gain_done"])])
        TR.give(d, xgtok[g])

    pf = [None]
    cones = [a_(ab["rc"] + 288, 256), None]

    def post_pool(cts, bks, tok, frs):
        ss = [TR.take() for _ in "ab"]
        ts = yield from evac([(b, s.ap, s.free) for b, s in zip(bks, ss)], tok, frs)
        if cts[0] == 0:
            pf[0] = tm["b2free"]
            cones[1] = dve(lambda e: e.memset(cones[0], 1.0), pf[0])
            tasks.append(["hout", hyena_out(), 0])
        for ct, s, t in zip(cts, ss, ts):
            chain("pool", pool_task_late(ct, s, t))
        yield

    def pool_task_late(ct, s, t):
        yield from pool_task(ct, s, t, pf[0])

    def post_gu(cts, bks, tok, frs):
        e0 = cts[0] - 22
        ss = [TR.take() for _ in "ab"]
        ts = yield from evac([(b, s.ap, s.free) for b, s in zip(bks, ss)], tok, frs)
        yield
        ts = [act(lambda e, i=i: e.activation(ss[i].ap, ss[i].ap, ACT.Gelu_apprx_tanh), ts[i]) for i in range(2)]
        yield
        drain("gmlp")
        ts = [dve(lambda e, i=i: e.tensor_tensor(ss[i].ap, ss[i].ap, vg(e0 + i), ALU.mult), ts[i], vgtok[e0 + i]) for i in range(2)]
        out = yield from split([(XG, 10 + e0 + i, ss[i].ap, ts[i], [tm["vt_done"], tm["zf_done"]]) for i in range(2)])
        for i in range(2):
            xgtok[10 + e0 + i] = out[i]
            TR.give(ss[i], out[i])

    W2 = T_["w_in_2"]
    first = True
    for base, n, post in ((8, 3, post_hv), (5, 3, post_hx1), (14, 3, post_gv), (2, 3, post_hx0), (0, 2, post_pool), (11, 3, post_gu)):
        for c in range(n):
            proj(W2, base + c, range(4), X1k, post, pre=pre_b2 if first else None)
            first = False
    for c in range(8):
        proj(T_["w_out_2"], c, [0, 1], XGk, residual())
    for c in range(8):
        proj(T_["w_out_2"], c, [2, 3], XGk, residual((lambda k: P("norm_ffn_2", k), "ffn2", 1e-6)))

    def pre_ffn2():
        begin("ffn2")
        made.clear()
        fr = done()
        for i in range(16):
            slot_free[i] = fr

    def post_gate2(cts, bks, tok, frs):
        ss = [TR.take() for _ in "ab"]
        ts = yield from cconv(bks, tok, frs, [(s.ap, s.free) for s in ss], cts, "fc_w", "fc_b", 88)
        yield
        for i in range(2):
            g_tok[i] = act(lambda e, i=i: e.activation(ss[i].ap, ss[i].ap, ACT.Silu), ts[i])
            SG[i] = ss[i]

    def post_val2(cts, bks, tok, frs):
        ss = [TR.take() for _ in "ab"]
        ts = yield from cconv(bks, tok, frs, [(s.ap, s.free) for s in ss], [FT + c for c in cts], "fc_w", "fc_b", 88)
        yield
        yield from product(cts, ss, ts, dve)

    ffn(T_["w_gate_2"], T_["w_val_2"], T_["w_down_2"], post_gate2, post_val2, pre_ffn2,
        (None, "out", 1e-6))

    run()
    drain_all()
    rs_ap, rt, _ = res["out"]
    s_out = [sem(f"d_out{i}") for i in range(4)]
    outs = []
    for i, eng in ((3, pool), (0, dve), (1, dve), (2, dve)):
        o = hT[:, i * 1024:(i + 1) * 1024]
        o3 = o.rearrange("p (k t) -> p k t", k=4)
        t = eng(lambda e, o3=o3: e.tensor_tensor(o3, o3, rs_ap.unsqueeze(1).to_broadcast([128, 4, 256]), ALU.mult),
                rt, h[4 * i:4 * i + 4])
        outs.append(dma("sp", s_out[i], T_["out"][:, i * 1024:(i + 1) * 1024], o, t))

    with nc.Block() as block:
        @block.sync
        def _(eng):
            for waits, fn, _ in q["sp"].items:
                for s, v in waits:
                    eng.wait_ge(s, v)
                fn(eng)
            for s, v in outs:
                eng.wait_ge(s, v)

        @block.tensor
        def _(eng):
            q["pe"].play(eng)

        @block.vector
        def _(eng):
            q["dve"].play(eng)

        @block.scalar
        def _(eng):
            q["act"].play(eng)

        @block.gpsimd
        def _(eng):
            q["pool"].play(eng)

    for g in reversed(pguards):
        g.__exit__(None, None, None)
    slab.__exit__(None, None, None)
    for g in reversed(sems):
        g.__exit__(None, None, None)


def kernel(**inputs):
    import math
    import numpy as np
    import concourse.bacc as bacc
    from concourse.bass_utils import run_bass_kernel_spmd

    f = np.float32
    I = {k: np.asarray(v) for k, v in inputs.items()}

    def pack(w, n=256, k=4):
        r, c = w.shape
        return np.ascontiguousarray(w.reshape(r // (128 * k), k, 128, c // n, n).transpose(3, 0, 2, 1, 4)).reshape(
            c // n, r // (128 * k), 128, k * n)

    def cols(v):
        return v.reshape(-1, 128).T

    def taps(w):
        return w.reshape(-1, 128).T

    def pad(v):
        o = np.zeros((128, 1), f)
        o[:v.shape[0], 0] = v
        return o

    w_in = I["w_in"][0]
    arr = {}
    arr["w_zx"] = pack(w_in[:, 0:5120])
    wd = np.zeros((2048, 128), f)
    wd[:, 0:32] = w_in[:, 5120:5152]
    arr["w_dt"] = pack(wd, 128, 8)
    arr["w_sc"] = pack(w_in[:, 5152:])
    arr["w_ossd"] = pack(I["w_out"][0][0:2048])
    arr["w_osc"] = pack(I["w_out"][0][2048:])
    for n in ("w_q", "w_k", "w_v", "w_o", "w_gate", "w_up", "w_down"):
        arr[n] = pack(I[n][0])
    arr["w_in_2"] = pack(I["w_in_2"][0])
    arr["w_out_2"] = pack(I["w_out_2"][0])
    arr["w_gate_2"] = pack(I["ffn_w_up_2"][0][:, 0:5632])
    arr["w_val_2"] = pack(I["ffn_w_up_2"][0][:, 5632:])
    arr["w_down_2"] = pack(I["ffn_w_down_2"][0])

    def fm(x):
        return np.ascontiguousarray(x.T.reshape(-1, 128, 256).transpose(1, 0, 2)).reshape(128, -1)

    arr["xT"] = fm(I["x"][0])
    arr["memT"] = fm(I["mem"][0])
    rc = np.ones((4, 16), f)
    t = np.arange(256)
    for g, w in enumerate((2, 4, 8, 16)):
        cnt = np.minimum(t + w // 2 - 1, 255) - np.maximum(t - w // 2, 0) + 1
        full = (w / cnt).astype(f)
        rc[g, 0:8], rc[g, 8:16] = full[0:8], full[248:256]
    P = {
        "norm_mix": cols(I["norm_mix"][0]), "conv_w": taps(I["ssd_conv_w"][0]), "conv_b": cols(I["ssd_conv_b"][0]),
        "ssd_norm": cols(I["ssd_norm"][0]), "d_skip": cols(np.repeat(I["d_skip"][0], 64)),
        "sc_w": taps(I["sc_conv_w"][0]), "sc_norm": cols(I["sc_norm"][0]), "mem_norm": cols(I["mem_norm"]),
        "norm_xa": cols(I["norm_xa"][0]), "norm_ffn": cols(I["norm_ffn"][0]), "norm_final": cols(I["norm_final"]),
        "norm_mix_2": cols(I["norm_mix_2"][0]), "pool_b": cols(I["pool_b_2"][0].reshape(-1)),
        "pool_scale": cols(I["pool_scale_2"][0]), "hy_w": taps(I["hy_short_w_2"][0]), "hy_b": cols(I["hy_short_b_2"][0]),
        "hy_skip": cols(I["hy_skip_2"][0]), "norm_ffn_2": cols(I["norm_ffn_2"][0]), "fc_w": taps(I["ffn_conv_w_2"][0]),
        "fc_b": cols(I["ffn_conv_b_2"][0]), "norm_final_2": cols(I["norm_final_2"]), "dt_bias": pad(I["dt_bias"][0]),
        "a_log": pad(I["a_log"][0]), "f_b1": pad(I["hy_filt_b1_2"][0]), "f_fr1": pad(I["hy_filt_freq1_2"][0]),
        "f_b2": pad(I["hy_filt_b2_2"][0]), "f_fr2": pad(I["hy_filt_freq2_2"][0]),
        "rcnt": np.broadcast_to(rc.reshape(1, 64), (128, 64)),
    }
    arr["par"] = np.ascontiguousarray(np.concatenate([P[n] for n, _ in PARAMS], axis=1))
    arr["ident"] = np.eye(128, dtype=f)
    s_, l_ = np.arange(128)[:, None], np.arange(128)[None, :]
    tri = (l_ >= s_).astype(f)
    arr["mask"] = np.ascontiguousarray(np.concatenate([tri, np.ones((128, 128), f), tri], axis=1))

    n = np.arange(256)[:, None]
    b = np.arange(256)[None, :]
    ang = 2 * np.pi * ((n * b) % 512) / 512
    sgn = (1.0 - 2.0 * (n % 2))
    Fm = np.concatenate([np.cos(ang), -np.sin(ang)], axis=1)
    Fm[:, 256:257] = sgn
    wgt = np.full((256, 1), 2.0)
    wgt[0] = 1.0
    Im = np.concatenate([wgt * np.cos(ang.T), -wgt * np.sin(ang.T)], axis=0) / 512
    Im[256, :] = sgn[:, 0] / 512

    def rows(m, k):
        return np.ascontiguousarray(m.astype(f).reshape(k, 128, -1).transpose(1, 0, 2)).reshape(128, -1)
    arr["dftF"], arr["dftI"] = rows(Fm, 2), rows(Im, 4)
    tt = np.linspace(0.0, 1.0, 256, dtype=f)[:, None]
    ww = (f(2.0 * math.pi) * np.arange(256, dtype=f)[:, None] / f(256)).astype(f)
    ff = np.linspace(1e-4, 15, 16, dtype=f)[None, :]
    arr["feat"] = np.ascontiguousarray(np.concatenate([tt, np.cos(ff * ww), -np.sin(ff * ww)], axis=1).astype(f).T)
    deltas = np.linspace(math.log(1e-2) / 1.5, math.log(1e-2) / 0.3, 768, dtype=f)
    arr["decay"] = rows(np.exp(-tt * np.abs(deltas)[None, :]), 2)
    arr["f_w1"], arr["f_w2"], arr["f_w3"] = (np.ascontiguousarray(I[f"hy_filt_w{i}_2"][0]) for i in (1, 2, 3))
    arr["gm_ws"] = np.ascontiguousarray(I["gm_w_s_2"][0].transpose(2, 0, 1)).reshape(128, 768)
    arr["gm_bs"] = np.ascontiguousarray(np.broadcast_to(I["gm_b_s_2"][0].reshape(1, 768), (128, 768)))
    arr["pool_w"] = np.ascontiguousarray(I["pool_w_2"][0].transpose(1, 0, 2)).reshape(128, 512)
    arr["gm_gb"] = np.ascontiguousarray(np.broadcast_to(
        np.concatenate([I["gm_ln_g_2"][0], I["gm_ln_b_2"][0]])[None, :], (128, 1536)))

    nc = bacc.Bacc("TRN2", target_bir_lowering=False, num_devices=1)
    T_ = {k: nc.dram_tensor(f"in_{k}", v.shape, mybir.dt.from_np(v.dtype), kind="ExternalInput").ap() for k, v in arr.items()}
    T_["out"] = nc.dram_tensor("out_0", (128, 4096), F32, kind="ExternalOutput").ap()
    program(nc, T_)
    r = run_bass_kernel_spmd(nc, [{f"in_{k}": v for k, v in arr.items()}], core_ids=[0])
    o = r.results[0]["out_0"]
    return np.ascontiguousarray(o.reshape(128, 16, 256).transpose(2, 1, 0)).reshape(1, 256, 2048)
```
